# Optimizing a Trainium2 kernel written in Bass

```python
import jax, jax.numpy as jnp
from jax import lax
import numpy as np

D_MODEL = 2048
BATCH = 1
SEQ = 256
DEPTH = 1

CHUNK = 64
HEAD_DIM = 128
N_HEADS_SB = 8
N_HEADS_FOX = 8
W_SB = N_HEADS_SB * HEAD_DIM
W_FOX = N_HEADS_FOX * HEAD_DIM
MIX_WIDTH = W_SB + W_FOX
IN_COLS = 3 * W_SB + 3 * W_FOX + N_HEADS_FOX
D_FF = 4 * D_MODEL
Q_BLOCK = 128
EPS = 1e-6


def rmsnorm(x, g):
    xf = x.astype(jnp.float32)
    var = jnp.mean(xf * xf, axis=-1, keepdims=True)
    return (xf * lax.rsqrt(var + EPS) * g.astype(jnp.float32)).astype(x.dtype)

def head_rmsnorm(o, g):
    of = o.astype(jnp.float32)
    of = of * lax.rsqrt(jnp.mean(of * of, axis=-1, keepdims=True) + EPS)
    b, h, s, d = o.shape
    of = jnp.transpose(of, (0, 2, 1, 3)).reshape(b, s, h * d)
    return (of * g.astype(jnp.float32)).astype(o.dtype)

def split_heads(t, n_heads):
    b, s, _ = t.shape
    return jnp.transpose(t.reshape(b, s, n_heads, HEAD_DIM), (0, 2, 1, 3))

def stick_breaking_attention(q, k, v):
    seq = q.shape[2]
    scale = HEAD_DIM ** -0.5
    outs = []
    for i in range(seq // Q_BLOCK):
        end = (i + 1) * Q_BLOCK
        qb = q[:, :, i * Q_BLOCK:end]
        kb = k[:, :, :end]
        vb = v[:, :, :end]
        z = jnp.einsum('bhqd,bhkd->bhqk', qb, kb).astype(jnp.float32) * scale
        t_pos = i * Q_BLOCK + jnp.arange(Q_BLOCK)
        s_pos = jnp.arange(end)
        causal = s_pos[None, :] < t_pos[:, None]
        log_beta = jax.nn.log_sigmoid(z)
        log_keep = jnp.where(causal, jax.nn.log_sigmoid(-z), 0.0)
        rest = lax.cumsum(log_keep, axis=3, reverse=True) - log_keep
        a = jnp.where(causal, jnp.exp(log_beta + rest), 0.0)
        outs.append(jnp.einsum('bhqk,bhkd->bhqd', a.astype(v.dtype), vb))
    return jnp.concatenate(outs, axis=2)

def forgetting_attention(q, k, v, log_f):
    seq = q.shape[2]
    scale = HEAD_DIM ** -0.5
    c = lax.cumsum(log_f.astype(jnp.float32), axis=2)
    outs = []
    for i in range(seq // Q_BLOCK):
        end = (i + 1) * Q_BLOCK
        qb = q[:, :, i * Q_BLOCK:end]
        kb = k[:, :, :end]
        vb = v[:, :, :end]
        z = jnp.einsum('bhqd,bhkd->bhqk', qb, kb).astype(jnp.float32) * scale
        z = z + c[:, :, i * Q_BLOCK:end, None] - c[:, :, None, :end]
        t_pos = i * Q_BLOCK + jnp.arange(Q_BLOCK)
        s_pos = jnp.arange(end)
        causal = s_pos[None, :] <= t_pos[:, None]
        p = jax.nn.softmax(jnp.where(causal, z, -jnp.inf), axis=-1)
        outs.append(jnp.einsum('bhqk,bhkd->bhqd', p.astype(v.dtype), vb))
    return jnp.concatenate(outs, axis=2)

def first_inputs(seed: int = 0) -> dict:
    key = jax.random.key(seed)
    ks = jax.random.split(key, 12)
    f32 = jnp.float32
    x = jax.random.normal(ks[0], (BATCH, SEQ, D_MODEL), f32)
    g_attn = 1.0 + 0.05 * jax.random.normal(ks[1], (DEPTH, D_MODEL), f32)
    w_in = jax.random.normal(ks[2], (DEPTH, D_MODEL, IN_COLS), f32) * D_MODEL ** -0.5
    b_f = jax.random.uniform(ks[3], (DEPTH, N_HEADS_FOX), f32, 1.0, 4.0)
    g_out_sb = 1.0 + 0.05 * jax.random.normal(ks[4], (DEPTH, W_SB), f32)
    g_out_fox = 1.0 + 0.05 * jax.random.normal(ks[5], (DEPTH, W_FOX), f32)
    w_out = jax.random.normal(ks[6], (DEPTH, MIX_WIDTH, D_MODEL), f32) * MIX_WIDTH ** -0.5
    g_mlp = 1.0 + 0.05 * jax.random.normal(ks[7], (DEPTH, D_MODEL), f32)
    w_up = jax.random.normal(ks[8], (DEPTH, D_MODEL, D_FF), f32) * D_MODEL ** -0.5
    w_down = jax.random.normal(ks[9], (DEPTH, D_FF, D_MODEL), f32) * D_FF ** -0.5
    g_final = 1.0 + 0.05 * jax.random.normal(ks[10], (D_MODEL,), f32)
    return {"x": x, "g_attn": g_attn, "w_in": w_in, "b_f": b_f,
            "g_out_sb": g_out_sb, "g_out_fox": g_out_fox, "w_out": w_out,
            "g_mlp": g_mlp, "w_up": w_up, "w_down": w_down, "g_final": g_final}

def first_block(x, g_attn, w_in, b_f, g_out_sb, g_out_fox, w_out, g_mlp, w_up, w_down, g_final):
    o0 = 3 * W_SB
    o1 = o0 + 3 * W_FOX
    for l in range(DEPTH):
        h = rmsnorm(x, g_attn[l])
        proj = jnp.einsum('bsd,de->bse', h, w_in[l])
        qa = split_heads(proj[..., 0:W_SB], N_HEADS_SB)
        ka = split_heads(proj[..., W_SB:2 * W_SB], N_HEADS_SB)
        va = split_heads(proj[..., 2 * W_SB:o0], N_HEADS_SB)
        qf = split_heads(proj[..., o0:o0 + W_FOX], N_HEADS_FOX)
        kf = split_heads(proj[..., o0 + W_FOX:o0 + 2 * W_FOX], N_HEADS_FOX)
        vf = split_heads(proj[..., o0 + 2 * W_FOX:o1], N_HEADS_FOX)
        f_logit = proj[..., o1:].astype(jnp.float32) + b_f[l].astype(jnp.float32)
        log_f = jnp.transpose(jax.nn.log_sigmoid(f_logit), (0, 2, 1))

        o_sb = stick_breaking_attention(qa, ka, va)
        o_fox = forgetting_attention(qf, kf, vf, log_f)
        mixed = jnp.concatenate([head_rmsnorm(o_sb, g_out_sb[l]),
                                 head_rmsnorm(o_fox, g_out_fox[l])], axis=-1)
        x = x + jnp.einsum('bse,ed->bsd', mixed, w_out[l])

        h2 = rmsnorm(x, g_mlp[l])
        u = jax.nn.relu(jnp.einsum('bsd,df->bsf', h2, w_up[l]))
        x = x + jnp.einsum('bsf,fd->bsd', u * u, w_down[l])
    return rmsnorm(x, g_final)


A_HEADS = 8
A_DK = 128
A_DV = 128
A_WIDTH = A_HEADS * A_DV

B_QK_HEADS = 4
B_V_HEADS = 8
B_DK = 128
B_DV = 128
B_WIDTH = B_V_HEADS * B_DV
CONV = 4
B_CONV_CH = 2 * B_QK_HEADS * B_DK + B_WIDTH

MIX_WIDTH_2 = A_WIDTH + B_WIDTH

IN_SIZES = (A_HEADS * A_DK, A_HEADS * A_DK, A_WIDTH, A_WIDTH,
            B_QK_HEADS * B_DK, B_QK_HEADS * B_DK, B_WIDTH, B_WIDTH,
            B_V_HEADS, B_V_HEADS)
IN_WIDTH = 4 * A_HEADS * A_DK + 2 * B_QK_HEADS * B_DK + 2 * B_WIDTH + 2 * B_V_HEADS

P_HEADS = 8
N_KEYS = 128
N_EXPERTS = N_KEYS * N_KEYS
P_DKEY = 256
P_TOPK = 16
P_BLOCK = 128


def _rmsnorm(x, g):
    xf = x.astype(jnp.float32)
    y = xf * lax.rsqrt(jnp.mean(xf * xf, axis=-1, keepdims=True) + EPS)
    return (y * g.astype(jnp.float32)).astype(x.dtype)

def _gated_rmsnorm(o, z, g):
    of = o.astype(jnp.float32)
    y = of * lax.rsqrt(jnp.mean(of * of, axis=-1, keepdims=True) + EPS)
    return y * g.astype(jnp.float32) * jax.nn.silu(z.astype(jnp.float32))

def _l2norm(x):
    xf = x.astype(jnp.float32)
    return xf * lax.rsqrt(jnp.sum(xf * xf, axis=-1, keepdims=True) + EPS)

def _chunk(t):
    b, s, h = t.shape[:3]
    rest = t.shape[3:]
    t = t.reshape((b, s // CHUNK, CHUNK, h) + rest)
    return t.transpose((1, 0, 3, 2) + tuple(range(4, t.ndim)))

def _unchunk(t):
    n, b, h, c, d = t.shape
    return t.transpose(1, 0, 3, 2, 4).reshape(b, n * c, h, d)

def _causal_conv_silu(x, w):
    s = x.shape[1]
    xp = jnp.pad(x, ((0, 0), (CONV - 1, 0), (0, 0)))
    y = xp[:, 0:s, :] * w[0]
    for j in range(1, CONV):
        y = y + xp[:, j:j + s, :] * w[j]
    return jax.nn.silu(y)

def _hgrn2(q, f_logit, v, lb):
    q = q.astype(jnp.float32)
    z = f_logit.astype(jnp.float32)
    v = v.astype(jnp.float32)
    lb = lb.astype(jnp.float32)
    log_f = jnp.log(lb + (1.0 - lb) * jax.nn.sigmoid(z))
    k = (1.0 - lb) * jax.nn.sigmoid(-z)
    qc, kc, vc = _chunk(q), _chunk(k), _chunk(v)
    bc = jnp.cumsum(_chunk(log_f), axis=-2)
    causal = jnp.tril(jnp.ones((CHUNK, CHUNK), dtype=bool))

    def step(S, inp):
        q_c, k_c, v_c, b_c = inp
        diff = b_c[..., :, None, :] - b_c[..., None, :, :]
        decay = jnp.exp(jnp.where(causal[:, :, None], diff, -jnp.inf))
        att = jnp.einsum('bhtd,bhsd,bhtsd->bhts', q_c, k_c, decay)
        o = (jnp.einsum('bhtd,bhdv->bhtv', q_c * jnp.exp(b_c), S)
             + jnp.einsum('bhts,bhsv->bhtv', att, v_c))
        b_last = b_c[..., -1:, :]
        S = (S * jnp.exp(b_last[..., 0, :, None])
             + jnp.einsum('bhsd,bhsv->bhdv', k_c * jnp.exp(b_last - b_c), v_c))
        return S, o

    S0 = jnp.zeros((q.shape[0], q.shape[2], A_DK, A_DV), jnp.float32)
    _, o = lax.scan(step, S0, (qc, kc, vc, bc))
    return _unchunk(o)

def _gated_delta(q, k, v, beta, g):
    q = _chunk(q.astype(jnp.float32) * (B_DK ** -0.5))
    k = _chunk(k.astype(jnp.float32))
    v = _chunk(v.astype(jnp.float32))
    beta = _chunk(beta.astype(jnp.float32))
    gc = jnp.cumsum(_chunk(g.astype(jnp.float32)), axis=-1)
    incl = jnp.tril(jnp.ones((CHUNK, CHUNK), dtype=bool))
    strict = jnp.tril(jnp.ones((CHUNK, CHUNK), dtype=bool), k=-1)
    L = jnp.exp(jnp.where(incl, gc[..., :, None] - gc[..., None, :], -jnp.inf))
    kb = k * beta[..., None]
    M = jnp.eye(CHUNK, dtype=jnp.float32) + jnp.where(
        strict, jnp.einsum('...td,...sd->...ts', kb, k) * L, 0.0)
    u = lax.linalg.triangular_solve(M, v * beta[..., None], left_side=True,
                                    lower=True, unit_diagonal=True)
    w = lax.linalg.triangular_solve(M, kb * jnp.exp(gc)[..., None], left_side=True,
                                    lower=True, unit_diagonal=True)
    a_qk = jnp.einsum('...td,...sd->...ts', q, k) * L
    qg = q * jnp.exp(gc)[..., None]
    g_last = gc[..., -1:]
    kd = k * jnp.exp(g_last - gc)[..., None]
    dl = jnp.exp(g_last)[..., None]

    def step(S, inp):
        qg_c, kd_c, u_c, w_c, a_c, dl_c = inp
        v_new = u_c - jnp.einsum('bhtd,bhdv->bhtv', w_c, S)
        o = (jnp.einsum('bhtd,bhdv->bhtv', qg_c, S)
             + jnp.einsum('bhts,bhsv->bhtv', a_c, v_new))
        S = S * dl_c + jnp.einsum('bhsd,bhsv->bhdv', kd_c, v_new)
        return S, o

    S0 = jnp.zeros((qg.shape[1], qg.shape[2], B_DK, B_DV), jnp.float32)
    _, o = lax.scan(step, S0, (qg, kd, u, w, a_qk, dl))
    return _unchunk(o)

def _peer(xn, w_query, sub_keys, u_tab, v_tab):
    b, s, d = xn.shape
    t = b * s
    xt = xn.reshape(t, d)
    qry = jnp.einsum('td,dhk->thk', xt, w_query).astype(jnp.float32)
    half = P_DKEY // 2
    s1 = jnp.einsum('thk,hnk->thn', qry[..., :half], sub_keys[0].astype(jnp.float32))
    s2 = jnp.einsum('thk,hnk->thn', qry[..., half:], sub_keys[1].astype(jnp.float32))
    v1, i1 = lax.top_k(s1, P_TOPK)
    v2, i2 = lax.top_k(s2, P_TOPK)
    cand = (v1[..., :, None] + v2[..., None, :]).reshape(t, P_HEADS, P_TOPK * P_TOPK)
    best, pos = lax.top_k(cand, P_TOPK)
    expert = (jnp.take_along_axis(i1, pos // P_TOPK, axis=-1) * N_KEYS
              + jnp.take_along_axis(i2, pos % P_TOPK, axis=-1))
    gate = jax.nn.softmax(best, axis=-1)
    nblk = t // P_BLOCK

    def blk(args):
        xb, eb, gb = args
        hid = jax.nn.gelu(jnp.einsum('pd,phkd->phk', xb, u_tab[eb]).astype(jnp.float32),
                          approximate=False)
        return jnp.einsum('phk,phkd->pd', (gb * hid).astype(xb.dtype), v_tab[eb])

    y = lax.map(blk, (xt.reshape(nblk, P_BLOCK, d),
                      expert.reshape(nblk, P_BLOCK, P_HEADS, P_TOPK),
                      gate.reshape(nblk, P_BLOCK, P_HEADS, P_TOPK)))
    return y.reshape(b, s, d)

def second_inputs(seed: int = 0) -> dict:
    key = jax.random.key(seed)
    ks = jax.random.split(key, 20)
    f32 = jnp.float32
    nrm = lambda k, shape, scale: jax.random.normal(k, shape, f32) * scale
    gain = lambda k, shape: 1.0 + 0.02 * jax.random.normal(k, shape, f32)
    dt = jnp.exp(jax.random.uniform(ks[8], (DEPTH, B_V_HEADS), f32,
                                    minval=np.log(1e-3), maxval=np.log(1e-1)))
    return {
        "x": nrm(ks[0], (BATCH, SEQ, D_MODEL), 1.0),
        "attn_norm_g": gain(ks[1], (DEPTH, D_MODEL)),
        "w_in": nrm(ks[2], (DEPTH, D_MODEL, IN_WIDTH), D_MODEL ** -0.5),
        "hgrn_lb_logits": nrm(ks[3], (DEPTH + 1, A_HEADS, A_DK), 0.1),
        "hgrn_norm_g": gain(ks[4], (DEPTH, A_DV)),
        "gdn_conv_w": nrm(ks[5], (DEPTH, CONV, B_CONV_CH), CONV ** -0.5),
        "gdn_A_log": jnp.log(jax.random.uniform(ks[6], (DEPTH, B_V_HEADS), f32,
                                                minval=1.0, maxval=16.0)),
        "gdn_dt_bias": dt + jnp.log(-jnp.expm1(-dt)),
        "gdn_norm_g": gain(ks[7], (DEPTH, B_DV)),
        "w_out": nrm(ks[9], (DEPTH, MIX_WIDTH_2, D_MODEL), MIX_WIDTH_2 ** -0.5),
        "ffn_norm_g": gain(ks[10], (DEPTH, D_MODEL)),
        "peer_w_query": nrm(ks[11], (DEPTH, D_MODEL, P_HEADS, P_DKEY), D_MODEL ** -0.5),
        "peer_sub_keys": nrm(ks[12], (DEPTH, 2, P_HEADS, N_KEYS, P_DKEY // 2),
                             (P_DKEY // 2) ** -0.5),
        "peer_u": nrm(ks[13], (DEPTH, N_EXPERTS, D_MODEL), D_MODEL ** -0.5),
        "peer_v": nrm(ks[14], (DEPTH, N_EXPERTS, D_MODEL), P_HEADS ** -0.5),
        "final_norm_g": gain(ks[15], (D_MODEL,)),
    }

def second_block(x, attn_norm_g, w_in, hgrn_lb_logits, hgrn_norm_g, gdn_conv_w, gdn_A_log,
              gdn_dt_bias, gdn_norm_g, w_out, ffn_norm_g, peer_w_query, peer_sub_keys,
              peer_u, peer_v, final_norm_g):
    b, s, _ = x.shape
    lb_all = jnp.cumsum(jax.nn.softmax(hgrn_lb_logits.astype(jnp.float32), axis=0), axis=0)
    offs = []
    acc = 0
    for n in IN_SIZES[:-1]:
        acc += n
        offs.append(acc)
    rep = B_V_HEADS // B_QK_HEADS
    h = x
    for l in range(DEPTH):
        xn = _rmsnorm(h, attn_norm_g[l])
        proj = xn @ w_in[l]
        a_q, a_f, a_i, a_g, b_q, b_k, b_v, b_z, b_b, b_a = jnp.split(proj, offs, axis=-1)
        o_a = _hgrn2(a_q.reshape(b, s, A_HEADS, A_DK), a_f.reshape(b, s, A_HEADS, A_DK),
                     a_i.reshape(b, s, A_HEADS, A_DV), lb_all[l])
        o_a = _gated_rmsnorm(o_a, a_g.reshape(b, s, A_HEADS, A_DV), hgrn_norm_g[l])
        qkv = _causal_conv_silu(jnp.concatenate([b_q, b_k, b_v], axis=-1), gdn_conv_w[l])
        nqk = B_QK_HEADS * B_DK
        gq = _l2norm(qkv[..., :nqk].reshape(b, s, B_QK_HEADS, B_DK))
        gk = _l2norm(qkv[..., nqk:2 * nqk].reshape(b, s, B_QK_HEADS, B_DK))
        gv = qkv[..., 2 * nqk:].reshape(b, s, B_V_HEADS, B_DV)
        gq = jnp.repeat(gq, rep, axis=2)
        gk = jnp.repeat(gk, rep, axis=2)
        beta = jax.nn.sigmoid(b_b.astype(jnp.float32))
        g = -jnp.exp(gdn_A_log[l].astype(jnp.float32)) * jax.nn.softplus(
            b_a.astype(jnp.float32) + gdn_dt_bias[l].astype(jnp.float32))
        o_b = _gated_delta(gq, gk, gv, beta, g)
        o_b = _gated_rmsnorm(o_b, b_z.reshape(b, s, B_V_HEADS, B_DV), gdn_norm_g[l])
        mix = jnp.concatenate([o_a.reshape(b, s, A_WIDTH), o_b.reshape(b, s, B_WIDTH)],
                              axis=-1).astype(x.dtype)
        h = h + mix @ w_out[l]
        hn = _rmsnorm(h, ffn_norm_g[l])
        h = h + _peer(hn, peer_w_query[l], peer_sub_keys[l], peer_u[l], peer_v[l])
    return _rmsnorm(h, final_norm_g)


def setup_inputs(seed=0):
    out = dict(first_inputs(seed))
    for name, value in second_inputs(seed + 1).items():
        if name != "x":
            out[name + "_2"] = value
    return out


def reference(
    x, g_attn, w_in, b_f, g_out_sb, g_out_fox, w_out, g_mlp, w_up, w_down, g_final,
    attn_norm_g_2, w_in_2, hgrn_lb_logits_2, hgrn_norm_g_2, gdn_conv_w_2, gdn_A_log_2,
    gdn_dt_bias_2, gdn_norm_g_2, w_out_2, ffn_norm_g_2, peer_w_query_2, peer_sub_keys_2,
    peer_u_2, peer_v_2, final_norm_g_2,
):
    x = first_block(
        x, g_attn, w_in, b_f, g_out_sb, g_out_fox, w_out, g_mlp, w_up, w_down, g_final,
    )
    return second_block(
        x, attn_norm_g_2, w_in_2, hgrn_lb_logits_2, hgrn_norm_g_2, gdn_conv_w_2, gdn_A_log_2,
        gdn_dt_bias_2, gdn_norm_g_2, w_out_2, ffn_norm_g_2, peer_w_query_2, peer_sub_keys_2,
        peer_u_2, peer_v_2, final_norm_g_2,
    )


_drawn_inputs = setup_inputs


def setup_inputs(seed=0):
    import zlib

    import numpy as np

    out = dict(_drawn_inputs(seed))
    spreads = {}
    factors = {'hgrn_norm_g_2': 59.525,
     'gdn_norm_g_2': 60.451,
     'final_norm_g_2': 24.516,
     'ffn_norm_g_2': 21.146}
    for name, (base, spread) in spreads.items():
        noise = np.random.default_rng([zlib.crc32(name.encode()), seed]).standard_normal(out[name].shape)
        drawn = base * np.exp(spread * noise) if base else spread * noise
        out[name] = __import__('jax').numpy.asarray(drawn.astype(out[name].dtype))
    for name, factor in factors.items():
        out[name] = (out[name] * factor).astype(out[name].dtype)
    return out
```

```python
import numpy as np
from contextlib import ExitStack
import concourse.bass as bass
from concourse import mybir

F32 = mybir.dt.float32
F32R = mybir.dt.float32r
U32 = mybir.dt.uint32
ALU = mybir.AluOpType
ACT = mybir.ActivationFunctionType
AX = mybir.AxisListType

P = 128
TT = 2
D = 2048
KT = D // P
NB = 512
CH = 2048
SLOTS = 4
AHEAD = 3
H = 8
HD = 128
EPS = 1e-6
SCALE = HD ** -0.5
NEG = -30000.0

W1 = 6 * H * HD
W2 = 7168
G1, G2 = W1 // NB, W2 // NB
MLP_SB = 8192 // NB
PEER_SB = 16384 // NB
NK = 128
TOPK = 16

Q_IN1 = 0
Q_OUT1 = Q_IN1 + G1
Q_MLP = Q_OUT1 + 4
Q_IN2 = Q_MLP + 2 * MLP_SB
Q_OUT2 = Q_IN2 + G2
Q_WQ = Q_OUT2 + 4
Q_PEER = Q_WQ + 4
Q_END = Q_PEER + 2 * PEER_SB

C_ID, C_ONES, C_GT, C_LEV, C_LE, C_MASK, C_IOTA = 0, 1, 2, 3, 10, 11, 19
N_CONST = 20
A_NGE, A_NONES, A_SBM, A_SBA, A_FXA = 0, 1, 2, 5, 8
N_ATT = 11
S_GATTN, S_GOUT1, S_GMLP, S_GATTN2, S_GHGRN, S_GGDN, S_GFFN, S_BF, S_ALOG, S_DTB, S_CONV = 0, 16, 32, 48, 64, 65, 66, 82, 90, 98, 106
N_SMALL = 106 + 64


def constants():
    p, f = np.arange(P)[:, None], np.arange(P)[None, :]
    c = np.zeros((P, N_CONST, P), np.float32)
    c[:, C_ID] = p == f
    c[:, C_ONES] = 1
    c[:, C_GT] = p > f
    c[:, C_LE] = p <= f
    c[:, C_MASK] = p == f
    for lev in range(7):
        m = 1 << lev
        mid = f // (2 * m) * (2 * m) + m
        upper = (f // m) % 2 == 1
        c[:, C_LEV + lev] = np.where(upper, (p >= mid) & (p <= f), (p > f) & (p < mid))
        c[:, C_MASK + 1 + lev] = (p // (2 * m) == f // (2 * m)) & ((p // m) % 2 == 0) & upper
    c[:, C_IOTA] = f
    a = np.zeros((P, N_ATT, P), np.float32)
    a[:, A_NGE] = -1.0 * (p >= f)
    a[:, A_NONES] = -1
    a[:, A_SBM], a[:, A_SBM + 1], a[:, A_SBM + 2] = p < f, 1, p < f
    a[:, A_SBA] = a[:, A_SBA + 2] = np.where(p < f, 0.0, NEG)
    a[:, A_FXA] = a[:, A_FXA + 2] = np.where(f <= p, 0.0, -1e30)
    return c, a


def two_blocks(nc, x_d, cst_d, att_d, small_d, gfin1_d, gfin2_d, lbl_d, wf_d, wba_d, keys_d,
               w_in_d, w_out_d, w_mlp_d, w_in2_d, w_out2_d, wq_d, w_peer_d, out_d):
    ctx = ExitStack()
    gates_d = nc.dram_tensor("gates_scratch", (P, PEER_SB, 8, 4, 32), F32, kind="Internal").ap()
    with ctx:
        def sem(name):
            return ctx.enter_context(nc.semaphore(name))

        cursor = [(nc.sbuf_base + 31) // 32 * 32]

        def sb(name, shape, dt=F32, at=None):
            size = 4 * int(np.prod(shape[1:]))
            t = nc.alloc_sbuf_tensor_at(name, shape, dt, offset=cursor[0] if at is None else at)
            if at is None:
                cursor[0] += (size + 31) // 32 * 32
            return t

        raw = sb("raw", [P, SLOTS, CH])
        hi = sb("hi", [P, SLOTS, CH], F32R)
        lo = sb("lo", [P, SLOTS, CH], F32R)
        resid = sb("resid", [P, TT, D])
        cst = sb("cst", [P, N_CONST, P])
        small = sb("small", [P, N_SMALL])
        stat = sb("stat", [P, 8])
        wtail = sb("wtail", [P, KT, 16])
        wtail_h = sb("wtail_h", [P, KT, 16], F32R)
        wtail_l = sb("wtail_l", [P, KT, 16], F32R)
        tail = sb("tail", [P, TT, 16])
        at_x = cursor[0]
        xh = sb("xh", [P, KT, TT * P], F32R)
        xl = sb("xl", [P, KT, TT * P], F32R)
        at_y = cursor[0]

        def region(at):
            c = [at]

            def place(name, shape, dt=F32):
                t = sb(name, shape, dt, at=c[0])
                c[0] += (4 * int(np.prod(shape[1:])) + 31) // 32 * 32
                assert c[0] <= nc.sbuf_usable_end, (name, c[0], nc.sbuf_usable_end)
                return t
            return place

        y = region(at_y)
        nat = y("nat", [P, TT, D])
        y = region(at_y)
        proj1 = y("proj1", [P, TT, W1])
        att = y("att", [P, N_ATT, P])
        gfin = y("gfin", [P, D])
        y = region(at_y)
        proj2 = y("proj2", [P, TT, W2])
        y = region(at_y)
        hid = y("hid", [P, TT, NB])
        coef = y("coef", [P, 4, TT * P])
        coef_h = [y(f"coef_h{i}", [P, 4, TT * P], F32R) for i in range(2)]
        coef_l = [y(f"coef_l{i}", [P, 4, TT * P], F32R) for i in range(2)]
        gate_e = [y(f"gate_e{i}", [P, 8, 4, 32]) for i in range(2)]
        at_gate = at_y + 4 * 2 * 1024 * 4

        s = region(at_x)
        NQ = 3
        qkT = [s(f"qkT{i}", [P, 2, TT * P]) for i in range(2)]
        sc_e = [s(f"sc_e{i}", [P, 3 * P]) for i in range(2)]
        sc_s = [s(f"sc_s{i}", [P, 3 * P]) for i in range(2)]
        sc_a = [s(f"sc_a{i}", [P, 3 * P]) for i in range(2)]
        aT = [s(f"aT{i}", [P, 3 * P]) for i in range(2)]
        lfU = [s(f"lfU{i}", [P, 3, P]) for i in range(2)]
        fx = s("fx", [P, 2, 8, 4])
        lf = s("lf", [P, TT, H])
        hss = s("hss", [P, TT, 2 * H])
        hrs = s("hrs", [P, TT, 2 * H])
        junk = s("junk", [P, 2, TT, P])
        sp_t = s("sp_t", [P, 3, TT, 16])

        pj = [ctx.enter_context(nc.psum_tensor(f"pj{i}", [P, TT, NB], F32)) for i in range(2)]
        pt = ctx.enter_context(nc.psum_tensor("pt", [P, TT, NB], F32))
        pm = ctx.enter_context(nc.psum_tensor("pm", [P, TT, NB], F32))

        ident = cst[:, C_ID, :]

        s_const = sem("const_loaded")
        s_x = sem("x_loaded")
        s_att = sem("att_loaded")
        raw_ready = [sem(f"raw_ready{i}") for i in range(SLOTS)]
        hi_ready = sem("hi_ready")
        lo_ready = sem("lo_ready")
        pe_used = sem("pe_used")
        nm_sq, nm_var, nm_sd, nm_rs, nm_out = (sem(n) for n in ("norm_squares", "norm_var", "norm_sd", "norm_rstd", "norm_scaled"))
        tp, tp_h, tp_l = sem("transposed"), sem("stationary_hi"), sem("stationary_lo")
        in1_evac, out1_evac, in2_evac, out2_evac, wq_evac = (sem(n) for n in ("in1_evac", "out1_evac", "in2_evac", "out2_evac", "wq_evac"))
        ffn_sems = {n: {k: sem(f"{n}_{k}") for k in ("up_evac", "dn_evac", "hid_T", "coef", "coef_h", "coef_l")} for n in ("mlp", "peer")}
        dve_link = sem("dve_link")
        act_link = sem("act_link")
        wt_loaded, wt_h, wt_l, wt_pe, wt_out = (sem(n) for n in ("tail_loaded", "tail_hi", "tail_lo", "tail_product", "tail_out"))

        def link(eng, s, n, ins):
            n[0] += 1
            ins.then_inc(s, 1)
            eng.wait_ge(s, n[0])


        def next_ones(q, j):
            return (q + (j + AHEAD) // SLOTS, (j + AHEAD) % SLOTS)

        def make_hi(act, q, j, first=False):
            act.wait_ge(raw_ready[j], q * 16 + 16)
            if not first:
                act.wait_ge(pe_used, q * SLOTS + j - 3)
            nc.scalar.activation(hi[:, j, :], raw[:, j, :], ACT.Copy).then_inc(hi_ready, 1)

        def make_lo(dve, q, j):
            dve.wait_ge(hi_ready, q * SLOTS + j + 1)
            nc.vector.tensor_tensor(lo[:, j, :], raw[:, j, :], hi[:, j, :].bitcast(F32),
                                    ALU.subtract).then_inc(lo_ready, 1)

        def multiply(pe, q, j, pair, sh, sl, k0, first, last):
            pe.wait_ge(lo_ready, q * SLOTS + j + 1)
            for k in range(4):
                cols = slice(k * NB, (k + 1) * NB)
                for t in range(TT):
                    tok = slice(t * P, (t + 1) * P)
                    begin, end = first and k == 0, last and k == 3
                    nc.tensor.matmul(pair[:, t, :], sh[:, k0 + k, tok], hi[:, j, cols], start=begin, stop=False)
                    nc.tensor.matmul(pair[:, t, :], sh[:, k0 + k, tok], lo[:, j, cols], start=False, stop=False)
                    mm = nc.tensor.matmul(pair[:, t, :], sl[:, k0 + k, tok], hi[:, j, cols], start=False, stop=end)
            mm.then_inc(pe_used, 1)

        def turns(eng, n, body, start=0):
            body(start)
            if n - start > 1:
                with eng.Fori(start + 1, n) as i:
                    body(i)

        def wide_pe(pe, q0, groups, evac):
            def body(i):
                for g in range(2):
                    if not (isinstance(i, int) and i == 0):
                        pe.wait_ge(evac, i * 2 + g - 1)
                    for j in range(SLOTS):
                        multiply(pe, i * 2 + (q0 + g), j, pj[g], xh, xl, 4 * j, j == 0, j == SLOTS - 1)
            turns(pe, groups // 2, body)

        def wide_act(act, q0, groups, evac, out):
            def body(i):
                for g in range(2):
                    for j in range(SLOTS):
                        make_hi(act, *next_ones(i * 2 + (q0 + g), j))
                    if out is not None:
                        act.wait_ge(pe_used, (i * 2 + (q0 + g)) * SLOTS + SLOTS)
                        nc.scalar.activation(out[:, :, bass.ds((i * 2 + g) * NB, NB)], pj[g][:, :, :],
                                             ACT.Copy).then_inc(evac, 1)
            turns(act, groups // 2, body)

        def wide_dve(dve, q0, groups, evac, add):
            def body(i):
                for g in range(2):
                    for j in range(SLOTS):
                        make_lo(dve, *next_ones(i * 2 + (q0 + g), j))
                    if add:
                        dve.wait_ge(pe_used, (i * 2 + (q0 + g)) * SLOTS + SLOTS)
                        part = resid[:, :, bass.ds((i * 2 + g) * NB, NB)]
                        nc.vector.tensor_tensor(part, part, pj[g][:, :, :], ALU.add).then_inc(evac, 1)
            turns(dve, groups // 2, body)


        def job(s, n, last):
            return (5 * s + 1 + n - (1 if last else 0)) % 2

        def ffn_pe(pe, q0, blocks, S, between=None):
            def transposes(s):
                pe.wait_ge(S["up_evac"], s + 1)
                if not (isinstance(s, int) and s == 0):
                    pe.wait_ge(S["coef"], s)
                for k in range(4):
                    for t in range(TT):
                        tr = nc.tensor.transpose(pt[:, :, :].rearrange("p a n -> p (a n)")[:, k * 256 + t * P:k * 256 + t * P + P],
                                                 hid[:, t, k * P:(k + 1) * P], ident)
                tr.then_inc(S["hid_T"], 1)

            for j in range(SLOTS):
                multiply(pe, q0, j, pj[0], xh, xl, 4 * j, j == 0, j == SLOTS - 1)
            if between:
                between()
            transposes(0)

            def part(s, par, last=False):
                first = isinstance(s, int) and s == 0
                if not last:
                    if not first:
                        pe.wait_ge(S["dn_evac"], s * 4 - 1)
                    for j in range(SLOTS):
                        multiply(pe, s * 2 + (q0 + 1), j, pj[job(par, 0, last)], xh, xl, 4 * j, j == 0, j == SLOTS - 1)
                pe.wait_ge(S["coef_l"], s + 1)
                for n in range(4):
                    if n == 1 and not last:
                        transposes(s + 1)
                    w = 4 * s + n - (1 if last else 0)
                    if (n != 1 or last) and not (first and n == 0):
                        pe.wait_ge(S["dn_evac"], w if n == 0 or last else w - 1)
                    multiply(pe, s * 2 + (q0 + (1 if last else 2)), n, pj[job(par, 1 + n, last)],
                             coef_h[par], coef_l[par], 0, True, True)
            ffn_turns(pe, blocks, part)

        def ffn_turns(eng, blocks, part):
            part(0, 0)
            part(1, 1)
            with eng.Fori(1, blocks // 2 - 1) as i:
                part(i * 2, 0)
                part(i * 2 + 1, 1)
            part(blocks - 2, 0)
            part(blocks - 1, 1, last=True)

        def ffn_act(act, q0, blocks, S, func, square, end, between=None):
            def up(s, pair, q):
                act.wait_ge(pe_used, q * SLOTS + SLOTS)
                if not (isinstance(s, int) and s == 0):
                    act.wait_ge(S["hid_T"], s)
                nc.scalar.activation(hid[:, :, :], pair[:, :, :], func).then_inc(S["up_evac"], 1)

            def coefficients(s, par):
                if square:
                    act.wait_ge(S["hid_T"], s + 1)
                    if not (isinstance(s, int) and s == 0):
                        act.wait_ge(S["coef_l"], s)
                    nc.scalar.activation(coef[:, :, :], pt[:, :, :].rearrange("p a (b n) -> p (a b) n", b=2), ACT.Square).then_inc(S["coef"], 1)
                act.wait_ge(S["coef"], s + 1)
                if not square and not (isinstance(s, int) and s == blocks - 1):
                    load_gates(act, s + 1, 1 - par)
                if not (isinstance(s, int) and s <= 1):
                    act.wait_ge(pe_used, (s * 2 + (q0 - 1)) * SLOTS)
                nc.scalar.activation(coef_h[par][:, :, :], coef[:, :, :], ACT.Copy).then_inc(S["coef_h"], 1)

            for j in range(SLOTS):
                make_hi(act, *next_ones(q0, j))
            up(0, pj[0], q0)
            if between:
                between()
            coefficients(0, 0)

            def part(s, par, last=False):
                q = s * 2 + (q0 + 1)
                if not last:
                    for j in range(SLOTS):
                        make_hi(act, *next_ones(q, j))
                    up(s + 1, pj[job(par, 0, False)], q)
                    q = s * 2 + (q0 + 2)
                for j in range(SLOTS):
                    nq, nj = next_ones(q, j)
                    if not (isinstance(nq, int) and nq >= end):
                        make_hi(act, nq, nj)
                    if j == 1 and not last:
                        coefficients(s + 1, 1 - par)
            ffn_turns(act, blocks, part)

        def ffn_dve(dve, q0, blocks, S, gates, end, between=None):
            def coefficients(s, par):
                if gates is not None:
                    dve.wait_ge(S["hid_T"], s + 1)
                    dve.wait_ge(gates[par], (s - par) * 8 + 16 if not isinstance(s, int) else 16 * (s // 2) + 16)
                    if not (isinstance(s, int) and s == 0):
                        dve.wait_ge(S["coef_l"], s)
                    nc.vector.tensor_tensor(
                        coef[:, :, :].rearrange("p b (o t) -> p b o t", o=8),
                        pt[:, :, :].rearrange("p a (b n) -> p (a b) n", b=2).rearrange("p b (o t) -> p b o t", o=8),
                        gate_e[par][:, :, :, :].rearrange("p o b t -> p b o t"), ALU.mult).then_inc(S["coef"], 1)

            def coefficients_lo(s, par):
                dve.wait_ge(S["coef_h"], s + 1)
                nc.vector.tensor_tensor(coef_l[par][:, :, :], coef[:, :, :], coef_h[par][:, :, :].bitcast(F32),
                                        ALU.subtract).then_inc(S["coef_l"], 1)

            for j in range(SLOTS):
                make_lo(dve, *next_ones(q0, j))
            if between:
                between()
            coefficients(0, 0)
            coefficients_lo(0, 0)

            def part(s, par, last=False):
                q = s * 2 + (q0 + 1)
                if not last:
                    for j in range(SLOTS):
                        make_lo(dve, *next_ones(q, j))
                    q = s * 2 + (q0 + 2)
                for j in range(SLOTS):
                    nq, nj = next_ones(q, j)
                    if not (isinstance(nq, int) and nq >= end):
                        make_lo(dve, nq, nj)
                    if j == 2 and not last:
                        coefficients_lo(s + 1, 1 - par)
                    dve.wait_ge(pe_used, q * SLOTS + j + 1)
                    part_ = resid[:, :, j * NB:(j + 1) * NB]
                    nc.vector.tensor_tensor(part_, part_, pj[job(par, 1 + j, last)][:, :, :],
                                            ALU.add).then_inc(S["dn_evac"], 1)
                    if j == 1 and not last:
                        coefficients(s + 1, 1 - par)
            ffn_turns(dve, blocks, part)


        def norm_act(act, n):
            for t in range(TT):
                ins = nc.scalar.activation(nat[:, t, :], resid[:, t, :], ACT.Square, accum_out=stat[:, t:t + 1])
                ins.then_inc(nm_sq, 1)
            act.wait_ge(nm_var, n + 1)
            nc.scalar.activation(stat[:, 4:6], stat[:, 2:4], ACT.Sqrt).then_inc(nm_sd, 1)

        def norm_dve(dve, n, out, gain=None):
            dve.wait_ge(nm_sq, 2 * n + 2)
            nc.vector.tensor_scalar(stat[:, 2:4], stat[:, 0:2], 1.0 / D, EPS, ALU.mult, ALU.add).then_inc(nm_var, 1)
            dve.wait_ge(nm_sd, n + 1)
            nc.vector.reciprocal(stat[:, 6:8], stat[:, 4:6]).then_inc(nm_rs, 1)
            dve.wait_ge(nm_rs, n + 1)
            for t in range(TT):
                if gain is None:
                    ins = nc.vector.tensor_scalar(out[:, t, :], resid[:, t, :], stat[:, 6 + t:7 + t], None, ALU.mult)
                else:
                    ins = nc.vector.scalar_tensor_tensor(out[:, t, :], resid[:, t, :], stat[:, 6 + t:7 + t], gain,
                                                         ALU.mult, ALU.mult)
                ins.then_inc(nm_out, 1)


        def station_pe(pe, n, src):
            for b in range(4):
                if b >= 2:
                    pe.wait_ge(tp_l, 4 * n + b - 1)
                for k in range(4):
                    for t in range(TT):
                        col = (4 * b + k) * P
                        at = (k % 2) * 256 + t * P
                        tr = nc.tensor.transpose(pj[b % 2][:, k // 2, at:at + P], src[:, t, col:col + P], ident)
                tr.then_inc(tp, 1)

        def station_act(act, n, gain):
            for b in range(4):
                act.wait_ge(tp, 4 * n + b + 1)
                for k in range(4):
                    ins = nc.scalar.activation(xh[:, 4 * b + k, :], pj[b % 2][:, k // 2, (k % 2) * 256:(k % 2) * 256 + 256],
                                               ACT.Copy, scale=small[:, gain(4 * b + k):gain(4 * b + k) + 1])
                ins.then_inc(tp_h, 1)

        def station_dve(dve, n, gain):
            for b in range(4):
                dve.wait_ge(tp_h, 4 * n + b + 1)
                for k in range(4):
                    ins = nc.vector.scalar_tensor_tensor(
                        xl[:, 4 * b + k, :], pj[b % 2][:, k // 2, (k % 2) * 256:(k % 2) * 256 + 256],
                        small[:, gain(4 * b + k):gain(4 * b + k) + 1], xh[:, 4 * b + k, :].bitcast(F32),
                        ALU.mult, ALU.subtract)
                ins.then_inc(tp_l, 1)


        def tail_act(act, n, cols):
            act.wait_ge(wt_loaded, 16 * n + 16)
            nc.scalar.activation(wtail_h[:, :, 0:cols], wtail[:, :, 0:cols], ACT.Copy).then_inc(wt_h, 1)

        def tail_dve(dve, n, cols):
            dve.wait_ge(wt_h, n + 1)
            nc.vector.tensor_tensor(wtail_l[:, :, 0:cols], wtail[:, :, 0:cols], wtail_h[:, :, 0:cols].bitcast(F32),
                                    ALU.subtract).then_inc(wt_l, 1)

        def tail_pe(pe, n, cols):
            pe.wait_ge(wt_l, n + 1)
            for t in range(TT):
                tok = slice(t * P, (t + 1) * P)
                for k in range(KT):
                    o = pm[:, t, 0:cols]
                    nc.tensor.matmul(o, xh[:, k, tok], wtail_h[:, k, 0:cols], start=k == 0, stop=False)
                    nc.tensor.matmul(o, xh[:, k, tok], wtail_l[:, k, 0:cols], start=False, stop=False)
                    mm = nc.tensor.matmul(o, xl[:, k, tok], wtail_h[:, k, 0:cols], start=False, stop=k == KT - 1)
            mm.then_inc(wt_pe, 1)

        NH = 2 * H
        qk_cp, qk_T = sem("qk_copied"), sem("qk_transposed")
        z_done, z_read, fz_read, sp_ln, sp_done = sem("scores"), sem("sb_scores_read"), sem("fox_scores_read"), sem("sb_log"), sem("sb_softplus")
        cum_done, a_done, o_done, o_cp, o_sq = sem("cumulated"), sem("weights"), sem("out_summed"), sem("out_copied"), sem("out_squared")
        lfu_done, mx_done, p_done, rs_done, lf_done = sem("decay_factors"), sem("fox_max"), sem("fox_exp"), sem("fox_inverse_sum"), sem("log_f")
        hn_var, hn_sd, hn_rs, hn_out = sem("head_var"), sem("head_sd"), sem("head_rstd"), sem("head_scaled")
        lf_x, lf_ln = sem("lf_logit"), sem("lf_log")
        att_start = sem("att_start")

        def qcol(h):
            return h * P if h < H else 3 * H * P + (h - H) * P

        z_bank = [pj[1][:, 0, 0:384], pj[1][:, 1, 0:384], pt[:, 0, 0:384]]
        t_bank = [pj[0][:, 0, :], pj[0][:, 1, :]]
        pT_bank = pt[:, 1, 0:384]

        def att1_pe(pe):
            def transpose_qk(h):
                if h >= 2:
                    pe.wait_ge(qk_cp, h - 1)
                for i in range(2):
                    for t in range(TT):
                        c = qcol(h) + i * H * P
                        tr = nc.tensor.transpose(t_bank[h % 2][:, i * 256 + t * P:i * 256 + t * P + P], proj1[:, t, c:c + P], ident)
                tr.then_inc(qk_T, 1)

            def scores(h):
                pe.wait_ge(qk_cp, h + 1)
                if h >= 3:
                    if h - 3 < H:
                        pe.wait_ge(z_read, h - 2)
                    else:
                        pe.wait_ge(fz_read, h - 2 - H)
                z, qT, kT = z_bank[h % 3], qkT[h % 2][:, 0, :], qkT[h % 2][:, 1, :]
                if h < H:
                    nc.tensor.matmul(z[:, 0:256], kT[:, 0:P], qT[:, 0:256], start=True, stop=False, skip_group_check=True)
                    mm = nc.tensor.matmul(z[:, 256:384], kT[:, P:256], qT[:, P:256], start=False, stop=False, skip_group_check=True)
                else:
                    g = lfU[h % 2]
                    pe.wait_ge(lfu_done, h - H + 1)
                    nc.tensor.matmul(z[:, 0:P], qT[:, 0:P], kT[:, 0:P], start=True, stop=False, skip_group_check=True)
                    nc.tensor.matmul(z[:, 0:P], g[:, 0, :], cst[:, C_GT, :], start=False, stop=False, skip_group_check=True)
                    nc.tensor.matmul(z[:, P:384], qT[:, P:256], kT[:, 0:256], start=False, stop=False, skip_group_check=True)
                    nc.tensor.matmul(z[:, P:384], g[:, 1, :], cst[:, C_ONES:C_ONES + 2, :].rearrange("p a n -> p (a n)"), start=False, stop=False, skip_group_check=True)
                    mm = nc.tensor.matmul(z[:, P:256], g[:, 2, :], cst[:, C_GT, :], start=False, stop=True, skip_group_check=True)
                mm.then_inc(z_done, 1)

            def cumulate(h):
                z = z_bank[h % 3]
                if h < H:
                    pe.wait_ge(sp_done, h + 1)
                    s_ = sc_s[h % 2]
                    nc.tensor.matmul(z[:, 0:256], att[:, A_NGE, :], s_[:, 0:256], start=False, stop=False, skip_group_check=True)
                    nc.tensor.matmul(z[:, P:256], att[:, A_NONES, :], s_[:, 256:384], start=False, stop=False, skip_group_check=True)
                    mm = nc.tensor.matmul(z[:, 256:384], att[:, A_NGE, :], s_[:, 256:384], start=False, stop=True, skip_group_check=True)
                else:
                    pe.wait_ge(p_done, h - H + 1)
                    pe.wait_ge(a_done, h)
                    for i in range(3):
                        mm = nc.tensor.transpose(pT_bank[:, i * P:(i + 1) * P], sc_e[h % 2][:, i * P:(i + 1) * P], ident)
                mm.then_inc(cum_done, 1)

            def sum_v(h):
                pe.wait_ge(a_done, h + 1)
                if h >= 2:
                    pe.wait_ge(o_cp, h - 1)
                o, a, c = pm[:, h % 2, :], aT[h % 2], qcol(h) + 2 * H * P
                nc.tensor.matmul(o[:, 0:P], a[:, 0:P], proj1[:, 0, c:c + P], start=True, stop=False, skip_group_check=True)
                nc.tensor.matmul(o[:, P:256], a[:, P:256], proj1[:, 0, c:c + P], start=False, stop=False, skip_group_check=True)
                nc.tensor.matmul(o[:, P:256], a[:, 256:384], proj1[:, 1, c:c + P], start=False, stop=True,
                                 skip_group_check=True).then_inc(o_done, 1)

            pe.wait_ge(in1_evac, G1)
            pe.wait_ge(wt_out, 1)
            pe.wait_ge(s_att, 16)
            for i in range(NH + 3):
                for stage, f in enumerate((transpose_qk, scores, cumulate, sum_v)):
                    if 0 <= i - stage < NH:
                        f(i - stage)

        def att1_act(act, n):
            def exponents(h):
                e = sc_e[h % 2]
                if h >= 2:
                    act.wait_ge(cum_done, h - 1)
                if h < H:
                    act.wait_ge(z_done, h + 1)
                    link(act, act_link, n, nc.scalar.activation(e[:, :], z_bank[h % 3], ACT.Abs))
                    link(act, act_link, n, nc.scalar.activation(e[:, :], e[:, :], ACT.Exp, scale=-1.0))
                    nc.scalar.activation(e[:, :], e[:, :], ACT.Ln, bias=1.0).then_inc(sp_ln, 1)
                else:
                    act.wait_ge(mx_done, h - H + 1)
                    f, s_ = fx[:, :, h - H, :], sc_s[h % 2]
                    nc.scalar.activation(e[:, 0:P], s_[:, 0:P], ACT.Exp, bias=f[:, 0, 0:1], accum_out=f[:, 0, 1:2])
                    nc.scalar.activation(e[:, P:384], s_[:, P:384], ACT.Exp, bias=f[:, 1, 0:1],
                                         accum_out=f[:, 1, 1:2]).then_inc(p_done, 1)

            def weights(h):
                if h >= 2:
                    act.wait_ge(o_done, h - 1)
                if h < H:
                    act.wait_ge(z_read, h + 1)
                    nc.scalar.activation(aT[h % 2][:, :], sc_a[h % 2][:, :], ACT.Exp).then_inc(a_done, 1)
                else:
                    act.wait_ge(cum_done, h + 1)
                    nc.scalar.activation(aT[h % 2][:, :], pT_bank, ACT.Copy).then_inc(a_done, 1)

            def squares(h):
                act.wait_ge(o_cp, h + 1)
                if h >= 2:
                    act.wait_ge(o_sq, h - 1)
                for t in range(TT):
                    ins = nc.scalar.activation(junk[:, h % 2, t, :], proj1[:, t, h * P:(h + 1) * P], ACT.Square, accum_out=hss[:, t, h:h + 1])
                ins.then_inc(o_sq, 1)

            act.wait_ge(lf_x, 1)
            link(act, act_link, n, nc.scalar.activation(sp_t[:, 1, :, 0:H], sp_t[:, 0, :, 0:H], ACT.Abs))
            link(act, act_link, n, nc.scalar.activation(sp_t[:, 1, :, 0:H], sp_t[:, 1, :, 0:H], ACT.Exp, scale=-1.0))
            nc.scalar.activation(sp_t[:, 1, :, 0:H], sp_t[:, 1, :, 0:H], ACT.Ln, bias=1.0).then_inc(lf_ln, 1)
            for i in range(NH + 3):
                for stage, f in enumerate((None, exponents, weights, squares)):
                    if f and 0 <= i - stage < NH:
                        f(i - stage)
            act.wait_ge(hn_var, 1)
            nc.scalar.activation(hrs[:, :, :], hss[:, :, :], ACT.Sqrt).then_inc(hn_sd, 1)

        def att1_dve(dve, n):
            def copy_qk(h):
                dve.wait_ge(qk_T, h + 1)
                if h >= 2:
                    dve.wait_ge(z_done, h - 1)
                nc.vector.tensor_scalar(qkT[h % 2][:, 0, :], t_bank[h % 2][:, 0:256], SCALE, None, ALU.mult)
                nc.vector.tensor_copy(qkT[h % 2][:, 1, :], t_bank[h % 2][:, 256:512]).then_inc(qk_cp, 1)

            def exponents(h):
                s_ = sc_s[h % 2]
                if h < H:
                    dve.wait_ge(sp_ln, h + 1)
                    link(dve, dve_link, n, nc.vector.scalar_tensor_tensor(s_[:, :], z_bank[h % 3], 0.0, sc_e[h % 2][:, :], ALU.max, ALU.add))
                    nc.vector.tensor_tensor(s_[:, :], s_[:, :], att[:, A_SBM:A_SBM + 3, :].rearrange("p a n -> p (a n)"),
                                            ALU.mult).then_inc(sp_done, 1)
                else:
                    dve.wait_ge(z_done, h + 1)
                    if h >= H + 2:
                        dve.wait_ge(p_done, h - H - 1)
                    nc.vector.tensor_tensor(s_[:, :], z_bank[h % 3], att[:, A_FXA:A_FXA + 3, :].rearrange("p a n -> p (a n)"),
                                            ALU.add).then_inc(fz_read, 1)
                    dve.wait_ge(fz_read, h - H + 1)
                    f = fx[:, :, h - H, :]
                    nc.vector.tensor_reduce(f[:, 0, 0:1], s_[:, 0:P], AX.X, ALU.max, negate=True)
                    nc.vector.tensor_reduce(f[:, 1, 0:1], s_[:, P:384], AX.X, ALU.max, negate=True).then_inc(mx_done, 1)

            def weights(h):
                if h < H:
                    dve.wait_ge(cum_done, h + 1)
                    if h >= 2:
                        dve.wait_ge(a_done, h - 1)
                    nc.vector.scalar_tensor_tensor(sc_a[h % 2][:, :], z_bank[h % 3], 0.0,
                                                   att[:, A_SBA:A_SBA + 3, :].rearrange("p a n -> p (a n)"),
                                                   ALU.min, ALU.add).then_inc(z_read, 1)
                else:
                    dve.wait_ge(p_done, h - H + 1)
                    nc.vector.reciprocal(fx[:, :, h - H, 2:3], fx[:, :, h - H, 1:2]).then_inc(rs_done, 1)

            def copy_o(h):
                dve.wait_ge(o_done, h + 1)
                o = pm[:, h % 2, 0:256].rearrange("p (t n) -> p t n", t=TT)
                if h < H:
                    nc.vector.tensor_copy(proj1[:, :, h * P:(h + 1) * P], o).then_inc(o_cp, 1)
                else:
                    dve.wait_ge(rs_done, h - H + 1)
                    for t in range(TT):
                        ins = nc.vector.tensor_scalar(proj1[:, t, h * P:(h + 1) * P], o[:, t, :], fx[:, t, h - H, 2:3], None, ALU.mult)
                    ins.then_inc(o_cp, 1)

            dve.wait_ge(wt_pe, 1)
            nc.vector.tensor_copy(tail[:, :, 0:H], pm[:, :, 0:H]).then_inc(wt_out, 1)
            dve.wait_ge(wt_out, 1)
            nc.vector.tensor_tensor(sp_t[:, 0, :, 0:H], tail[:, :, 0:H],
                                    small[:, S_BF:S_BF + H].unsqueeze(1).broadcast_to([P, TT, H]), ALU.add).then_inc(lf_x, 1)
            dve.wait_ge(lf_ln, 1)
            nc.vector.scalar_tensor_tensor(lf[:, :, :], sp_t[:, 0, :, 0:H], 0.0, sp_t[:, 1, :, 0:H],
                                           ALU.min, ALU.subtract).then_inc(lf_done, 1)
            for i in range(NH + 3):
                for stage, f in enumerate((copy_qk, exponents, weights, copy_o)):
                    if 0 <= i - stage < NH:
                        f(i - stage)
            dve.wait_ge(o_sq, NH)
            nc.vector.tensor_scalar(hss[:, :, :], hss[:, :, :], 1.0 / HD, EPS, ALU.mult, ALU.add).then_inc(hn_var, 1)
            dve.wait_ge(hn_sd, 1)
            nc.vector.reciprocal(hss[:, :, :], hrs[:, :, :]).then_inc(hn_rs, 1)
            dve.wait_ge(hn_rs, 1)
            for t in range(TT):
                o = proj1[:, t, 0:D].rearrange("p (h n) -> p h n", h=NH)
                nc.vector.tensor_tensor(o, o, hss[:, t, :].unsqueeze(2).broadcast_to([P, NH, HD]), ALU.mult).then_inc(hn_out, 1)

        def att1_pool(pool):
            pool.wait_ge(lf_done, 1)
            for h in range(H):
                if h >= 2:
                    pool.wait_ge(z_done, H + h - 1)
                g = lfU[h % 2]
                nc.gpsimd.tensor_scalar(g[:, 0, :], cst[:, C_LE, :], lf[:, 0, h:h + 1], None, ALU.mult)
                nc.gpsimd.tensor_scalar(g[:, 1, :], cst[:, C_LE, :], lf[:, 1, h:h + 1], None, ALU.mult)
                nc.gpsimd.tensor_scalar(g[:, 2, :], cst[:, C_ONES, :], lf[:, 0, h:h + 1], None, ALU.mult).then_inc(lfu_done, 1)

        A_Q, A_F, A_I, A_G = 0, H * P, 2 * H * P, 3 * H * P
        B_Q, B_K, B_V, B_Z = 4 * H * P, 4 * H * P + 512, 5 * H * P, 6 * H * P
        at_z = at_y + 4 * TT * W2

        s = region(at_x)
        hk = s("hk", [P, TT, H * P])
        at_h = at_x + 4 * TT * H * P
        s = region(at_h)
        hsig = s("hsig", [P, TT, H * P])
        lb = s("lb", [P, 2, H * P])
        lbl = region(at_z)("lbl", [P, 2, H * P])
        s = region(at_h)
        hE = [s(f"hE{i}", [P, 8, P]) for i in range(2)]
        hKE = [s(f"hKE{i}", [P, 8, P]) for i in range(2)]
        hqk = [s(f"hqk{i}", [P, 2, TT * P]) for i in range(2)]
        hA = s("hA", [P, 8, P])
        z = region(at_z)
        haT = [z(f"haT{i}", [P, 3 * P]) for i in range(2)]
        hkx = [z(f"hkx{i}", [P, P]) for i in range(2)]
        hjunk = z("hjunk", [P, 2, TT, P])
        mss = z("mss", [P, TT, 2 * H])
        mrs = z("mrs", [P, TT, 2 * H])
        at_z2 = at_z + 4 * (6 * P + 2 * P + 4 * P + 64)

        lbl_in, lb_steps, h_sig, h_f, h_logf = sem("lbl_loaded"), sem("lower_bound_steps"), sem("h_sigmoid"), sem("h_forget"), sem("h_log_forget")
        h_key, h_T, h_qk, h_X, h_E = sem("h_key"), sem("h_transposed"), sem("h_qk_copied"), sem("h_decay_sums"), sem("h_decays")
        h_KE, h_QE, h_A, h_aT, h_x, h_o, h_ocp, h_osq = (sem(n) for n in ("h_key_decayed", "h_query_decayed", "h_products", "h_weights", "h_cross", "h_out", "h_out_copied", "h_out_squared"))

        def hg_steps(fs):
            for i in range(2 * H + 4):
                for lag, f in fs:
                    if 0 <= i - lag < 2 * H:
                        f(i - lag)

        def hgrn_pe(pe):
            def products(c):
                h, t = c // 2, c % 2
                pe.wait_ge(h_QE, c + 1)
                pe.wait_ge(h_KE, c + 1)
                if c >= 1:
                    pe.wait_ge(h_aT, c)
                lev = 1 - t
                A = pt[:, :, :].rearrange("p a (b n) -> p (a b) n", n=P)
                k_, q_ = hqk[h % 2][:, 1, t * P:t * P + P], hqk[h % 2][:, 0, t * P:t * P + P]
                for b in range(2):
                    for i in range(4):
                        l = 4 * b + i - 1
                        kk, qq = (k_, q_) if l < 0 else (hKE[c % 2][:, lev + l, :], hE[c % 2][:, lev + l, :])
                        mm = nc.tensor.matmul(A[:, 4 * b + i, :], kk, qq, start=i == 0, stop=i == 3, skip_group_check=True)
                mm.then_inc(h_A, 1)
                if t == 1:
                    if h >= 1:
                        pe.wait_ge(h_x, h)
                    nc.tensor.matmul(pj[0][:, 1, 0:P], hkx[h % 2][:, :], hE[c % 2][:, 7, :], start=True, stop=True).then_inc(h_A, 1)

            def decay_sums(c):
                h, t = c // 2, c % 2
                if c >= 1:
                    pe.wait_ge(h_E, c)
                g = proj2[:, t, A_F + h * P:A_F + (h + 1) * P]
                for b in range(2):
                    c0 = (C_GT if t == 0 else C_LEV) + 4 * b
                    mm = nc.tensor.matmul(pj[1][:, b, :], g, cst[:, c0:c0 + 4, :].rearrange("p a n -> p (a n)"), start=True, stop=True)
                mm.then_inc(h_X, 1)

            def transposes(c):
                h, t = c // 2, c % 2
                if t:
                    return
                if h >= 1:
                    pe.wait_ge(h_qk, h)
                for i, src in enumerate((proj2[:, :, A_Q + h * P:A_Q + (h + 1) * P], hk[:, :, h * P:(h + 1) * P])):
                    for t in range(TT):
                        tr = nc.tensor.transpose(pj[0][:, 0, i * 256 + t * P:i * 256 + t * P + P], src[:, t, :], ident)
                tr.then_inc(h_T, 1)

            def sum_v(c):
                h, t = c // 2, c % 2
                if t == 0:
                    return
                pe.wait_ge(h_aT, c + 1)
                pe.wait_ge(h_x, h + 1)
                if h >= 2:
                    pe.wait_ge(h_ocp, h - 1)
                o, a, v0 = pm[:, h % 2, :], haT[h % 2], A_I + h * P
                nc.tensor.matmul(o[:, 0:P], a[:, 0:P], proj2[:, 0, v0:v0 + P], start=True, stop=False, skip_group_check=True)
                nc.tensor.matmul(o[:, P:256], a[:, P:256], proj2[:, 0, v0:v0 + P], start=False, stop=False, skip_group_check=True)
                nc.tensor.matmul(o[:, P:256], a[:, 256:384], proj2[:, 1, v0:v0 + P], start=False, stop=True,
                                 skip_group_check=True).then_inc(h_o, 1)

            pe.wait_ge(h_logf, 1)
            pe.wait_ge(h_key, 1)
            hg_steps(((2, products), (0, transposes), (0, decay_sums), (3, sum_v)))

        def hgrn_act(act, n):
            def copy_qk(c):
                h = c // 2
                if c % 2:
                    return
                act.wait_ge(h_T, h + 1)
                if h >= 2:
                    act.wait_ge(h_A, 3 * (h - 1))
                    act.wait_ge(h_KE, 2 * (h - 1))
                    act.wait_ge(h_QE, 2 * (h - 1))
                nc.scalar.activation(hqk[h % 2][:, :, :].rearrange("p a n -> p (a n)"), pj[0][:, 0, :], ACT.Copy).then_inc(h_qk, 1)

            def decays(c):
                act.wait_ge(h_X, c + 1)
                if c >= 2:
                    act.wait_ge(h_A, (c - 2) // 2 * 3 + 1 + 2 * ((c - 2) % 2))
                nc.scalar.activation(hE[c % 2][:, :, :].rearrange("p a n -> p (a n)"), pj[1][:, :, :].rearrange("p a n -> p (a n)"), ACT.Exp).then_inc(h_E, 1)

            def cross(c):
                h = c // 2
                if c % 2 == 0:
                    return
                act.wait_ge(h_A, 3 * h + 3)
                if h >= 2:
                    act.wait_ge(h_o, h - 1)
                nc.scalar.activation(haT[h % 2][:, P:256], pj[0][:, 1, 0:P], ACT.Copy).then_inc(h_x, 1)

            def squares(c):
                h = c // 2
                if c % 2 == 0:
                    return
                act.wait_ge(h_ocp, h + 1)
                if h >= 2:
                    act.wait_ge(h_osq, h - 1)
                for t in range(TT):
                    ins = nc.scalar.activation(hjunk[:, h % 2, t, :], proj2[:, t, h * P:(h + 1) * P], ACT.Square, accum_out=mss[:, t, h:h + 1])
                ins.then_inc(h_osq, 1)

            f_ = proj2[:, :, A_F:A_F + H * P]
            act.wait_ge(in2_evac, G2)
            act.wait_ge(lb_steps, 2)
            nc.scalar.activation(lb[:, :, :], lbl[:, :, :], ACT.Exp).then_inc(lb_steps, 1)
            nc.scalar.activation(hsig[:, :, :], f_, ACT.Sigmoid).then_inc(h_sig, 1)
            nc.scalar.activation(hk[:, :, :], f_, ACT.Sigmoid, scale=-1.0).then_inc(h_sig, 1)
            act.wait_ge(h_f, 2)
            nc.scalar.activation(f_, hsig[:, :, :], ACT.Ln).then_inc(h_logf, 1)
            hg_steps(((0, copy_qk), (0, decays), (2, cross), (3, squares)))

        def hgrn_dve(dve, n):
            def queries(c):
                h, t = c // 2, c % 2
                dve.wait_ge(h_KE, c + 1)
                e = hE[c % 2]
                q_ = hqk[h % 2][:, 0, t * P:t * P + P]
                nc.vector.tensor_tensor(e[:, :, :], e[:, :, :], q_.unsqueeze(1).broadcast_to([P, 8, P]), ALU.mult).then_inc(h_QE, 1)

            def weights(c):
                h, t = c // 2, c % 2
                dve.wait_ge(h_A, 3 * h + 1 + t)
                link(dve, dve_link, n, nc.vector.tensor_tensor(
                    hA[:, :, :], pt[:, :, :].rearrange("p a (b n) -> p (a b) n", n=P), cst[:, C_MASK:C_MASK + 8, :], ALU.mult))
                if t == 0 and h >= 2:
                    dve.wait_ge(h_o, h - 1)
                nc.vector.tensor_reduce(haT[h % 2][:, 2 * t * P:2 * t * P + P], hA[:, :, :].rearrange("p a n -> p n a"), AX.X, ALU.add).then_inc(h_aT, 1)

            def copy_o(c):
                h = c // 2
                if c % 2 == 0:
                    return
                dve.wait_ge(h_o, h + 1)
                nc.vector.tensor_copy(proj2[:, :, h * P:(h + 1) * P], pm[:, h % 2, 0:256].rearrange("p (t n) -> p t n", t=TT)).then_inc(h_ocp, 1)

            dve.wait_ge(lbl_in, 16)
            nc.vector.tensor_tensor(lb[:, 0, :], lbl[:, 0, :], lbl[:, 1, :], ALU.max).then_inc(lb_steps, 1)
            dve.wait_ge(lb_steps, 1)
            nc.vector.tensor_tensor(lbl[:, :, :], lbl[:, :, :], lb[:, 0, :].unsqueeze(1).broadcast_to([P, 2, H * P]), ALU.subtract).then_inc(lb_steps, 1)
            dve.wait_ge(lb_steps, 3)
            link(dve, dve_link, n, nc.vector.tensor_tensor(lb[:, 1, :], lb[:, 1, :], lb[:, 0, :], ALU.add))
            link(dve, dve_link, n, nc.vector.reciprocal(lbl[:, 0, :], lb[:, 1, :]))
            link(dve, dve_link, n, nc.vector.tensor_tensor(lb[:, 0, :], lb[:, 0, :], lbl[:, 0, :], ALU.mult))
            link(dve, dve_link, n, nc.vector.tensor_scalar(lb[:, 1, :], lb[:, 0, :], -1.0, 1.0, ALU.mult, ALU.add))
            over = lambda i: lb[:, i, :].unsqueeze(1).broadcast_to([P, TT, H * P])
            dve.wait_ge(h_sig, 2)
            nc.vector.tensor_tensor(hsig[:, :, :], hsig[:, :, :], over(1), ALU.mult).then_inc(h_f, 1)
            dve.wait_ge(h_f, 1)
            nc.vector.tensor_tensor(hsig[:, :, :], hsig[:, :, :], over(0), ALU.add).then_inc(h_f, 1)
            nc.vector.tensor_tensor(hk[:, :, :], hk[:, :, :], over(1), ALU.mult).then_inc(h_key, 1)
            hg_steps(((2, weights), (0, queries), (3, copy_o)))

        def hgrn_pool(pool):
            pool.wait_ge(h_logf, 1)
            pool.wait_ge(h_key, 1)
            for c in range(2 * H):
                h, t = c // 2, c % 2
                pool.wait_ge(h_E, c + 1)
                pool.wait_ge(h_qk, h + 1)
                if c >= 2:
                    pool.wait_ge(h_A, (c - 2) // 2 * 3 + 1 + 2 * ((c - 2) % 2))
                k_ = hqk[h % 2][:, 1, t * P:t * P + P]
                if t == 0:
                    nc.gpsimd.tensor_tensor(hkx[h % 2][:, :], hE[c % 2][:, 0, :], k_, ALU.mult)
                lev = 1 - t
                nc.gpsimd.tensor_tensor(hKE[c % 2][:, lev:lev + 7, :], hE[c % 2][:, lev:lev + 7, :],
                                        k_.unsqueeze(1).broadcast_to([P, 7, P]), ALU.mult).then_inc(h_KE, 1)

        s = region(at_x)
        dN = s("dN", [P, 16, P])
        dT = s("dT", [P, 16, P])
        dU = s("dU", [P, 16, P])
        dB = [s(f"dB{i}", [P, 4, P]) for i in range(2)]
        dP = [s(f"dP{i}", [P, 4, P]) for i in range(2)]
        s = region(at_x)
        dqg = s("dqg", [P, H, P])
        dqgT = s("dqgT", [P, H, P])
        s = region(at_x + 4 * 16 * P)
        cy = [s(f"cy{i}", [P, TT * P]) for i in range(4)]
        dkb = [s(f"dkb{i}", [P, 4, P]) for i in range(2)]
        dsq = s("dsq", [P, TT, 2 * 512])
        s = region(at_x + 4 * 32 * P)
        dgS = [s(f"dgS{i}", [P, 4, P]) for i in range(2)]
        dE = [s(f"dE{i}", [P, 4, P]) for i in range(2)]
        s = region(at_x + 4 * 16 * P)
        dS = s("dS", [P, H, P])
        dwT = s("dwT", [P, H, P])
        s = region(at_x + 4 * 48 * P)
        dvn = [s(f"dvn{i}", [P, 4, P]) for i in range(4)]
        z = region(at_z)
        dkq = z("dkq", [P, 4, P])
        dkbT = z("dkbT", [P, 4, P])
        dEm = z("dEm", [P, 4, P])
        z = region(at_z2)
        gt = z("gt", [P, 6, TT, H])
        dn = z("dn", [P, 3, TT, H])
        dkd = proj2[:, 0, A_I:A_I + H * P].rearrange("p (a n) -> p a n", a=H)
        dX = proj2[:, 1, A_I:A_I + H * P].rearrange("p (a n) -> p a n", a=H)

        def aqk(m):
            return proj2[:, m // 2, A_F + (m % 2) * 512:A_F + (m % 2) * 512 + 512]

        c_T, c_tap, c_y, c_silu, c_B, c_out = sem("c_transposed"), sem("c_taps"), sem("c_convolved"), sem("c_silu"), sem("c_back"), sem("c_out")
        g_step, g_pe = sem("gate_steps"), sem("gate_sums")
        l_step = sem("l2_steps")
        d_pool, d_vb, d_T, d_cp, d_E, d_Em, d_S, d_N = (sem(n) for n in ("d_operands", "d_vbeta", "d_transposed", "d_copied", "d_decays", "d_masked", "d_scores", "d_weighted"))
        d_B, d_PP, d_Pc, d_dd, d_TU = (sem(n) for n in ("inv_level", "inv_product", "inv_copied", "inv_deltas", "inv_updated"))
        f_pe, f_cp, f_dve, f_pool = sem("state_products"), sem("state_copied"), sem("state_out"), sem("state_queries")
        m_step = sem("mix_steps")
        NL = 7

        def conv_pe(pe):
            def forward(c):
                if c >= 2:
                    pe.wait_ge(c_y, c - 1)
                for t in range(TT):
                    tr = nc.tensor.transpose(pj[0][:, c % 2, t * P:t * P + P], proj2[:, t, B_Q + c * P:B_Q + (c + 1) * P], ident)
                tr.then_inc(c_T, 1)

            def back(c):
                pe.wait_ge(c_silu, c + 1)
                if c >= 2:
                    pe.wait_ge(c_out, c - 1)
                for t in range(TT):
                    tr = nc.tensor.transpose(pj[1][:, c % 2, t * P:t * P + P], cy[c % 4][:, t * P:t * P + P], ident)
                tr.then_inc(c_B, 1)

            pe.wait_ge(h_osq, H)
            pe.wait_ge(h_ocp, H)
            for i in range(18):
                if i < 16:
                    forward(i)
                if i >= 2:
                    back(i - 2)

        def conv_act(act, n):
            for i in range(18):
                if i < 16:
                    act.wait_ge(c_y, i + 1)
                    nc.scalar.activation(cy[i % 4][:, :], cy[i % 4][:, :], ACT.Silu).then_inc(c_silu, 1)
                if i >= 2:
                    c = i - 2
                    act.wait_ge(c_B, c + 1)
                    nc.scalar.activation(proj2[:, :, B_Q + c * P:B_Q + (c + 1) * P],
                                         pj[1][:, c % 2, 0:256].rearrange("p (t n) -> p t n", t=TT), ACT.Copy).then_inc(c_out, 1)

        def conv_dve(dve, n):
            w = lambda c, j: small[:, S_CONV + 4 * c + j:S_CONV + 4 * c + j + 1]
            for c0 in range(0, 16, 2):
                for j in range(4):
                    for c in (c0, c0 + 1):
                        y_, x_ = cy[c % 4], pj[0][:, c % 2, 0:256]
                        if j == 0:
                            dve.wait_ge(c_T, c + 1)
                            if c >= 4:
                                dve.wait_ge(c_B, c - 3)
                            nc.vector.tensor_scalar(y_[:, :], x_, w(c, 3), None, ALU.mult).then_inc(c_tap, 1)
                        else:
                            dve.wait_ge(c_tap, 3 * c0 + (c - c0) + 2 * (j - 1) + 1)
                            ins = nc.vector.scalar_tensor_tensor(y_[:, j:], x_[:, 0:256 - j], w(c, 3 - j), y_[:, j:], ALU.mult, ALU.add)
                            ins.then_inc(c_tap if j < 3 else c_y, 1)

        def gates_act(act, n):
            nc.scalar.activation(gt[:, 0, :, :], tail[:, :, 0:H], ACT.Sigmoid).then_inc(g_step, 1)
            act.wait_ge(g_step, 2)
            link(act, act_link, n, nc.scalar.activation(gt[:, 2, :, :], gt[:, 1, :, :], ACT.Abs))
            link(act, act_link, n, nc.scalar.activation(gt[:, 2, :, :], gt[:, 2, :, :], ACT.Exp, scale=-1.0))
            nc.scalar.activation(gt[:, 4, 0, :], small[:, S_ALOG:S_ALOG + H], ACT.Exp)
            nc.scalar.activation(gt[:, 2, :, :], gt[:, 2, :, :], ACT.Ln, bias=1.0).then_inc(g_step, 1)
            act.wait_ge(g_pe, 1)
            nc.scalar.activation(gt[:, 5, :, :], pm[:, 0, 0:2 * H].rearrange("p (t h) -> p t h", t=TT), ACT.Exp).then_inc(g_step, 1)

        def gates_dve(dve, n):
            dve.wait_ge(g_step, 1)
            nc.vector.tensor_tensor(gt[:, 1, :, :], tail[:, :, H:2 * H], small[:, S_DTB:S_DTB + H].unsqueeze(1).broadcast_to([P, TT, H]), ALU.add).then_inc(g_step, 1)
            dve.wait_ge(g_step, 3)
            link(dve, dve_link, n, nc.vector.scalar_tensor_tensor(gt[:, 3, :, :], gt[:, 1, :, :], 0.0, gt[:, 2, :, :], ALU.max, ALU.add))
            for t in range(TT):
                ins = nc.vector.scalar_tensor_tensor(gt[:, 3, t, :], gt[:, 3, t, :], -1.0, gt[:, 4, 0, :], ALU.mult, ALU.mult)
            link(dve, dve_link, n, ins)
            ins = nc.vector.tensor_copy(dn[:, 0, :, :], gt[:, 3, :, :])
            ins.then_inc(l_step, 1)

        def gates_pe(pe):
            pe.wait_ge(l_step, 1)
            nc.tensor.matmul(pm[:, 0, 0:H], cst[:, C_GT, :], gt[:, 3, 0, :], start=True, stop=True)
            nc.tensor.matmul(pm[:, 0, H:2 * H], cst[:, C_LE, :], gt[:, 3, 1, :], start=True, stop=True).then_inc(g_pe, 1)

        def l2_act(act, n):
            act.wait_ge(l_step, 2)
            nc.scalar.activation(dn[:, 1, :, :], dn[:, 0, :, :], ACT.Sqrt).then_inc(l_step, 1)

        def l2_dve(dve, n):
            qk = proj2[:, :, B_Q:B_Q + 1024]
            dve.wait_ge(c_out, 16)
            link(dve, dve_link, n, nc.vector.tensor_tensor(dsq[:, :, :], qk, qk, ALU.mult))
            link(dve, dve_link, n, nc.vector.tensor_reduce(dn[:, 0, :, :], dsq[:, :, :].rearrange("p t (h n) -> p t h n", n=P), AX.X, ALU.add))
            nc.vector.tensor_scalar(dn[:, 0, :, :], dn[:, 0, :, :], EPS, None, ALU.add).then_inc(l_step, 1)
            dve.wait_ge(l_step, 3)
            link(dve, dve_link, n, nc.vector.reciprocal(dn[:, 2, :, :], dn[:, 1, :, :]))
            link(dve, dve_link, n, nc.vector.tensor_scalar(dn[:, 2, :, 0:4], dn[:, 2, :, 0:4], SCALE, None, ALU.mult))
            for t in range(TT):
                x_ = proj2[:, t, B_Q:B_Q + 1024].rearrange("p (h n) -> p h n", n=P)
                nc.vector.tensor_tensor(x_, x_, dn[:, 2, t, :].unsqueeze(2).broadcast_to([P, H, P]), ALU.mult).then_inc(l_step, 1)

        def delta_pool(pool):
            pool.wait_ge(l_step, 5)
            pool.wait_ge(g_step, 4)
            pool.wait_ge(c_out, 16)
            for m in range(4):
                c, hf = m // 2, m % 2
                if m >= 2:
                    pool.wait_ge(d_T, m - 1)
                for i in range(4):
                    h = 4 * hf + i
                    k_ = proj2[:, c, B_K + h // 2 * P:B_K + h // 2 * P + P]
                    nc.gpsimd.tensor_scalar(dgS[m % 2][:, i, :], cst[:, C_GT, :], gt[:, 3, c, h:h + 1], None, ALU.mult)
                    nc.gpsimd.tensor_scalar(dkb[m % 2][:, i, :], k_, gt[:, 0, c, h:h + 1], None, ALU.mult).then_inc(d_pool, 1)
            for c in range(2):
                for h in range(H):
                    v_ = proj2[:, c, B_V + h * P:B_V + (h + 1) * P]
                    k_ = proj2[:, c, B_K + h // 2 * P:B_K + h // 2 * P + P]
                    nc.gpsimd.tensor_scalar(v_, v_, gt[:, 0, c, h:h + 1], None, ALU.mult)
                    if c == 0:
                        ins = nc.gpsimd.tensor_scalar(dkd[:, h, :], k_, gt[:, 5, 0, h:h + 1], None, ALU.mult)
                    else:
                        nc.gpsimd.tensor_scalar(dX[:, h, :], k_, gt[:, 0, 1, h:h + 1], -1.0, ALU.mult, ALU.mult).then_inc(d_vb, 1)
                        pool.wait_ge(d_vb, h + 1)
                        ins = nc.gpsimd.tensor_scalar(dX[:, h, :], dX[:, h, :], gt[:, 5, 1, h:h + 1], None, ALU.mult)
            ins.then_inc(d_vb, 1)
            for i in range(4 * NL):
                lev, m = i // 4, i % 4
                pool.wait_ge(d_N, m + 1)
                if i >= 2:
                    pool.wait_ge(d_PP, i - 1)
                if 2 <= i < 6:
                    pool.wait_ge(d_TU, i - 1)
                nc.gpsimd.tensor_tensor(dB[i % 2][:, :, :], dN[:, 4 * m:4 * m + 4, :],
                                        cst[:, C_MASK + 1 + lev, :].unsqueeze(1).broadcast_to([P, 4, P]), ALU.mult).then_inc(d_B, 1)
            for h in range(H):
                q_ = proj2[:, 1, B_Q + h // 2 * P:B_Q + h // 2 * P + P]
                ins = nc.gpsimd.tensor_scalar(dqg[:, h, :], q_, gt[:, 5, 1, h:h + 1], None, ALU.mult)
            ins.then_inc(f_pool, 1)

        def delta_pe(pe):
            def operands(m):
                c, hf = m // 2, m % 2
                pe.wait_ge(d_pool, 4 * m + 4)
                if m >= 1:
                    pe.wait_ge(d_cp, m)
                    pe.wait_ge(d_E, m)
                for i, c0 in enumerate((B_K, B_K + P, B_Q, B_Q + P)):
                    c0 += 2 * hf * P
                    nc.tensor.transpose(pj[0][:, 0, i * P:(i + 1) * P], proj2[:, c, c0:c0 + P], ident)
                for i in range(4):
                    nc.tensor.transpose(pj[0][:, 1, i * P:(i + 1) * P], dkb[m % 2][:, i, :], ident)
                for i in range(4):
                    mm = nc.tensor.matmul(pj[1][:, 0, i * P:(i + 1) * P], dgS[m % 2][:, i, :], cst[:, C_LE, :], start=True, stop=True)
                mm.then_inc(d_T, 1)

            def scores(m):
                pe.wait_ge(d_cp, m + 1)
                if m >= 1:
                    pe.wait_ge(d_N, m)
                for i in range(4):
                    nc.tensor.matmul(pj[1][:, 1, i * P:(i + 1) * P], dkq[:, i // 2, :], dkbT[:, i, :], start=True, stop=True)
                for i in range(2):
                    mm = nc.tensor.matmul(pt[:, 0, i * P:(i + 1) * P], dkq[:, i, :], dkq[:, 2 + i, :], start=True, stop=True)
                mm.then_inc(d_S, 1)

            pe.wait_ge(l_step, 5)
            for i in range(5):
                if i < 4:
                    operands(i)
                if i >= 1:
                    scores(i - 1)

            def product(i):
                lev, m = i // 4, i % 4
                pe.wait_ge(d_B, i + 1)
                pe.wait_ge(d_cp, 4)
                if lev == 0:
                    if i >= 2:
                        pe.wait_ge(d_TU, i - 1)
                    for a in range(4):
                        mm = nc.tensor.transpose(pj[0][:, i % 2, a * P:(a + 1) * P], dB[i % 2][:, a, :], ident)
                else:
                    pe.wait_ge(d_TU, i - 3)
                    if i >= 6:
                        pe.wait_ge(d_Pc, i - 4 - 1)
                    for a in range(4):
                        mm = nc.tensor.matmul(pj[0][:, i % 2, a * P:(a + 1) * P], dB[i % 2][:, a, :], dT[:, 4 * m + a, :], start=True, stop=True)
                mm.then_inc(d_PP, 1)

            def deltas(i):
                lev, m = i // 4, i % 4
                if lev == 0:
                    return
                pe.wait_ge(d_Pc, i - 4 + 1)
                pe.wait_ge(d_N, 4)
                if i >= 6:
                    pe.wait_ge(d_TU, i - 1)
                p_ = dP[i % 2]
                if lev < NL - 1:
                    for a in range(4):
                        nc.tensor.matmul((pj[1], pt)[i % 2][:, 0, a * P:(a + 1) * P], dU[:, 4 * m + a, :], p_[:, a, :], start=True, stop=True)
                for a in range(4):
                    mm = nc.tensor.matmul((pj[1], pt)[i % 2][:, 1, a * P:(a + 1) * P], p_[:, a, :], dU[:, 4 * m + a, :], start=True, stop=True)
                mm.then_inc(d_dd, 1)

            for i in range(4 * NL + 1):
                if i < 4 * NL:
                    product(i)
                if i >= 1:
                    deltas(i - 1)

            def four(out, f):
                for a in range(4):
                    mm = f(out[:, a * P:(a + 1) * P], a)
                mm.then_inc(f_pe, 1)

            def mm1(o, l, r, start=True, stop=True):
                return nc.tensor.matmul(o, l, r, start=start, stop=stop, skip_group_check=True)

            V = lambda c, h: proj2[:, c, B_V + h * P:B_V + (h + 1) * P]
            pe.wait_ge(d_TU, 4 * NL)
            pe.wait_ge(d_vb, H + 1)
            for hf in range(2):
                four(pj[0][:, hf, :], lambda o, a: mm1(o, dU[:, 4 * hf + a, :], V(0, 4 * hf + a)))
            for hf in range(2):
                four(pj[1][:, hf, :], lambda o, a: mm1(o, dX[:, 4 * hf + a, :], dU[:, 8 + 4 * hf + a, :]))
            pe.wait_ge(f_pool, 1)
            for hf in range(2):
                four(pt[:, hf, :], lambda o, a: nc.tensor.transpose(o, dqg[:, 4 * hf + a, :], ident))
            for hf in range(2):
                pe.wait_ge(f_cp, hf + 1)
                four(pm[:, hf, :], lambda o, a: mm1(o, dkd[:, 4 * hf + a, :], dvn[hf][:, a, :]))
            for hf in range(2):
                four(pj[0][:, hf, :], lambda o, a: mm1(o, aqk(hf)[:, a * P:(a + 1) * P], dvn[hf][:, a, :]))
            pe.wait_ge(f_cp, 8)

            def v1(o, a):
                mm1(o, dU[:, 8 + 4 * hf + a, :], V(1, 4 * hf + a), stop=False)
                return mm1(o, dwT[:, 4 * hf + a, :], dS[:, 4 * hf + a, :], start=False)
            for hf in range(2):
                four(pj[1][:, hf, :], v1)

            def o1(o, a):
                mm1(o, dqgT[:, 4 * hf + a, :], dS[:, 4 * hf + a, :], stop=False)
                return mm1(o, aqk(2 + hf)[:, a * P:(a + 1) * P], dvn[2 + hf][:, a, :], start=False)
            for hf in range(2):
                pe.wait_ge(f_cp, 9 + hf)
                four(pt[:, hf, :], o1)

        def delta_act(act, n):
            for m in range(4):
                act.wait_ge(d_T, m + 1)
                if m >= 1:
                    act.wait_ge(d_S, m)
                if m >= 2:
                    act.wait_ge(d_Em, m - 1)
                nc.scalar.activation(dkq[:, :, :].rearrange("p a n -> p (a n)"), pj[0][:, 0, :], ACT.Copy)
                nc.scalar.activation(dkbT[:, :, :].rearrange("p a n -> p (a n)"), pj[0][:, 1, :], ACT.Copy).then_inc(d_cp, 1)
                nc.scalar.activation(dE[m % 2][:, :, :].rearrange("p a n -> p (a n)"), pj[1][:, 0, :], ACT.Exp).then_inc(d_E, 1)
            for i in range(4, 4 * NL):
                act.wait_ge(d_PP, i + 1)
                if i >= 6:
                    act.wait_ge(d_dd, i - 5)
                nc.scalar.activation(dP[i % 2][:, :, :].rearrange("p a n -> p (a n)"), pj[0][:, i % 2, :], ACT.Copy).then_inc(d_Pc, 1)
            outs = ([dvn[0], dvn[1], dwT[:, 0:4], dwT[:, 4:8], dqgT[:, 0:4], dqgT[:, 4:8], dS[:, 0:4], dS[:, 4:8]])
            banks = [b[:, i, :] for b in (pj[0], pj[1], pt, pm) for i in range(2)]
            for i, (o, b) in enumerate(zip(outs, banks)):
                act.wait_ge(f_pe, i + 1)
                nc.scalar.activation(o[:, :, :].rearrange("p a n -> p (a n)"), b, ACT.Copy).then_inc(f_cp, 1)
            for hf in range(2):
                act.wait_ge(f_pe, 11 + hf)
                nc.scalar.activation(dvn[2 + hf][:, :, :].rearrange("p a n -> p (a n)"), pj[1][:, hf, :], ACT.Copy).then_inc(f_cp, 1)

        def delta_dve(dve, n):
            for m in range(4):
                c = m // 2
                dve.wait_ge(d_E, m + 1)
                if m >= 1:
                    dve.wait_ge(d_N, m)
                nc.vector.tensor_tensor(dEm[:, :, :], dE[m % 2][:, :, :], cst[:, C_LE, :].unsqueeze(1).broadcast_to([P, 4, P]), ALU.mult).then_inc(d_Em, 1)
                dve.wait_ge(d_Em, m + 1)
                dve.wait_ge(d_S, m + 1)
                nc.vector.scalar_tensor_tensor(dN[:, 4 * m:4 * m + 4, :].rearrange("p a n -> p (a n)"), pj[1][:, 1, :], -1.0,
                                               dEm[:, :, :].rearrange("p a n -> p (a n)"), ALU.mult, ALU.mult)
                nc.vector.tensor_tensor(aqk(m).rearrange("p (a b n) -> p a b n", a=2, b=2),
                                        pt[:, 0, 0:256].rearrange("p (a n) -> p a n", a=2).unsqueeze(2).broadcast_to([P, 2, 2, P]),
                                        dEm[:, :, :].rearrange("p (a b) n -> p a b n", a=2), ALU.mult).then_inc(d_N, 1)
            eye = cst[:, C_ID, :].unsqueeze(1).broadcast_to([P, 4, P])
            for i in range(4 * NL):
                lev, m = i // 4, i % 4
                T_, U_ = dT[:, 4 * m:4 * m + 4, :], dU[:, 4 * m:4 * m + 4, :]
                if lev == 0:
                    dve.wait_ge(d_B, i + 1)
                    nc.vector.tensor_tensor(U_, dB[i % 2][:, :, :], eye, ALU.add)
                    dve.wait_ge(d_PP, i + 1)
                    nc.vector.tensor_tensor(T_, pj[0][:, i % 2, :].rearrange("p (a n) -> p a n", a=4), eye, ALU.add).then_inc(d_TU, 1)
                else:
                    dve.wait_ge(d_dd, i - 4 + 1)
                    bank = (pj[1], pt)[i % 2]
                    if lev < NL - 1:
                        nc.vector.tensor_tensor(T_, T_, bank[:, 0, :].rearrange("p (a n) -> p a n", a=4), ALU.add)
                    nc.vector.tensor_tensor(U_, U_, bank[:, 1, :].rearrange("p (a n) -> p a n", a=4), ALU.add).then_inc(d_TU, 1)
            for i in range(4):
                c, hf = i // 2, i % 2
                dve.wait_ge(f_pe, (9, 10, 13, 14)[i])
                o = proj2[:, c, A_F + hf * 512:A_F + hf * 512 + 512]
                nc.vector.tensor_copy(o, (pj[0], pt)[c][:, hf, :]).then_inc(f_dve, 1)


        def mix_act(act, n):
            nc.scalar.activation(proj2[:, :, A_G:A_G + H * P], proj2[:, :, A_G:A_G + H * P], ACT.Silu)
            nc.scalar.activation(proj2[:, :, B_Z:B_Z + H * P], proj2[:, :, B_Z:B_Z + H * P], ACT.Silu).then_inc(m_step, 1)
            act.wait_ge(m_step, 3)
            nc.scalar.activation(mrs[:, :, :], mss[:, :, :], ACT.Sqrt).then_inc(m_step, 1)

        def mix_dve(dve, n):
            dve.wait_ge(f_dve, 4)
            o = proj2[:, :, A_F:A_F + H * P]
            link(dve, dve_link, n, nc.vector.tensor_tensor(dsq[:, :, :], o, o, ALU.mult))
            dve.wait_ge(m_step, 1)
            nc.vector.tensor_reduce(mss[:, :, H:2 * H], dsq[:, :, :].rearrange("p t (h n) -> p t h n", n=P), AX.X, ALU.add).then_inc(m_step, 1)
            dve.wait_ge(m_step, 2)
            nc.vector.tensor_scalar(mss[:, :, :], mss[:, :, :], 1.0 / HD, EPS, ALU.mult, ALU.add).then_inc(m_step, 1)
            dve.wait_ge(m_step, 4)
            link(dve, dve_link, n, nc.vector.reciprocal(mss[:, :, :], mrs[:, :, :]))
            for t in range(TT):
                o = proj2[:, t, 0:D].rearrange("p (h n) -> p h n", n=P)
                link(dve, dve_link, n, nc.vector.tensor_tensor(o, o, mss[:, t, :].unsqueeze(2).broadcast_to([P, 2 * H, P]), ALU.mult))
            for c0, g0 in ((0, A_G), (H * P, B_Z)):
                nc.vector.tensor_tensor(proj2[:, :, c0:c0 + H * P], proj2[:, :, c0:c0 + H * P], proj2[:, :, g0:g0 + H * P], ALU.mult).then_inc(m_step, 1)

        HS = 2 * H
        y = region(at_y + 4 * TT * NB)
        qn = y("qn", [P, TT, D])
        qT = y("qT", [P, HS, TT * P])
        sc = y("sc", [P, TT, HS, NK])
        keys = y("keys", [P, HS, NK])
        vals = y("vals", [P, TT, HS, TOPK])
        idx = y("idx", [P, TT, HS, TOPK], U32)
        at_q = at_y + 4 * TT * NB
        y = region(at_q)
        cand = y("cand", [P, TT, H, TOPK * TOPK])
        y = region(at_q)
        slotT = y("slotT", [P, 3, TT * P])
        hotA = [y(f"hotA{i}", [P, 4, NK]) for i in range(2)]
        hotB = [y(f"hotB{i}", [P, 4, NK]) for i in range(2)]
        slot_c = y("slot_c", [P, 64])
        y = region(at_q + 4 * TT * D)
        idxf = y("idxf", [P, TT, HS, TOPK])
        pq = y("pq", [P, 2, TT * H * TOPK], U32)
        pqf = y("pqf", [P, 2, TT, H * TOPK])
        res = y("res", [P, 3, TT, H * TOPK])
        best = y("best", [P, TT, H, TOPK])
        pos = y("pos", [P, TT, H, TOPK], U32)
        gsum = y("gsum", [P, 2, TT * H])
        stage = [region(at_q + 4 * TT * D * (1 + i))(f"stage{i}", [P, NK, 32]) for i in range(2)]
        oh = region(at_q + 3 * 4 * TT * D)("oh", [P, H * TOPK, TOPK])
        r_keys, r_T, r_c, r_S, r_sc = sem("keys_loaded"), sem("query_transposed"), sem("query_copied"), sem("key_scores"), sem("key_scores_copied")
        tk, r_exp, r_sel, r_slotT, r_slot = sem("top_steps"), sem("gate_exp"), sem("select_steps"), sem("slots_transposed"), sem("slots_copied")
        r_A, r_B, r_G, r_gc = sem("first_onehots"), sem("second_onehots"), sem("gate_products"), sem("gates_copied")
        r_c64 = sem("slots_fixed")
        pool_step = sem("pool_passed_a_wait")
        g_wr = [sem("gates_written0"), sem("gates_written1")]
        GROUPS = TT * P // 4

        def router_pe(pe):
            def forward(b):
                if b >= 2:
                    pe.wait_ge(r_c, b - 1)
                for i in range(4):
                    for t in range(TT):
                        at = (i % 2) * 256 + t * P
                        tr = nc.tensor.transpose(pj[b % 2][:, i // 2, at:at + P], qn[:, t, (4 * b + i) * P:(4 * b + i + 1) * P], ident)
                tr.then_inc(r_T, 1)

            def scores(b):
                pe.wait_ge(r_c, b + 1)
                if b >= 2:
                    pe.wait_ge(r_sc, b - 1)
                for t in range(TT):
                    for i in range(4):
                        mm = nc.tensor.matmul((pt, pm)[b % 2][:, t, i * P:(i + 1) * P], qT[:, 4 * b + i, t * P:(t + 1) * P],
                                              keys[:, 4 * b + i, :], start=True, stop=True)
                mm.then_inc(r_S, 1)

            pe.wait_ge(wq_evac, 4)
            pe.wait_ge(r_keys, 16)
            for b in range(5):
                if b < 4:
                    forward(b)
                if b >= 1:
                    scores(b - 1)

        def router_act(act):
            for b in range(5):
                if b < 4:
                    act.wait_ge(r_T, b + 1)
                    nc.scalar.activation(qT[:, 4 * b:4 * b + 4, :].rearrange("p a n -> p (a n)"), pj[b % 2][:, :, :].rearrange("p a n -> p (a n)"), ACT.Copy).then_inc(r_c, 1)
                if b >= 1:
                    act.wait_ge(r_S, b)
                    nc.scalar.activation(sc[:, :, 4 * b - 4:4 * b, :], (pt, pm)[(b - 1) % 2][:, :, :].rearrange("p t (a n) -> p t a n", n=NK), ACT.Copy).then_inc(r_sc, 1)

        def top16(dve, base, n, src, val, ind):
            for k in range(5):
                for i in range(n):
                    if k:
                        dve.wait_ge(tk, base + (k - 1) * n + i + 1)
                    v, x_ = val(i), ind(i)
                    half = slice(0, 8) if k < 3 else slice(8, 16)
                    if k in (0, 3):
                        ins = nc.vector.max(v[:, half], src(i))
                    elif k in (1, 4):
                        ins = nc.vector.max_index(x_[:, half], v[:, half], src(i))
                    else:
                        ins = nc.vector.match_replace(src(i), v[:, 0:8], src(i), -3.0e38)
                    ins.then_inc(tk, 1)
            return base + 5 * n

        def router_dve(dve, n):
            dve.wait_ge(r_sc, 4)
            k = top16(dve, 0, TT * HS, lambda i: sc[:, i // HS, i % HS, :], lambda i: vals[:, i // HS, i % HS, :],
                      lambda i: idx[:, i // HS, i % HS, :])
            dve.wait_ge(tk, k)
            v4 = vals[:, :, :, :].rearrange("p t (h s) k -> p t h s k", s=2)
            for t in range(TT):
                nc.vector.tensor_tensor(cand[:, t, :, :].rearrange("p h (a b) -> p h a b", a=TOPK),
                                        v4[:, t, :, 0, :].unsqueeze(3).broadcast_to([P, H, TOPK, TOPK]),
                                        v4[:, t, :, 1, :].unsqueeze(2).broadcast_to([P, H, TOPK, TOPK]), ALU.add).then_inc(tk, 1)
            dve.wait_ge(tk, k + 2)
            k = top16(dve, k + 2, TT * H, lambda i: cand[:, i // H, i % H, :], lambda i: best[:, i // H, i % H, :],
                      lambda i: pos[:, i // H, i % H, :])
            dve.wait_ge(tk, k)
            gate_ = res[:, 0, :, :].rearrange("p t (h j) -> p (t h) j", j=TOPK)
            b_ = best[:, :, :, :].rearrange("p t h j -> p (t h) j")
            nc.vector.tensor_tensor(gate_, b_, b_[:, :, 0:1].broadcast_to([P, TT * H, TOPK]), ALU.subtract).then_inc(r_exp, 1)
            pos_ = pos[:, :, :, :].rearrange("p t h j -> p (t h j)")
            nc.vector.tensor_scalar(pq[:, 0, :], pos_, 4, None, ALU.logical_shift_right)
            nc.vector.tensor_copy(idxf[:, :, :, :], idx[:, :, :, :])
            link(dve, dve_link, n, nc.vector.tensor_scalar(pq[:, 1, :], pos_, 15, None, ALU.bitwise_and))
            link(dve, dve_link, n, nc.vector.tensor_copy(pqf[:, :, :, :].rearrange("p s t j -> p (s t j)"), pq[:, :, :].rearrange("p s j -> p (s j)")))
            dve.wait_ge(r_exp, 2)
            link(dve, dve_link, n, nc.vector.tensor_reduce(gsum[:, 0, :], gate_, AX.X, ALU.add))
            link(dve, dve_link, n, nc.vector.reciprocal(gsum[:, 1, :], gsum[:, 0, :]))
            nc.vector.tensor_tensor(gate_, gate_, gsum[:, 1, :].unsqueeze(2).broadcast_to([P, TT * H, TOPK]), ALU.mult)
            for s_ in range(2):
                for t in range(TT):
                    link(dve, dve_link, n, nc.vector.tensor_tensor(
                        oh[:, :, :], pqf[:, s_, t, :].unsqueeze(2).broadcast_to([P, H * TOPK, TOPK]),
                        cst[:, C_IOTA, 0:TOPK].unsqueeze(1).broadcast_to([P, H * TOPK, TOPK]), ALU.is_equal))
                    o4 = oh[:, :, :].rearrange("p (h j) a -> p h j a", h=H)
                    i4 = idxf[:, t, :, :].rearrange("p (h s) k -> p h s k", s=2)[:, :, s_, :]
                    link(dve, dve_link, n, nc.vector.tensor_tensor(o4, o4, i4.unsqueeze(2).broadcast_to([P, H, TOPK, TOPK]), ALU.mult))
                    link(dve, dve_link, n, nc.vector.tensor_reduce(res[:, 1 + s_, t, :], oh[:, :, :], AX.X, ALU.add))
            ins = nc.vector.tensor_copy(gsum[:, 0, 0:1], gsum[:, 1, 0:1])
            ins.then_inc(r_sel, 1)
            dve.wait_ge(r_slot, 2)

            def body(i):
                for g in range(16):
                    if not (isinstance(i, int) and i == 0 and g < 2):
                        dve.wait_ge(r_G, i * 16 + g - 1)
                    for a in range(4):
                        tok = i * 64 + (4 * g + a)
                        ins = nc.vector.tensor_scalar(hotA[g % 2][:, a, :], cst[:, C_IOTA, :], slotT[:, 1, bass.ds(tok, 1)],
                                                      slotT[:, 0, bass.ds(tok, 1)], ALU.is_equal, ALU.mult)
                    ins.then_inc(r_A, 1)
            turns(dve, GROUPS // 16, body)

        def gates_build_pool(pool):
            pool.wait_ge(r_slot, 2)

            def body(i):
                if not (isinstance(i, int) and i == 0):
                    pool.wait_ge(r_B, i * 16)
                nc.gpsimd.tensor_copy(slot_c[:, :], slotT[:, 2, bass.ds(i * 64, 64)]).then_inc(r_c64, 1)
                pool.wait_ge(r_c64, i + 1)
                pool.sem_inc(pool_step, 1)
                for g in range(16):
                    if not (isinstance(i, int) and i == 0 and g < 2):
                        pool.wait_ge(r_G, i * 16 + g - 1)
                        pool.sem_inc(pool_step, 1)
                    for a in range(4):
                        ins = nc.gpsimd.tensor_scalar(hotB[g % 2][:, a, :], cst[:, C_IOTA, :], slot_c[:, 4 * g + a:4 * g + a + 1], None, ALU.is_equal)
                    ins.then_inc(r_B, 1)
            turns(pool, GROUPS // 16, body)

        def gates_build_pe(pe):
            pe.wait_ge(r_sel, 1)
            pe.wait_ge(r_sc, 4)
            for q_ in range(3):
                for t in range(TT):
                    tr = nc.tensor.transpose(pm[:, q_ // 2, (q_ % 2) * 256 + t * P:(q_ % 2) * 256 + t * P + P], res[:, q_, t, :], ident)
            tr.then_inc(r_slotT, 1)

            def body(i):
                for g in range(16):
                    first = isinstance(i, int) and i == 0
                    if first and g < 2:
                        pe.wait_ge(r_slot, 2)
                    else:
                        pe.wait_ge(r_gc, i * 16 + g - 1)
                    pe.wait_ge(r_A, i * 16 + g + 1)
                    pe.wait_ge(r_B, i * 16 + g + 1)
                    for a in range(4):
                        mm = nc.tensor.matmul(pm[:, g % 2, a * P:(a + 1) * P], hotA[g % 2][:, a, :], hotB[g % 2][:, a, :], start=True, stop=True)
                    mm.then_inc(r_G, 1)
            turns(pe, GROUPS // 16, body)

        def load_gates(act, s, par):
            act.dma_start(gate_e[par][:, :, :, :], gates_d[:, bass.ds(s, 1), :, :, :].rearrange("p a o b t -> p (a o) b t")).then_inc(gates_loaded[par], 16)

        def gates_build_act(act):
            act.wait_ge(r_exp, 1)
            nc.scalar.activation(res[:, 0, :, :], res[:, 0, :, :], ACT.Exp).then_inc(r_exp, 1)
            act.wait_ge(r_slotT, 1)
            nc.scalar.activation(slotT[:, 0:2, :].rearrange("p a n -> p (a n)"), pm[:, 0, :], ACT.Copy).then_inc(r_slot, 1)
            nc.scalar.activation(slotT[:, 2, :], pm[:, 1, 0:256], ACT.Copy).then_inc(r_slot, 1)

            def body(i):
                for g in range(16):
                    half, k = g // 8, g % 8
                    if k == 0 and not (isinstance(i, int) and i == 0):
                        act.wait_ge(g_wr[half], i * 16)
                    act.wait_ge(r_G, i * 16 + g + 1)
                    nc.scalar.activation(stage[half][:, :, 4 * k:4 * k + 4].rearrange("p b t -> p t b"),
                                         pm[:, g % 2, :].rearrange("p (t b) -> p t b", t=4), ACT.Copy).then_inc(r_gc, 1)
                    if k == 7:
                        act.wait_ge(r_gc, i * 16 + g + 1)
                        act.dma_start(gates_d[:, :, bass.ds(i * 2 + half, 1), :, :].rearrange("p s o b t -> p s (o b t)"),
                                      stage[half][:, :, :].rearrange("p (s b) t -> p s (b t)", b=4)).then_inc(g_wr[half], 16)
            turns(act, GROUPS // 16, body)
            for half in range(2):
                act.wait_ge(g_wr[half], 16 * (GROUPS // 16))
            load_gates(act, 0, 0)

        s_out = sem("out_written")
        gfin_in = sem("gfin_loaded")
        gates_loaded = [sem("gates_loaded0"), sem("gates_loaded1")]
        block = ctx.enter_context(nc.Block())

        @block.sync
        def _(sp):
            def stream(w, q0, quads, start=0):
                def body(i):
                    for j in range(SLOTS):
                        src = w[bass.ds(i * SLOTS + j, 1), :, :].rearrange("a p n -> p (a n)")
                        if not (isinstance(i, int) and q0 + i == 0):
                            sp.wait_ge(lo_ready, (i + q0) * SLOTS + j - 3)
                        sp.dma_start(raw[:, j, :], src).then_inc(raw_ready[j], 16)
                turns(sp, quads, body, start)

            sp.dma_start(cst[:, :, :], cst_d).then_inc(s_const, 16)
            sp.dma_start(small[:, :], small_d).then_inc(s_const, 16)
            sp.dma_start(resid[:, :, :], x_d.rearrange("(t p) d -> p t d", p=P)).then_inc(s_x, 16)
            sp.dma_start(wtail[:, :, 0:8], wf_d).then_inc(wt_loaded, 16)
            sp.dma_start(att[:, :, :], att_d).then_inc(s_att, 16)
            sp.dma_start(gfin[:, :], gfin1_d.broadcast_to([P, D])).then_inc(gfin_in, 16)
            stream(w_in_d, Q_IN1, G1)
            stream(w_out_d, Q_OUT1, 4)
            sp.wait_ge(wt_l, 1)
            sp.dma_start(wtail[:, :, :], wba_d).then_inc(wt_loaded, 16)
            stream(w_mlp_d, Q_MLP, 2 * MLP_SB)
            stream(w_in2_d, Q_IN2, G2)
            sp.wait_ge(nm_out, 6)
            sp.dma_start(lbl[:, :, :], lbl_d.broadcast_to([P, 2, H * P])).then_inc(lbl_in, 16)
            stream(w_out2_d, Q_OUT2, 4)
            sp.wait_ge(tp_l, 20)
            sp.dma_start(keys[:, :, :], keys_d).then_inc(r_keys, 16)
            stream(wq_d, Q_WQ, 4)
            stream(w_peer_d, Q_PEER, 2 * PEER_SB)
            sp.wait_ge(ffn_sems["peer"]["coef"], 1)
            sp.dma_start(gfin[:, :], gfin2_d.broadcast_to([P, D])).then_inc(gfin_in, 16)
            for t in range(TT):
                sp.wait_ge(nm_out, 11 + t)
                sp.dma_start(out_d[t * P:(t + 1) * P, :], nat[:, t, :]).then_inc(s_out, 16)
            sp.wait_ge(s_out, 32)

        @block.scalar
        def _(act):
            n = [0]
            act.wait_ge(s_const, 32)
            act.wait_ge(s_x, 16)
            norm_act(act, 0)
            for j in range(AHEAD):
                make_hi(act, 0, j, first=True)
            tail_act(act, 0, 8)
            station_act(act, 0, lambda k: S_GATTN + k)
            wide_act(act, Q_IN1, G1, in1_evac, proj1)
            att1_act(act, n)
            station_act(act, 1, lambda k: S_GOUT1 + k)
            wide_act(act, Q_OUT1, 4, None, None)
            act.wait_ge(out1_evac, 4)
            norm_act(act, 1)
            station_act(act, 2, lambda k: S_GMLP + k)
            ffn_act(act, Q_MLP, MLP_SB, ffn_sems["mlp"], ACT.Relu, True, Q_END)
            act.wait_ge(ffn_sems["mlp"]["dn_evac"], 4 * MLP_SB)
            norm_act(act, 2)
            act.wait_ge(nm_out, 6)
            norm_act(act, 3)
            tail_act(act, 1, 16)
            station_act(act, 3, lambda k: S_GATTN2 + k)
            wide_act(act, Q_IN2, G2, in2_evac, proj2)
            hgrn_act(act, n)
            gates_act(act, n)
            conv_act(act, n)
            l2_act(act, n)
            delta_act(act, n)
            mix_act(act, n)
            station_act(act, 4, lambda k: S_GHGRN if k < H else S_GGDN)
            wide_act(act, Q_OUT2, 4, None, None)
            act.wait_ge(out2_evac, 4)
            norm_act(act, 4)
            station_act(act, 5, lambda k: S_GFFN + k)
            wide_act(act, Q_WQ, 4, wq_evac, qn)
            router_act(act)
            ffn_act(act, Q_PEER, PEER_SB, ffn_sems["peer"], ACT.Gelu, False, Q_END, lambda: gates_build_act(act))
            act.wait_ge(ffn_sems["peer"]["dn_evac"], 4 * PEER_SB)
            norm_act(act, 5)

        @block.vector
        def _(dve):
            n = [0]
            dve.wait_ge(s_const, 32)
            norm_dve(dve, 0, nat)
            for j in range(AHEAD):
                make_lo(dve, 0, j)
            tail_dve(dve, 0, 8)
            station_dve(dve, 0, lambda k: S_GATTN + k)
            wide_dve(dve, Q_IN1, G1, None, False)
            att1_dve(dve, n)
            station_dve(dve, 1, lambda k: S_GOUT1 + k)
            wide_dve(dve, Q_OUT1, 4, out1_evac, True)
            norm_dve(dve, 1, nat)
            station_dve(dve, 2, lambda k: S_GMLP + k)
            ffn_dve(dve, Q_MLP, MLP_SB, ffn_sems["mlp"], None, Q_END)
            dve.wait_ge(gfin_in, 16)
            norm_dve(dve, 2, resid, gfin[:, :])
            norm_dve(dve, 3, nat)
            tail_dve(dve, 1, 16)
            station_dve(dve, 3, lambda k: S_GATTN2 + k)
            wide_dve(dve, Q_IN2, G2, None, False)
            dve.wait_ge(wt_pe, 2)
            nc.vector.tensor_copy(tail[:, :, :], pm[:, :, 0:16]).then_inc(wt_out, 1)
            hgrn_dve(dve, n)
            gates_dve(dve, n)
            conv_dve(dve, n)
            l2_dve(dve, n)
            delta_dve(dve, n)
            mix_dve(dve, n)
            station_dve(dve, 4, lambda k: S_GHGRN if k < H else S_GGDN)
            wide_dve(dve, Q_OUT2, 4, out2_evac, True)
            norm_dve(dve, 4, nat)
            station_dve(dve, 5, lambda k: S_GFFN + k)
            wide_dve(dve, Q_WQ, 4, None, False)
            ffn_dve(dve, Q_PEER, PEER_SB, ffn_sems["peer"], gates_loaded, Q_END, lambda: router_dve(dve, n))
            dve.wait_ge(gfin_in, 32)
            norm_dve(dve, 5, nat, gfin[:, :])

        @block.gpsimd
        def _(pool):
            att1_pool(pool)
            hgrn_pool(pool)
            delta_pool(pool)
            gates_build_pool(pool)

        @block.tensor
        def _(pe):
            pe.wait_ge(s_const, 32)
            pe.wait_ge(nm_out, 2)
            station_pe(pe, 0, nat)
            pe.wait_ge(tp_l, 4)
            tail_pe(pe, 0, 8)
            wide_pe(pe, Q_IN1, G1, in1_evac)
            att1_pe(pe)
            pe.wait_ge(hn_out, 2)
            station_pe(pe, 1, proj1)
            pe.wait_ge(tp_l, 8)
            wide_pe(pe, Q_OUT1, 4, out1_evac)
            pe.wait_ge(nm_out, 4)
            station_pe(pe, 2, nat)
            pe.wait_ge(tp_l, 12)
            ffn_pe(pe, Q_MLP, MLP_SB, ffn_sems["mlp"])
            pe.wait_ge(nm_out, 8)
            station_pe(pe, 3, nat)
            pe.wait_ge(tp_l, 16)
            tail_pe(pe, 1, 16)
            wide_pe(pe, Q_IN2, G2, in2_evac)
            pe.wait_ge(in2_evac, G2)
            pe.wait_ge(wt_out, 2)
            hgrn_pe(pe)
            gates_pe(pe)
            conv_pe(pe)
            delta_pe(pe)
            pe.wait_ge(m_step, 6)
            station_pe(pe, 4, proj2)
            pe.wait_ge(tp_l, 20)
            wide_pe(pe, Q_OUT2, 4, out2_evac)
            pe.wait_ge(nm_out, 10)
            station_pe(pe, 5, nat)
            pe.wait_ge(tp_l, 24)
            wide_pe(pe, Q_WQ, 4, wq_evac)
            router_pe(pe)
            ffn_pe(pe, Q_PEER, PEER_SB, ffn_sems["peer"], lambda: gates_build_pe(pe))


def up_chunks(w):
    g = w.shape[1] // NB
    return np.ascontiguousarray(w.reshape(4, 4, P, g, NB).transpose(3, 0, 2, 1, 4)).reshape(4 * g, P, CH)


def down_chunks(w):
    s = w.shape[0] // NB
    return np.ascontiguousarray(w.reshape(s, 4, P, 4, NB).transpose(0, 3, 2, 1, 4)).reshape(4 * s, P, CH)


def ffn_chunks(up, down):
    n = up.shape[0] // 4
    up, down = up.reshape(n, 4, P, CH), down.reshape(n, 4, P, CH)
    out = np.empty((2 * n, 4, P, CH), np.float32)
    out[0], out[-1] = up[0], down[-1]
    out[1:-1:2], out[2:-1:2] = up[1:], down[:-1]
    return out.reshape(8 * n, P, CH)


def lay_out(x, g_attn, w_in, b_f, g_out_sb, g_out_fox, w_out, g_mlp, w_up, w_down, g_final,
            attn_norm_g_2, w_in_2, hgrn_lb_logits_2, hgrn_norm_g_2, gdn_conv_w_2, gdn_A_log_2,
            gdn_dt_bias_2, gdn_norm_g_2, w_out_2, ffn_norm_g_2, peer_w_query_2, peer_sub_keys_2,
            peer_u_2, peer_v_2, final_norm_g_2):
    f = lambda a: np.asarray(a, np.float32)
    cst, att = constants()
    col = lambda g: f(g).reshape(-1, P).T
    row = lambda g: np.broadcast_to(f(g).reshape(1, -1), (P, f(g).size))
    conv = f(gdn_conv_w_2)[0].reshape(4, 16, P).transpose(2, 1, 0).reshape(P, 64)
    small = np.concatenate([
        col(g_attn), col(g_out_sb), col(g_out_fox), col(g_mlp), col(attn_norm_g_2), col(hgrn_norm_g_2),
        col(gdn_norm_g_2), col(ffn_norm_g_2), row(b_f), row(gdn_A_log_2), row(gdn_dt_bias_2), conv], axis=1)
    w_in, w_in_2 = f(w_in)[0], f(w_in_2)[0]
    narrow = lambda w: np.ascontiguousarray(w.reshape(KT, P, -1).transpose(1, 0, 2))
    u = f(peer_u_2)[0].reshape(NK, PEER_SB, 4, 4, 4, P).transpose(1, 3, 5, 4, 2, 0)
    v = f(peer_v_2)[0].reshape(NK, PEER_SB, 4, 4, NB).transpose(1, 3, 0, 2, 4)
    keys = f(peer_sub_keys_2)[0].transpose(3, 1, 0, 2)
    return {
        "x": f(x)[0], "cst": cst, "att": att, "small": np.ascontiguousarray(small),
        "gfin1": f(g_final).reshape(1, D), "gfin2": f(final_norm_g_2).reshape(1, D),
        "lbl": f(hgrn_lb_logits_2).reshape(1, 2, H * P),
        "wf": narrow(w_in[:, W1:]), "wba": narrow(w_in_2[:, W2:]),
        "keys": np.ascontiguousarray(keys).reshape(P, 16, P),
        "w_in": up_chunks(w_in[:, :W1]), "w_out": up_chunks(f(w_out)[0]),
        "w_mlp": ffn_chunks(up_chunks(f(w_up)[0]), down_chunks(f(w_down)[0])),
        "w_in2": up_chunks(w_in_2[:, :W2]), "w_out2": up_chunks(f(w_out_2)[0]),
        "w_q": up_chunks(f(peer_w_query_2)[0].reshape(D, D)),
        "w_peer": ffn_chunks(np.ascontiguousarray(u).reshape(4 * PEER_SB, P, CH),
                             np.ascontiguousarray(v).reshape(4 * PEER_SB, P, CH)),
    }


def kernel(**inputs):
    import concourse.bacc as bacc
    from concourse.bass_utils import run_bass_kernel_spmd

    nc = bacc.Bacc("TRN2", target_bir_lowering=False, num_devices=1, dynamic_dma_scratch_size=1024)
    arrays = lay_out(**inputs)
    args = [nc.dram_tensor(name, a.shape, F32, kind="ExternalInput").ap() for name, a in arrays.items()]
    out = nc.dram_tensor("out", (TT * P, D), F32, kind="ExternalOutput").ap()
    two_blocks(nc, *args, out)
    r = run_bass_kernel_spmd(nc, [arrays], core_ids=[0])
    return r.results[0]["out"].reshape(1, TT * P, D)
```

```python
import numpy as np
from contextlib import ExitStack
import concourse.bass as bass
from concourse import mybir

F32 = mybir.dt.float32
F32R = mybir.dt.float32r
U32 = mybir.dt.uint32
ALU = mybir.AluOpType
ACT = mybir.ActivationFunctionType
AX = mybir.AxisListType

P = 128
TT = 2
D = 2048
KT = D // P
NB = 512
CH = 2048
SLOTS = 4
AHEAD = 3
H = 8
HD = 128
EPS = 1e-6
SCALE = HD ** -0.5
NEG = -30000.0

W1 = 6 * H * HD
W2 = 7168
G1, G2 = W1 // NB, W2 // NB
MLP_SB = 8192 // NB
PEER_SB = 16384 // NB
NK = 128
TOPK = 16

Q_IN1 = 0
Q_OUT1 = Q_IN1 + G1
Q_MLP = Q_OUT1 + 4
Q_IN2 = Q_MLP + 2 * MLP_SB
Q_OUT2 = Q_IN2 + G2
Q_WQ = Q_OUT2 + 4
Q_PEER = Q_WQ + 4
Q_END = Q_PEER + 2 * PEER_SB

C_ID, C_ONES, C_GT, C_LEV, C_LE, C_MASK, C_IOTA = 0, 1, 2, 3, 10, 11, 19
N_CONST = 20
A_NGE, A_NONES, A_SBM, A_SBA, A_FXA = 0, 1, 2, 5, 8
N_ATT = 11
S_GATTN, S_GOUT1, S_GMLP, S_GATTN2, S_GHGRN, S_GGDN, S_GFFN, S_BF, S_ALOG, S_DTB, S_CONV = 0, 16, 32, 48, 64, 65, 66, 82, 90, 98, 106
N_SMALL = 106 + 64


def constants():
    p, f = np.arange(P)[:, None], np.arange(P)[None, :]
    c = np.zeros((P, N_CONST, P), np.float32)
    c[:, C_ID] = p == f
    c[:, C_ONES] = 1
    c[:, C_GT] = p > f
    c[:, C_LE] = p <= f
    c[:, C_MASK] = p == f
    for lev in range(7):
        m = 1 << lev
        mid = f // (2 * m) * (2 * m) + m
        upper = (f // m) % 2 == 1
        c[:, C_LEV + lev] = np.where(upper, (p >= mid) & (p <= f), (p > f) & (p < mid))
        c[:, C_MASK + 1 + lev] = (p // (2 * m) == f // (2 * m)) & ((p // m) % 2 == 0) & upper
    c[:, C_IOTA] = f
    a = np.zeros((P, N_ATT, P), np.float32)
    a[:, A_NGE] = -1.0 * (p >= f)
    a[:, A_NONES] = -1
    a[:, A_SBM], a[:, A_SBM + 1], a[:, A_SBM + 2] = p < f, 1, p < f
    a[:, A_SBA] = a[:, A_SBA + 2] = np.where(p < f, 0.0, NEG)
    a[:, A_FXA] = a[:, A_FXA + 2] = np.where(f <= p, 0.0, -1e30)
    return c, a


def two_blocks(nc, x_d, cst_d, att_d, small_d, gfin1_d, gfin2_d, lbl_d, wf_d, wba_d, keys_d,
               w_in_d, w_out_d, w_mlp_d, w_in2_d, w_out2_d, wq_d, w_peer_d, out_d):
    ctx = ExitStack()
    gates_d = nc.dram_tensor("gates_scratch", (P, PEER_SB, 8, 4, 32), F32, kind="Internal").ap()
    with ctx:
        def sem(name):
            return ctx.enter_context(nc.semaphore(name))

        cursor = [(nc.sbuf_base + 31) // 32 * 32]

        def sb(name, shape, dt=F32, at=None):
            size = 4 * int(np.prod(shape[1:]))
            t = nc.alloc_sbuf_tensor_at(name, shape, dt, offset=cursor[0] if at is None else at)
            if at is None:
                cursor[0] += (size + 31) // 32 * 32
            return t

        raw = sb("raw", [P, SLOTS, CH])
        hi = sb("hi", [P, SLOTS, CH], F32R)
        lo = sb("lo", [P, SLOTS, CH], F32R)
        resid = sb("resid", [P, TT, D])
        cst = sb("cst", [P, N_CONST, P])
        small = sb("small", [P, N_SMALL])
        stat = sb("stat", [P, 8])
        at_tail = cursor[0]
        wtail = sb("wtail", [P, KT, 16])
        wtail_h = sb("wtail_h", [P, KT, 16], F32R)
        wtail_l = sb("wtail_l", [P, KT, 16], F32R)
        tail = sb("tail", [P, TT, 16])
        at_x = cursor[0]
        xh = sb("xh", [P, KT, TT * P], F32R)
        xl = sb("xl", [P, KT, TT * P], F32R)
        at_y = cursor[0]

        def region(at):
            c = [at]

            def place(name, shape, dt=F32):
                t = sb(name, shape, dt, at=c[0])
                c[0] += (4 * int(np.prod(shape[1:])) + 31) // 32 * 32
                assert c[0] <= nc.sbuf_usable_end, (name, c[0], nc.sbuf_usable_end)
                return t
            return place

        y = region(at_y)
        nat = y("nat", [P, TT, D])
        y = region(at_y)
        proj1 = y("proj1", [P, TT, W1])
        att = y("att", [P, N_ATT, P])
        gfin = y("gfin", [P, D])
        y = region(at_y)
        proj2 = y("proj2", [P, TT, W2])
        y = region(at_y)
        hid = y("hid", [P, TT, NB])
        coef = y("coef", [P, 4, TT * P])
        coef_h = [y(f"coef_h{i}", [P, 4, TT * P], F32R) for i in range(2)]
        coef_l = [y(f"coef_l{i}", [P, 4, TT * P], F32R) for i in range(2)]
        gate_e = [y(f"gate_e{i}", [P, 8, 4, 32]) for i in range(2)]
        at_gate = at_y + 4 * 2 * 1024 * 4

        s = region(at_x)

        qkT = [s(f"qkT{i}", [P, 2, TT * P]) for i in range(2)]
        sc_e = [s(f"sc_e{i}", [P, 3 * P]) for i in range(2)]
        sc_s = [s(f"sc_s{i}", [P, 3 * P]) for i in range(2)]
        sc_a = [s(f"sc_a{i}", [P, 3 * P]) for i in range(2)]
        aT = [s(f"aT{i}", [P, 3 * P]) for i in range(2)]
        lfU = [s(f"lfU{i}", [P, 3, P]) for i in range(2)]
        fx = s("fx", [P, 2, 8, 4])
        lf = s("lf", [P, TT, H])
        hss = s("hss", [P, TT, 2 * H])
        hrs = s("hrs", [P, TT, 2 * H])
        junk = s("junk", [P, 2, TT, P])
        sp_t = s("sp_t", [P, 3, TT, 16])

        pj = [ctx.enter_context(nc.psum_tensor(f"pj{i}", [P, TT, NB], F32)) for i in range(2)]
        pt = ctx.enter_context(nc.psum_tensor("pt", [P, TT, NB], F32))
        pm = ctx.enter_context(nc.psum_tensor("pm", [P, TT, NB], F32))

        ident = cst[:, C_ID, :]

        s_const = sem("const_loaded")
        s_x = [sem("x_loaded0"), sem("x_loaded1")]
        s_att = sem("att_loaded")
        raw_ready = [sem(f"raw_ready{i}") for i in range(SLOTS)]
        hi_ready = sem("hi_ready")
        lo_ready = sem("lo_ready")
        pe_used = sem("pe_used")
        nm_sq, nm_var, nm_sd, nm_rs, nm_out = (sem(n) for n in ("norm_squares", "norm_var", "norm_sd", "norm_rstd", "norm_scaled"))
        tp, tp_h, tp_l = sem("transposed"), sem("stationary_hi"), sem("stationary_lo")
        in1_evac, out1_evac, in2_evac, out2_evac, wq_evac = (sem(n) for n in ("in1_evac", "out1_evac", "in2_evac", "out2_evac", "wq_evac"))
        ffn_sems = {n: {k: sem(f"{n}_{k}") for k in ("up_evac", "dn_evac", "hid_T", "coef", "coef_h", "coef_l")} for n in ("mlp", "peer")}
        dve_link = sem("dve_link")
        act_link = sem("act_link")
        wt_loaded, wt_h, wt_l, wt_pe, wt_out = (sem(n) for n in ("tail_loaded", "tail_hi", "tail_lo", "tail_product", "tail_out"))

        def link(eng, s, n, ins):
            n[0] += 1
            ins.then_inc(s, 1)
            eng.wait_ge(s, n[0])


        def next_ones(q, j):
            return (q + (j + AHEAD) // SLOTS, (j + AHEAD) % SLOTS)

        def make_hi(act, q, j, first=False):
            act.wait_ge(raw_ready[j], q * 16 + 16)
            if not first:
                act.wait_ge(pe_used, q * SLOTS + j - 3)
            nc.scalar.activation(hi[:, j, :], raw[:, j, :], ACT.Copy).then_inc(hi_ready, 1)

        def make_lo(dve, q, j):
            dve.wait_ge(hi_ready, q * SLOTS + j + 1)
            nc.vector.tensor_tensor(lo[:, j, :], raw[:, j, :], hi[:, j, :].bitcast(F32),
                                    ALU.subtract).then_inc(lo_ready, 1)

        def multiply(pe, q, j, pair, sh, sl, k0, first, last):
            pe.wait_ge(lo_ready, q * SLOTS + j + 1)
            for k in range(4):
                cols = slice(k * NB, (k + 1) * NB)
                for t in range(TT):
                    tok = slice(t * P, (t + 1) * P)
                    begin, end = first and k == 0, last and k == 3
                    nc.tensor.matmul(pair[:, t, :], sh[:, k0 + k, tok], hi[:, j, cols], start=begin, stop=False)
                    nc.tensor.matmul(pair[:, t, :], sh[:, k0 + k, tok], lo[:, j, cols], start=False, stop=False)
                    mm = nc.tensor.matmul(pair[:, t, :], sl[:, k0 + k, tok], hi[:, j, cols], start=False, stop=end)
            mm.then_inc(pe_used, 1)

        def turns(eng, n, body, start=0):
            body(start)
            if n - start > 1:
                with eng.Fori(start + 1, n) as i:
                    body(i)

        def wide_pe(pe, q0, groups, evac, n):
            def body(i):
                for g in range(2):
                    if not (isinstance(i, int) and i == 0):
                        pe.wait_ge(evac, i * 2 + g - 1)
                    for j in range(SLOTS):
                        if g == 0 and isinstance(i, int) and i == 0:
                            pe.wait_ge(tp_l, 4 * n + j + 1)
                        multiply(pe, i * 2 + (q0 + g), j, pj[g], xh, xl, 4 * j, j == 0, j == SLOTS - 1)
            turns(pe, groups // 2, body)

        def wide_act(act, q0, groups, evac, out, between=None):
            def body(i):
                for g in range(2):
                    for j in range(SLOTS):
                        make_hi(act, *next_ones(i * 2 + (q0 + g), j))
                    if out is not None:
                        act.wait_ge(pe_used, (i * 2 + (q0 + g)) * SLOTS + SLOTS)
                        nc.scalar.activation(out[:, :, bass.ds((i * 2 + g) * NB, NB)], pj[g][:, :, :],
                                             ACT.Copy).then_inc(evac, 1)
                if between and isinstance(i, int):
                    between()
            turns(act, groups // 2, body)

        def wide_dve(dve, q0, groups, evac, add, between=None):
            def body(i):
                for g in range(2):
                    for j in range(SLOTS):
                        make_lo(dve, *next_ones(i * 2 + (q0 + g), j))
                    if add:
                        dve.wait_ge(pe_used, (i * 2 + (q0 + g)) * SLOTS + SLOTS)
                        part = resid[:, :, bass.ds((i * 2 + g) * NB, NB)]
                        nc.vector.tensor_tensor(part, part, pj[g][:, :, :], ALU.add).then_inc(evac, 1)
                if between and isinstance(i, int):
                    between()
            turns(dve, groups // 2, body)


        def job(s, n, last):
            return (5 * s + 1 + n - (1 if last else 0)) % 2

        def ffn_pe(pe, q0, blocks, S, n, step=None, between=None):
            def transposes(s):
                pe.wait_ge(S["up_evac"], s + 1)
                if not (isinstance(s, int) and s == 0):
                    pe.wait_ge(S["coef"], s)
                for k in range(4):
                    for t in range(TT):
                        tr = nc.tensor.transpose(pt[:, :, :].rearrange("p a n -> p (a n)")[:, k * 256 + t * P:k * 256 + t * P + P],
                                                 hid[:, t, k * P:(k + 1) * P], ident)
                tr.then_inc(S["hid_T"], 1)

            for j in range(SLOTS):
                pe.wait_ge(tp_l, 4 * n + j + 1)
                multiply(pe, q0, j, pj[0], xh, xl, 4 * j, j == 0, j == SLOTS - 1)
                if step:
                    step(j)
            if between:
                between()
            transposes(0)

            def part(s, par, last=False):
                first = isinstance(s, int) and s == 0
                if not last:
                    if not first:
                        pe.wait_ge(S["dn_evac"], s * 4 - 1)
                    for j in range(SLOTS):
                        multiply(pe, s * 2 + (q0 + 1), j, pj[job(par, 0, last)], xh, xl, 4 * j, j == 0, j == SLOTS - 1)
                pe.wait_ge(S["coef_l"], s + 1)
                for n in range(4):
                    if n == 1 and not last:
                        transposes(s + 1)
                    w = 4 * s + n - (1 if last else 0)
                    if (n != 1 or last) and not (first and n == 0):
                        pe.wait_ge(S["dn_evac"], w if n == 0 or last else w - 1)
                    multiply(pe, s * 2 + (q0 + (1 if last else 2)), n, pj[job(par, 1 + n, last)],
                             coef_h[par], coef_l[par], 0, True, True)
            ffn_turns(pe, blocks, part)

        def ffn_turns(eng, blocks, part):
            part(0, 0)
            part(1, 1)
            with eng.Fori(1, blocks // 2 - 1) as i:
                part(i * 2, 0)
                part(i * 2 + 1, 1)
            part(blocks - 2, 0)
            part(blocks - 1, 1, last=True)

        def ffn_act(act, q0, blocks, S, func, square, end, step=None, between=None):
            def up(s, pair, q):
                act.wait_ge(pe_used, q * SLOTS + SLOTS)
                if not (isinstance(s, int) and s == 0):
                    act.wait_ge(S["hid_T"], s)
                nc.scalar.activation(hid[:, :, :], pair[:, :, :], func).then_inc(S["up_evac"], 1)

            def coefficients(s, par):
                if square:
                    act.wait_ge(S["hid_T"], s + 1)
                    if not (isinstance(s, int) and s == 0):
                        act.wait_ge(S["coef_l"], s)
                    nc.scalar.activation(coef[:, :, :], pt[:, :, :].rearrange("p a (b n) -> p (a b) n", b=2), ACT.Square).then_inc(S["coef"], 1)
                act.wait_ge(S["coef"], s + 1)
                if not square and not (isinstance(s, int) and s == blocks - 1):
                    load_gates(act, s + 1, 1 - par)
                if not (isinstance(s, int) and s <= 1):
                    act.wait_ge(pe_used, (s * 2 + (q0 - 1)) * SLOTS)
                nc.scalar.activation(coef_h[par][:, :, :], coef[:, :, :], ACT.Copy).then_inc(S["coef_h"], 1)

            for j in range(SLOTS):
                make_hi(act, *next_ones(q0, j))
                if step:
                    step(j)
            up(0, pj[0], q0)
            if between:
                between()
            coefficients(0, 0)

            def part(s, par, last=False):
                q = s * 2 + (q0 + 1)
                if not last:
                    for j in range(SLOTS):
                        make_hi(act, *next_ones(q, j))
                    up(s + 1, pj[job(par, 0, False)], q)
                    q = s * 2 + (q0 + 2)
                for j in range(SLOTS):
                    nq, nj = next_ones(q, j)
                    if not (isinstance(nq, int) and nq >= end):
                        make_hi(act, nq, nj)
                    if j == 1 and not last:
                        coefficients(s + 1, 1 - par)
            ffn_turns(act, blocks, part)

        def ffn_dve(dve, q0, blocks, S, gates, end, step=None, between=None):
            def coefficients(s, par):
                if gates is not None:
                    dve.wait_ge(S["hid_T"], s + 1)
                    dve.wait_ge(gates[par], (s - par) * 8 + 16 if not isinstance(s, int) else 16 * (s // 2) + 16)
                    if not (isinstance(s, int) and s == 0):
                        dve.wait_ge(S["coef_l"], s)
                    nc.vector.tensor_tensor(
                        coef[:, :, :].rearrange("p b (o t) -> p b o t", o=8),
                        pt[:, :, :].rearrange("p a (b n) -> p (a b) n", b=2).rearrange("p b (o t) -> p b o t", o=8),
                        gate_e[par][:, :, :, :].rearrange("p o b t -> p b o t"), ALU.mult).then_inc(S["coef"], 1)

            def coefficients_lo(s, par):
                dve.wait_ge(S["coef_h"], s + 1)
                nc.vector.tensor_tensor(coef_l[par][:, :, :], coef[:, :, :], coef_h[par][:, :, :].bitcast(F32),
                                        ALU.subtract).then_inc(S["coef_l"], 1)

            for j in range(SLOTS):
                make_lo(dve, *next_ones(q0, j))
                if step:
                    step(j)
            if between:
                between()
            coefficients(0, 0)
            coefficients_lo(0, 0)

            def part(s, par, last=False):
                q = s * 2 + (q0 + 1)
                if not last:
                    for j in range(SLOTS):
                        make_lo(dve, *next_ones(q, j))
                    q = s * 2 + (q0 + 2)
                for j in range(SLOTS):
                    nq, nj = next_ones(q, j)
                    if not (isinstance(nq, int) and nq >= end):
                        make_lo(dve, nq, nj)
                    if j == 2 and not last:
                        coefficients_lo(s + 1, 1 - par)
                    dve.wait_ge(pe_used, q * SLOTS + j + 1)
                    part_ = resid[:, :, j * NB:(j + 1) * NB]
                    nc.vector.tensor_tensor(part_, part_, pj[job(par, 1 + j, last)][:, :, :],
                                            ALU.add).then_inc(S["dn_evac"], 1)
                    if j == 1 and not last:
                        coefficients(s + 1, 1 - par)
            ffn_turns(dve, blocks, part)


        def norm_act(act, n, loaded=None):
            for t in range(TT):
                if loaded:
                    act.wait_ge(loaded[t], 16)
                ins = nc.scalar.activation(nat[:, t, :], resid[:, t, :], ACT.Square, accum_out=stat[:, t:t + 1])
                ins.then_inc(nm_sq, 1)
            act.wait_ge(nm_var, n + 1)
            nc.scalar.activation(stat[:, 4:6], stat[:, 2:4], ACT.Sqrt).then_inc(nm_sd, 1)

        def norm_dve(dve, n, out, gain=None):
            dve.wait_ge(nm_sq, 2 * n + 2)
            nc.vector.tensor_scalar(stat[:, 2:4], stat[:, 0:2], 1.0 / D, EPS, ALU.mult, ALU.add).then_inc(nm_var, 1)
            dve.wait_ge(nm_sd, n + 1)
            nc.vector.reciprocal(stat[:, 6:8], stat[:, 4:6]).then_inc(nm_rs, 1)
            dve.wait_ge(nm_rs, n + 1)
            for b in range(4):
                c = slice(b * NB, (b + 1) * NB)
                for t in range(TT):
                    if gain is None:
                        ins = nc.vector.tensor_scalar(out[:, t, c], resid[:, t, c], stat[:, 6 + t:7 + t], None, ALU.mult)
                    else:
                        ins = nc.vector.scalar_tensor_tensor(out[:, t, c], resid[:, t, c], stat[:, 6 + t:7 + t], gain[:, c],
                                                             ALU.mult, ALU.mult)
                ins.then_inc(nm_out, 1)

        st_ps = [pt, pm]

        def station_pe(pe, n, src, norm=None):
            for b in range(4):
                if norm is not None:
                    pe.wait_ge(nm_out, 4 * norm + b + 1)
                if b >= 2:
                    pe.wait_ge(tp_l, 4 * n + b - 1)
                for k in range(4):
                    for t in range(TT):
                        col = (4 * b + k) * P
                        at = (k % 2) * 256 + t * P
                        tr = nc.tensor.transpose(st_ps[b % 2][:, k // 2, at:at + P], src[:, t, col:col + P], ident)
                tr.then_inc(tp, 1)

        def station_act(act, n, gain):
            for b in range(4):
                act.wait_ge(tp, 4 * n + b + 1)
                for k in range(4):
                    ins = nc.scalar.activation(xh[:, 4 * b + k, :], st_ps[b % 2][:, k // 2, (k % 2) * 256:(k % 2) * 256 + 256],
                                               ACT.Copy, scale=small[:, gain(4 * b + k):gain(4 * b + k) + 1])
                ins.then_inc(tp_h, 1)

        def station_dve(dve, n, gain):
            for b in range(4):
                dve.wait_ge(tp_h, 4 * n + b + 1)
                for k in range(4):
                    ins = nc.vector.scalar_tensor_tensor(
                        xl[:, 4 * b + k, :], st_ps[b % 2][:, k // 2, (k % 2) * 256:(k % 2) * 256 + 256],
                        small[:, gain(4 * b + k):gain(4 * b + k) + 1], xh[:, 4 * b + k, :].bitcast(F32),
                        ALU.mult, ALU.subtract)
                ins.then_inc(tp_l, 1)


        def tail_act(act, n, cols):
            act.wait_ge(wt_loaded, 16 * n + 16)
            nc.scalar.activation(wtail_h[:, :, 0:cols], wtail[:, :, 0:cols], ACT.Copy).then_inc(wt_h, 1)

        def tail_dve(dve, n, cols):
            dve.wait_ge(wt_h, n + 1)
            nc.vector.tensor_tensor(wtail_l[:, :, 0:cols], wtail[:, :, 0:cols], wtail_h[:, :, 0:cols].bitcast(F32),
                                    ALU.subtract).then_inc(wt_l, 1)

        def tail_pe(pe, n, cols):
            pe.wait_ge(wt_l, n + 1)
            for t in range(TT):
                tok = slice(t * P, (t + 1) * P)
                for k in range(KT):
                    o = pm[:, t, 0:cols]
                    nc.tensor.matmul(o, xh[:, k, tok], wtail_h[:, k, 0:cols], start=k == 0, stop=False)
                    nc.tensor.matmul(o, xh[:, k, tok], wtail_l[:, k, 0:cols], start=False, stop=False)
                    mm = nc.tensor.matmul(o, xl[:, k, tok], wtail_h[:, k, 0:cols], start=False, stop=k == KT - 1)
            mm.then_inc(wt_pe, 1)

        NH = 2 * H
        qk_cp, qk_T = sem("qk_copied"), sem("qk_transposed")
        z_done, z_read, fz_read, sp_ln, sp_done = sem("scores"), sem("sb_scores_read"), sem("fox_scores_read"), sem("sb_log"), sem("sb_softplus")
        cum_done, a_done, o_done, o_cp, o_sq = sem("cumulated"), sem("weights"), sem("out_summed"), sem("out_copied"), sem("out_squared")
        lfu_done, mx_done, p_done, rs_done, lf_done = sem("decay_factors"), sem("fox_max"), sem("fox_exp"), sem("fox_inverse_sum"), sem("log_f")
        hn_var, hn_sd, hn_rs, hn_out = sem("head_var"), sem("head_sd"), sem("head_rstd"), sem("head_scaled")
        lf_x, lf_ln = sem("lf_logit"), sem("lf_log")


        def qcol(h):
            return h * P if h < H else 3 * H * P + (h - H) * P

        z_bank = [pj[1][:, 0, 0:384], pj[1][:, 1, 0:384], pt[:, 0, 0:384]]
        t_bank = [pj[0][:, 0, :], pj[0][:, 1, :]]
        pT_bank = pt[:, 1, 0:384]

        def att1_pe(pe):
            def transpose_qk(h):
                if h >= 2:
                    pe.wait_ge(qk_cp, h - 1)
                for i in range(2):
                    for t in range(TT):
                        c = qcol(h) + i * H * P
                        tr = nc.tensor.transpose(t_bank[h % 2][:, i * 256 + t * P:i * 256 + t * P + P], proj1[:, t, c:c + P], ident)
                tr.then_inc(qk_T, 1)

            def scores(h):
                pe.wait_ge(qk_cp, h + 1)
                if h >= 3:
                    if h - 3 < H:
                        pe.wait_ge(z_read, h - 2)
                    else:
                        pe.wait_ge(fz_read, h - 2 - H)
                z, qT, kT = z_bank[h % 3], qkT[h % 2][:, 0, :], qkT[h % 2][:, 1, :]
                if h < H:
                    nc.tensor.matmul(z[:, 0:256], kT[:, 0:P], qT[:, 0:256], start=True, stop=False, skip_group_check=True)
                    mm = nc.tensor.matmul(z[:, 256:384], kT[:, P:256], qT[:, P:256], start=False, stop=False, skip_group_check=True)
                else:
                    g = lfU[h % 2]
                    pe.wait_ge(lfu_done, h - H + 1)
                    nc.tensor.matmul(z[:, 0:P], qT[:, 0:P], kT[:, 0:P], start=True, stop=False, skip_group_check=True)
                    nc.tensor.matmul(z[:, 0:P], g[:, 0, :], cst[:, C_GT, :], start=False, stop=False, skip_group_check=True)
                    nc.tensor.matmul(z[:, P:384], qT[:, P:256], kT[:, 0:256], start=False, stop=False, skip_group_check=True)
                    nc.tensor.matmul(z[:, P:384], g[:, 1, :], cst[:, C_ONES:C_ONES + 2, :].rearrange("p a n -> p (a n)"), start=False, stop=False, skip_group_check=True)
                    mm = nc.tensor.matmul(z[:, P:256], g[:, 2, :], cst[:, C_GT, :], start=False, stop=True, skip_group_check=True)
                mm.then_inc(z_done, 1)

            def cumulate(h):
                z = z_bank[h % 3]
                if h < H:
                    pe.wait_ge(sp_done, h + 1)
                    s_ = sc_s[h % 2]
                    nc.tensor.matmul(z[:, 0:256], att[:, A_NGE, :], s_[:, 0:256], start=False, stop=False, skip_group_check=True)
                    nc.tensor.matmul(z[:, P:256], att[:, A_NONES, :], s_[:, 256:384], start=False, stop=False, skip_group_check=True)
                    mm = nc.tensor.matmul(z[:, 256:384], att[:, A_NGE, :], s_[:, 256:384], start=False, stop=True, skip_group_check=True)
                else:
                    pe.wait_ge(p_done, h - H + 1)
                    pe.wait_ge(a_done, h)
                    for i in range(3):
                        mm = nc.tensor.transpose(pT_bank[:, i * P:(i + 1) * P], sc_e[h % 2][:, i * P:(i + 1) * P], ident)
                mm.then_inc(cum_done, 1)

            def sum_v(h):
                pe.wait_ge(a_done, h + 1)
                if h >= 2:
                    pe.wait_ge(o_cp, h - 1)
                o, a, c = pm[:, h % 2, :], aT[h % 2], qcol(h) + 2 * H * P
                nc.tensor.matmul(o[:, 0:P], a[:, 0:P], proj1[:, 0, c:c + P], start=True, stop=False, skip_group_check=True)
                nc.tensor.matmul(o[:, P:256], a[:, P:256], proj1[:, 0, c:c + P], start=False, stop=False, skip_group_check=True)
                nc.tensor.matmul(o[:, P:256], a[:, 256:384], proj1[:, 1, c:c + P], start=False, stop=True,
                                 skip_group_check=True).then_inc(o_done, 1)

            pe.wait_ge(in1_evac, G1)
            pe.wait_ge(wt_out, 1)
            pe.wait_ge(s_att, 16)
            for i in range(NH + 3):
                for stage, f in enumerate((transpose_qk, scores, cumulate, sum_v)):
                    if 0 <= i - stage < NH:
                        f(i - stage)

        def att1_act(act, n):
            def exponents(h):
                e = sc_e[h % 2]
                if h >= 2:
                    act.wait_ge(cum_done, h - 1)
                if h < H:
                    act.wait_ge(z_done, h + 1)
                    link(act, act_link, n, nc.scalar.activation(e[:, :], z_bank[h % 3], ACT.Abs))
                    link(act, act_link, n, nc.scalar.activation(e[:, :], e[:, :], ACT.Exp, scale=-1.0))
                    nc.scalar.activation(e[:, :], e[:, :], ACT.Ln, bias=1.0).then_inc(sp_ln, 1)
                else:
                    act.wait_ge(mx_done, h - H + 1)
                    f, s_ = fx[:, :, h - H, :], sc_s[h % 2]
                    nc.scalar.activation(e[:, 0:P], s_[:, 0:P], ACT.Exp, bias=f[:, 0, 0:1], accum_out=f[:, 0, 1:2])
                    nc.scalar.activation(e[:, P:384], s_[:, P:384], ACT.Exp, bias=f[:, 1, 0:1],
                                         accum_out=f[:, 1, 1:2]).then_inc(p_done, 1)

            def weights(h):
                if h >= 2:
                    act.wait_ge(o_done, h - 1)
                if h < H:
                    act.wait_ge(z_read, h + 1)
                    nc.scalar.activation(aT[h % 2][:, :], sc_a[h % 2][:, :], ACT.Exp).then_inc(a_done, 1)
                else:
                    act.wait_ge(cum_done, h + 1)
                    nc.scalar.activation(aT[h % 2][:, :], pT_bank, ACT.Copy).then_inc(a_done, 1)

            def squares(h):
                act.wait_ge(o_cp, h + 1)
                if h >= 2:
                    act.wait_ge(o_sq, h - 1)
                for t in range(TT):
                    ins = nc.scalar.activation(junk[:, h % 2, t, :], proj1[:, t, h * P:(h + 1) * P], ACT.Square, accum_out=hss[:, t, h:h + 1])
                ins.then_inc(o_sq, 1)

            act.wait_ge(lf_x, 1)
            link(act, act_link, n, nc.scalar.activation(sp_t[:, 1, :, 0:H], sp_t[:, 0, :, 0:H], ACT.Abs))
            link(act, act_link, n, nc.scalar.activation(sp_t[:, 1, :, 0:H], sp_t[:, 1, :, 0:H], ACT.Exp, scale=-1.0))
            nc.scalar.activation(sp_t[:, 1, :, 0:H], sp_t[:, 1, :, 0:H], ACT.Ln, bias=1.0).then_inc(lf_ln, 1)
            for i in range(NH + 3):
                for stage, f in enumerate((None, exponents, weights, squares)):
                    if f and 0 <= i - stage < NH:
                        f(i - stage)
            act.wait_ge(hn_var, 1)
            nc.scalar.activation(hrs[:, :, :], hss[:, :, :], ACT.Sqrt).then_inc(hn_sd, 1)

        def att1_dve(dve, n):
            def copy_qk(h):
                dve.wait_ge(qk_T, h + 1)
                if h >= 2:
                    dve.wait_ge(z_done, h - 1)
                nc.vector.tensor_scalar(qkT[h % 2][:, 0, :], t_bank[h % 2][:, 0:256], SCALE, None, ALU.mult)
                nc.vector.tensor_copy(qkT[h % 2][:, 1, :], t_bank[h % 2][:, 256:512]).then_inc(qk_cp, 1)

            def exponents(h):
                s_ = sc_s[h % 2]
                if h < H:
                    dve.wait_ge(sp_ln, h + 1)
                    link(dve, dve_link, n, nc.vector.scalar_tensor_tensor(s_[:, :], z_bank[h % 3], 0.0, sc_e[h % 2][:, :], ALU.max, ALU.add))
                    nc.vector.tensor_tensor(s_[:, :], s_[:, :], att[:, A_SBM:A_SBM + 3, :].rearrange("p a n -> p (a n)"),
                                            ALU.mult).then_inc(sp_done, 1)
                else:
                    dve.wait_ge(z_done, h + 1)
                    if h >= H + 2:
                        dve.wait_ge(p_done, h - H - 1)
                    nc.vector.tensor_tensor(s_[:, :], z_bank[h % 3], att[:, A_FXA:A_FXA + 3, :].rearrange("p a n -> p (a n)"),
                                            ALU.add).then_inc(fz_read, 1)
                    dve.wait_ge(fz_read, h - H + 1)
                    f = fx[:, :, h - H, :]
                    nc.vector.tensor_reduce(f[:, 0, 0:1], s_[:, 0:P], AX.X, ALU.max, negate=True)
                    nc.vector.tensor_reduce(f[:, 1, 0:1], s_[:, P:384], AX.X, ALU.max, negate=True).then_inc(mx_done, 1)

            def weights(h):
                if h < H:
                    dve.wait_ge(cum_done, h + 1)
                    if h >= 2:
                        dve.wait_ge(a_done, h - 1)
                    nc.vector.scalar_tensor_tensor(sc_a[h % 2][:, :], z_bank[h % 3], 0.0,
                                                   att[:, A_SBA:A_SBA + 3, :].rearrange("p a n -> p (a n)"),
                                                   ALU.min, ALU.add).then_inc(z_read, 1)
                else:
                    dve.wait_ge(p_done, h - H + 1)
                    nc.vector.reciprocal(fx[:, :, h - H, 2:3], fx[:, :, h - H, 1:2]).then_inc(rs_done, 1)

            def copy_o(h):
                dve.wait_ge(o_done, h + 1)
                o = pm[:, h % 2, 0:256].rearrange("p (t n) -> p t n", t=TT)
                if h < H:
                    nc.vector.tensor_copy(proj1[:, :, h * P:(h + 1) * P], o).then_inc(o_cp, 1)
                else:
                    dve.wait_ge(rs_done, h - H + 1)
                    for t in range(TT):
                        ins = nc.vector.tensor_scalar(proj1[:, t, h * P:(h + 1) * P], o[:, t, :], fx[:, t, h - H, 2:3], None, ALU.mult)
                    ins.then_inc(o_cp, 1)

            dve.wait_ge(wt_pe, 1)
            nc.vector.tensor_copy(tail[:, :, 0:H], pm[:, :, 0:H]).then_inc(wt_out, 1)
            dve.wait_ge(wt_out, 1)
            nc.vector.tensor_tensor(sp_t[:, 0, :, 0:H], tail[:, :, 0:H],
                                    small[:, S_BF:S_BF + H].unsqueeze(1).broadcast_to([P, TT, H]), ALU.add).then_inc(lf_x, 1)
            dve.wait_ge(lf_ln, 1)
            nc.vector.scalar_tensor_tensor(lf[:, :, :], sp_t[:, 0, :, 0:H], 0.0, sp_t[:, 1, :, 0:H],
                                           ALU.min, ALU.subtract).then_inc(lf_done, 1)
            for i in range(NH + 3):
                for stage, f in enumerate((copy_qk, exponents, weights, copy_o)):
                    if 0 <= i - stage < NH:
                        f(i - stage)
            dve.wait_ge(o_sq, NH)
            nc.vector.tensor_scalar(hss[:, :, :], hss[:, :, :], 1.0 / HD, EPS, ALU.mult, ALU.add).then_inc(hn_var, 1)
            dve.wait_ge(hn_sd, 1)
            nc.vector.reciprocal(hss[:, :, :], hrs[:, :, :]).then_inc(hn_rs, 1)
            dve.wait_ge(hn_rs, 1)
            for t in range(TT):
                o = proj1[:, t, 0:D].rearrange("p (h n) -> p h n", h=NH)
                nc.vector.tensor_tensor(o, o, hss[:, t, :].unsqueeze(2).broadcast_to([P, NH, HD]), ALU.mult).then_inc(hn_out, 1)

        def att1_pool(pool):
            pool.wait_ge(lf_done, 1)
            for h in range(H):
                if h >= 2:
                    pool.wait_ge(z_done, H + h - 1)
                g = lfU[h % 2]
                nc.gpsimd.tensor_scalar(g[:, 0, :], cst[:, C_LE, :], lf[:, 0, h:h + 1], None, ALU.mult)
                nc.gpsimd.tensor_scalar(g[:, 1, :], cst[:, C_LE, :], lf[:, 1, h:h + 1], None, ALU.mult)
                nc.gpsimd.tensor_scalar(g[:, 2, :], cst[:, C_ONES, :], lf[:, 0, h:h + 1], None, ALU.mult).then_inc(lfu_done, 1)

        A_Q, A_F, A_I, A_G = 0, H * P, 2 * H * P, 3 * H * P
        B_Q, B_K, B_V, B_Z = 4 * H * P, 4 * H * P + 512, 5 * H * P, 6 * H * P
        at_z = at_y + 4 * TT * W2

        s = region(at_x)
        hk = s("hk", [P, TT, H * P])
        at_h = at_x + 4 * TT * H * P
        lb = region(at_z)("lb", [P, 2, H * P])
        lb_e = proj2[:, :, B_Z:B_Z + H * P]
        s = region(at_h)
        hE = [s(f"hE{i}", [P, 8, P]) for i in range(2)]
        hKE = [s(f"hKE{i}", [P, 8, P]) for i in range(2)]
        hqk = [s(f"hqk{i}", [P, 2, TT * P]) for i in range(2)]
        hA = s("hA", [P, 8, P])
        z = region(at_z)
        haT = [z(f"haT{i}", [P, 3 * P]) for i in range(2)]
        hkx = [z(f"hkx{i}", [P, P]) for i in range(2)]
        hjunk = z("hjunk", [P, 2, TT, P])
        mss = z("mss", [P, TT, 2 * H])
        mrs = z("mrs", [P, TT, 2 * H])
        at_z2 = at_z + 4 * (6 * P + 2 * P + 4 * P + 64)

        lbl_in, lb_steps, h_sig, h_f, h_logf = sem("lbl_loaded"), sem("lower_bound_steps"), sem("h_sigmoid"), sem("h_forget"), sem("h_log_forget")
        h_key, h_T, h_qk, h_X, h_E = sem("h_key"), sem("h_transposed"), sem("h_qk_copied"), sem("h_decay_sums"), sem("h_decays")
        h_KE, h_QE, h_A, h_aT, h_x, h_o, h_ocp, h_osq = (sem(n) for n in ("h_key_decayed", "h_query_decayed", "h_products", "h_weights", "h_cross", "h_out", "h_out_copied", "h_out_squared"))

        def hg_steps(fs):
            for i in range(2 * H + 4):
                for lag, f in fs:
                    if 0 <= i - lag < 2 * H:
                        f(i - lag)

        def hcols(x_):
            return slice(x_ * H * P // 2, (x_ + 1) * H * P // 2)

        def fcols(x_):
            return proj2[:, :, A_F + x_ * H * P // 2:A_F + (x_ + 1) * H * P // 2]

        def bound_act(act):
            act.wait_ge(lb_steps, 2)
            nc.scalar.activation(lb_e, lb[:, :, :], ACT.Exp).then_inc(lb_steps, 1)
            act.wait_ge(lb_steps, 5)

        def bound_dve(dve, n):
            dve.wait_ge(lbl_in, 16)
            nc.vector.tensor_tensor(lb_e[:, 0, :], lb[:, 0, :], lb[:, 1, :], ALU.max).then_inc(lb_steps, 1)
            dve.wait_ge(lb_steps, 1)
            nc.vector.tensor_tensor(lb[:, :, :], lb[:, :, :], lb_e[:, 0:1, :].broadcast_to([P, 2, H * P]), ALU.subtract).then_inc(lb_steps, 1)
            dve.wait_ge(lb_steps, 3)
            link(dve, dve_link, n, nc.vector.tensor_tensor(lb_e[:, 1, :], lb_e[:, 1, :], lb_e[:, 0, :], ALU.add))
            link(dve, dve_link, n, nc.vector.reciprocal(lb[:, 0, :], lb_e[:, 1, :]))
            nc.vector.tensor_tensor(lb[:, 0, :], lb_e[:, 0, :], lb[:, 0, :], ALU.mult).then_inc(lb_steps, 1)
            dve.wait_ge(lb_steps, 4)
            nc.vector.tensor_scalar(lb[:, 1, :], lb[:, 0, :], -1.0, 1.0, ALU.mult, ALU.add).then_inc(lb_steps, 1)
            dve.wait_ge(lb_steps, 5)

        def hgrn_pe(pe):
            def products(c):
                h, t = c // 2, c % 2
                pe.wait_ge(h_QE, c + 1)
                pe.wait_ge(h_KE, c + 1)
                if c >= 1:
                    pe.wait_ge(h_aT, c)
                lev = 1 - t
                A = pt[:, :, :].rearrange("p a (b n) -> p (a b) n", n=P)
                k_, q_ = hqk[h % 2][:, 1, t * P:t * P + P], hqk[h % 2][:, 0, t * P:t * P + P]
                for b in range(2):
                    for i in range(4):
                        l = 4 * b + i - 1
                        kk, qq = (k_, q_) if l < 0 else (hKE[c % 2][:, lev + l, :], hE[c % 2][:, lev + l, :])
                        mm = nc.tensor.matmul(A[:, 4 * b + i, :], kk, qq, start=i == 0, stop=i == 3, skip_group_check=True)
                mm.then_inc(h_A, 1)
                if t == 1:
                    if h >= 1:
                        pe.wait_ge(h_x, h)
                    nc.tensor.matmul(pj[0][:, 1, 0:P], hkx[h % 2][:, :], hE[c % 2][:, 7, :], start=True, stop=True).then_inc(h_A, 1)

            def decay_sums(c):
                h, t = c // 2, c % 2
                if c == H:
                    pe.wait_ge(h_logf, 2)
                if c >= 1:
                    pe.wait_ge(h_E, c)
                g = proj2[:, t, A_F + h * P:A_F + (h + 1) * P]
                for b in range(2):
                    c0 = (C_GT if t == 0 else C_LEV) + 4 * b
                    mm = nc.tensor.matmul(pj[1][:, b, :], g, cst[:, c0:c0 + 4, :].rearrange("p a n -> p (a n)"), start=True, stop=True)
                mm.then_inc(h_X, 1)

            def transposes(c):
                h, t = c // 2, c % 2
                if t:
                    return
                if c == H:
                    pe.wait_ge(h_key, 2)
                if h >= 1:
                    pe.wait_ge(h_qk, h)
                for i, src in enumerate((proj2[:, :, A_Q + h * P:A_Q + (h + 1) * P], hk[:, :, h * P:(h + 1) * P])):
                    for t in range(TT):
                        tr = nc.tensor.transpose(pj[0][:, 0, i * 256 + t * P:i * 256 + t * P + P], src[:, t, :], ident)
                tr.then_inc(h_T, 1)

            def sum_v(c):
                h, t = c // 2, c % 2
                if t == 0:
                    return
                pe.wait_ge(h_aT, c + 1)
                pe.wait_ge(h_x, h + 1)
                if h >= 2:
                    pe.wait_ge(h_ocp, h - 1)
                o, a, v0 = pm[:, h % 2, :], haT[h % 2], A_I + h * P
                nc.tensor.matmul(o[:, 0:P], a[:, 0:P], proj2[:, 0, v0:v0 + P], start=True, stop=False, skip_group_check=True)
                nc.tensor.matmul(o[:, P:256], a[:, P:256], proj2[:, 0, v0:v0 + P], start=False, stop=False, skip_group_check=True)
                nc.tensor.matmul(o[:, P:256], a[:, 256:384], proj2[:, 1, v0:v0 + P], start=False, stop=True,
                                 skip_group_check=True).then_inc(h_o, 1)

            pe.wait_ge(h_logf, 1)
            pe.wait_ge(h_key, 1)
            hg_steps(((2, products), (0, transposes), (0, decay_sums), (3, sum_v)))

        def hgrn_act(act, n):
            def copy_qk(c):
                h = c // 2
                if c % 2:
                    return
                act.wait_ge(h_T, h + 1)
                if h >= 2:
                    act.wait_ge(h_A, 3 * (h - 1))
                    act.wait_ge(h_KE, 2 * (h - 1))
                    act.wait_ge(h_QE, 2 * (h - 1))
                nc.scalar.activation(hqk[h % 2][:, :, :].rearrange("p a n -> p (a n)"), pj[0][:, 0, :], ACT.Copy).then_inc(h_qk, 1)

            def decays(c):
                act.wait_ge(h_X, c + 1)
                if c >= 2:
                    act.wait_ge(h_A, (c - 2) // 2 * 3 + 1 + 2 * ((c - 2) % 2))
                nc.scalar.activation(hE[c % 2][:, :, :].rearrange("p a n -> p (a n)"), pj[1][:, :, :].rearrange("p a n -> p (a n)"), ACT.Exp).then_inc(h_E, 1)

            def cross(c):
                h = c // 2
                if c % 2 == 0:
                    return
                act.wait_ge(h_A, 3 * h + 3)
                if h >= 2:
                    act.wait_ge(h_o, h - 1)
                nc.scalar.activation(haT[h % 2][:, P:256], pj[0][:, 1, 0:P], ACT.Copy).then_inc(h_x, 1)

            def squares(c):
                h = c // 2
                if c % 2 == 0:
                    return
                act.wait_ge(h_ocp, h + 1)
                if h >= 2:
                    act.wait_ge(h_osq, h - 1)
                for t in range(TT):
                    ins = nc.scalar.activation(hjunk[:, h % 2, t, :], proj2[:, t, h * P:(h + 1) * P], ACT.Square, accum_out=mss[:, t, h:h + 1])
                ins.then_inc(h_osq, 1)

            act.wait_ge(in2_evac, G2)
            act.wait_ge(wt_pe, 2)
            for x_ in range(2):
                nc.scalar.activation(hk[:, :, hcols(x_)], fcols(x_), ACT.Sigmoid, scale=-1.0).then_inc(h_sig, 1)
                act.wait_ge(h_sig, 2 * x_ + 1)
                nc.scalar.activation(fcols(x_), fcols(x_), ACT.Sigmoid).then_inc(h_sig, 1)
            for x_ in range(2):
                act.wait_ge(h_f, 2 * x_ + 2)
                nc.scalar.activation(fcols(x_), fcols(x_), ACT.Ln).then_inc(h_logf, 1)
            hg_steps(((0, copy_qk), (0, decays), (2, cross), (3, squares)))

        def hgrn_dve(dve, n):
            def queries(c):
                h, t = c // 2, c % 2
                dve.wait_ge(h_KE, c + 1)
                e = hE[c % 2]
                q_ = hqk[h % 2][:, 0, t * P:t * P + P]
                nc.vector.tensor_tensor(e[:, :, :], e[:, :, :], q_.unsqueeze(1).broadcast_to([P, 8, P]), ALU.mult).then_inc(h_QE, 1)

            def weights(c):
                h, t = c // 2, c % 2
                dve.wait_ge(h_A, 3 * h + 1 + t)
                link(dve, dve_link, n, nc.vector.tensor_tensor(
                    hA[:, :, :], pt[:, :, :].rearrange("p a (b n) -> p (a b) n", n=P), cst[:, C_MASK:C_MASK + 8, :], ALU.mult))
                if t == 0 and h >= 2:
                    dve.wait_ge(h_o, h - 1)
                nc.vector.tensor_reduce(haT[h % 2][:, 2 * t * P:2 * t * P + P], hA[:, :, :].rearrange("p a n -> p n a"), AX.X, ALU.add).then_inc(h_aT, 1)

            def copy_o(c):
                h = c // 2
                if c % 2 == 0:
                    return
                dve.wait_ge(h_o, h + 1)
                nc.vector.tensor_copy(proj2[:, :, h * P:(h + 1) * P], pm[:, h % 2, 0:256].rearrange("p (t n) -> p t n", t=TT)).then_inc(h_ocp, 1)

            over = lambda i, x_: lb[:, i, hcols(x_)].unsqueeze(1).broadcast_to([P, TT, H * P // 2])
            for x_ in range(2):
                dve.wait_ge(h_sig, 2 * x_ + 2)
                nc.vector.tensor_tensor(fcols(x_), fcols(x_), over(1, x_), ALU.mult).then_inc(h_f, 1)
                dve.wait_ge(h_f, 2 * x_ + 1)
                nc.vector.tensor_tensor(fcols(x_), fcols(x_), over(0, x_), ALU.add).then_inc(h_f, 1)
                nc.vector.tensor_tensor(hk[:, :, hcols(x_)], hk[:, :, hcols(x_)], over(1, x_), ALU.mult).then_inc(h_key, 1)
            hg_steps(((2, weights), (0, queries), (3, copy_o)))

        def hgrn_pool(pool):
            pool.wait_ge(h_key, 2)
            for c in range(2 * H):
                h, t = c // 2, c % 2
                pool.wait_ge(h_E, c + 1)
                pool.wait_ge(h_qk, h + 1)
                if c >= 2:
                    pool.wait_ge(h_A, (c - 2) // 2 * 3 + 1 + 2 * ((c - 2) % 2))
                k_ = hqk[h % 2][:, 1, t * P:t * P + P]
                if t == 0:
                    nc.gpsimd.tensor_tensor(hkx[h % 2][:, :], hE[c % 2][:, 0, :], k_, ALU.mult)
                lev = 1 - t
                nc.gpsimd.tensor_tensor(hKE[c % 2][:, lev:lev + 7, :], hE[c % 2][:, lev:lev + 7, :],
                                        k_.unsqueeze(1).broadcast_to([P, 7, P]), ALU.mult).then_inc(h_KE, 1)

        s = region(at_x)
        dN = s("dN", [P, 16, P])
        dT = s("dT", [P, 16, P])
        dU = s("dU", [P, 16, P])
        dB = [s(f"dB{i}", [P, 4, P]) for i in range(2)]
        dP = [s(f"dP{i}", [P, 4, P]) for i in range(2)]
        s = region(at_x)
        dqg = s("dqg", [P, H, P])
        dqgT = s("dqgT", [P, H, P])
        s = region(at_x + 4 * 16 * P)
        cy = [s(f"cy{i}", [P, TT * P]) for i in range(4)]
        dkb = [s(f"dkb{i}", [P, 4, P]) for i in range(2)]
        dsq = s("dsq", [P, TT, 2 * 512])
        s = region(at_x + 4 * 32 * P)
        dgS = [s(f"dgS{i}", [P, 4, P]) for i in range(2)]
        dE = [s(f"dE{i}", [P, 4, P]) for i in range(2)]
        s = region(at_x + 4 * 16 * P)
        dS = s("dS", [P, H, P])
        dwT = s("dwT", [P, H, P])
        s = region(at_x + 4 * 48 * P)
        dvn = [s(f"dvn{i}", [P, 4, P]) for i in range(4)]
        z = region(at_z)
        dkq = z("dkq", [P, 4, P])
        dkbT = z("dkbT", [P, 4, P])
        dEm = z("dEm", [P, 4, P])
        z = region(at_z2)
        gt = z("gt", [P, 6, TT, H])
        dn = z("dn", [P, 3, TT, H])
        dkd = proj2[:, 0, A_I:A_I + H * P].rearrange("p (a n) -> p a n", a=H)
        dX = proj2[:, 1, A_I:A_I + H * P].rearrange("p (a n) -> p a n", a=H)

        def aqk(m):
            return proj2[:, m // 2, A_F + (m % 2) * 512:A_F + (m % 2) * 512 + 512]

        c_T, c_tap, c_y, c_silu, c_B, c_out = sem("c_transposed"), sem("c_taps"), sem("c_convolved"), sem("c_silu"), sem("c_back"), sem("c_out")
        g_step, g_pe = sem("gate_steps"), sem("gate_sums")
        l_step = sem("l2_steps")
        d_pool, d_vb, d_T, d_cp, d_E, d_Em, d_S, d_N = (sem(n) for n in ("d_operands", "d_vbeta", "d_transposed", "d_copied", "d_decays", "d_masked", "d_scores", "d_weighted"))
        d_B, d_PP, d_Pc, d_dd, d_TU = (sem(n) for n in ("inv_level", "inv_product", "inv_copied", "inv_deltas", "inv_updated"))
        f_pe, f_cp, f_dve, f_pool = sem("state_products"), sem("state_copied"), sem("state_out"), sem("state_queries")
        m_step = sem("mix_steps")
        NL = 7

        def conv_pe(pe):
            def forward(c):
                if c >= 2:
                    pe.wait_ge(c_y, c - 1)
                for t in range(TT):
                    tr = nc.tensor.transpose(pj[0][:, c % 2, t * P:t * P + P], proj2[:, t, B_Q + c * P:B_Q + (c + 1) * P], ident)
                tr.then_inc(c_T, 1)

            def back(c):
                pe.wait_ge(c_silu, c + 1)
                if c >= 2:
                    pe.wait_ge(c_out, c - 1)
                for t in range(TT):
                    tr = nc.tensor.transpose(pj[1][:, c % 2, t * P:t * P + P], cy[c % 4][:, t * P:t * P + P], ident)
                tr.then_inc(c_B, 1)

            pe.wait_ge(h_osq, H)
            pe.wait_ge(h_ocp, H)
            for i in range(18):
                if i < 16:
                    forward(i)
                if i >= 2:
                    back(i - 2)

        def conv_act(act, n):
            for i in range(18):
                if i < 16:
                    act.wait_ge(c_y, i + 1)
                    nc.scalar.activation(cy[i % 4][:, :], cy[i % 4][:, :], ACT.Silu).then_inc(c_silu, 1)
                if i >= 2:
                    c = i - 2
                    act.wait_ge(c_B, c + 1)
                    nc.scalar.activation(proj2[:, :, B_Q + c * P:B_Q + (c + 1) * P],
                                         pj[1][:, c % 2, 0:256].rearrange("p (t n) -> p t n", t=TT), ACT.Copy).then_inc(c_out, 1)

        def conv_dve(dve, n):
            w = lambda c, j: small[:, S_CONV + 4 * c + j:S_CONV + 4 * c + j + 1]
            for c0 in range(0, 16, 2):
                for j in range(4):
                    for c in (c0, c0 + 1):
                        y_, x_ = cy[c % 4], pj[0][:, c % 2, 0:256]
                        if j == 0:
                            dve.wait_ge(c_T, c + 1)
                            if c >= 4:
                                dve.wait_ge(c_B, c - 3)
                            nc.vector.tensor_scalar(y_[:, :], x_, w(c, 3), None, ALU.mult).then_inc(c_tap, 1)
                        else:
                            dve.wait_ge(c_tap, 3 * c0 + (c - c0) + 2 * (j - 1) + 1)
                            ins = nc.vector.scalar_tensor_tensor(y_[:, j:], x_[:, 0:256 - j], w(c, 3 - j), y_[:, j:], ALU.mult, ALU.add)
                            ins.then_inc(c_tap if j < 3 else c_y, 1)

        def gates_act(act, n):
            nc.scalar.activation(gt[:, 0, :, :], tail[:, :, 0:H], ACT.Sigmoid).then_inc(g_step, 1)
            act.wait_ge(g_step, 2)
            link(act, act_link, n, nc.scalar.activation(gt[:, 2, :, :], gt[:, 1, :, :], ACT.Abs))
            link(act, act_link, n, nc.scalar.activation(gt[:, 2, :, :], gt[:, 2, :, :], ACT.Exp, scale=-1.0))
            nc.scalar.activation(gt[:, 4, 0, :], small[:, S_ALOG:S_ALOG + H], ACT.Exp)
            nc.scalar.activation(gt[:, 2, :, :], gt[:, 2, :, :], ACT.Ln, bias=1.0).then_inc(g_step, 1)
            act.wait_ge(g_pe, 1)
            nc.scalar.activation(gt[:, 5, :, :], pm[:, 0, 0:2 * H].rearrange("p (t h) -> p t h", t=TT), ACT.Exp).then_inc(g_step, 1)

        def gates_dve(dve, n):
            dve.wait_ge(g_step, 1)
            nc.vector.tensor_tensor(gt[:, 1, :, :], tail[:, :, H:2 * H], small[:, S_DTB:S_DTB + H].unsqueeze(1).broadcast_to([P, TT, H]), ALU.add).then_inc(g_step, 1)
            dve.wait_ge(g_step, 3)
            link(dve, dve_link, n, nc.vector.scalar_tensor_tensor(gt[:, 3, :, :], gt[:, 1, :, :], 0.0, gt[:, 2, :, :], ALU.max, ALU.add))
            for t in range(TT):
                ins = nc.vector.scalar_tensor_tensor(gt[:, 3, t, :], gt[:, 3, t, :], -1.0, gt[:, 4, 0, :], ALU.mult, ALU.mult)
            link(dve, dve_link, n, ins)
            ins = nc.vector.tensor_copy(dn[:, 0, :, :], gt[:, 3, :, :])
            ins.then_inc(l_step, 1)

        def gates_pe(pe):
            pe.wait_ge(l_step, 1)
            nc.tensor.matmul(pm[:, 0, 0:H], cst[:, C_GT, :], gt[:, 3, 0, :], start=True, stop=True)
            nc.tensor.matmul(pm[:, 0, H:2 * H], cst[:, C_LE, :], gt[:, 3, 1, :], start=True, stop=True).then_inc(g_pe, 1)

        def l2_act(act, n):
            act.wait_ge(l_step, 2)
            nc.scalar.activation(dn[:, 1, :, :], dn[:, 0, :, :], ACT.Sqrt).then_inc(l_step, 1)

        def l2_dve(dve, n):
            qk = proj2[:, :, B_Q:B_Q + 1024]
            dve.wait_ge(c_out, 8)
            link(dve, dve_link, n, nc.vector.tensor_tensor(dsq[:, :, :], qk, qk, ALU.mult))
            link(dve, dve_link, n, nc.vector.tensor_reduce(dn[:, 0, :, :], dsq[:, :, :].rearrange("p t (h n) -> p t h n", n=P), AX.X, ALU.add))
            nc.vector.tensor_scalar(dn[:, 0, :, :], dn[:, 0, :, :], EPS, None, ALU.add).then_inc(l_step, 1)
            dve.wait_ge(l_step, 3)
            link(dve, dve_link, n, nc.vector.reciprocal(dn[:, 2, :, :], dn[:, 1, :, :]))
            link(dve, dve_link, n, nc.vector.tensor_scalar(dn[:, 2, :, 0:4], dn[:, 2, :, 0:4], SCALE, None, ALU.mult))
            for t in range(TT):
                x_ = proj2[:, t, B_Q:B_Q + 1024].rearrange("p (h n) -> p h n", n=P)
                nc.vector.tensor_tensor(x_, x_, dn[:, 2, t, :].unsqueeze(2).broadcast_to([P, H, P]), ALU.mult).then_inc(l_step, 1)

        def delta_pool(pool):
            pool.wait_ge(l_step, 5)
            pool.wait_ge(g_step, 4)
            pool.wait_ge(c_out, 16)
            for m in range(4):
                c, hf = m // 2, m % 2
                if m >= 2:
                    pool.wait_ge(d_T, m - 1)
                for i in range(4):
                    h = 4 * hf + i
                    k_ = proj2[:, c, B_K + h // 2 * P:B_K + h // 2 * P + P]
                    nc.gpsimd.tensor_scalar(dgS[m % 2][:, i, :], cst[:, C_GT, :], gt[:, 3, c, h:h + 1], None, ALU.mult)
                    nc.gpsimd.tensor_scalar(dkb[m % 2][:, i, :], k_, gt[:, 0, c, h:h + 1], None, ALU.mult).then_inc(d_pool, 1)

            def scaled(c, h):
                v_ = proj2[:, c, B_V + h * P:B_V + (h + 1) * P]
                k_ = proj2[:, c, B_K + h // 2 * P:B_K + h // 2 * P + P]
                nc.gpsimd.tensor_scalar(v_, v_, gt[:, 0, c, h:h + 1], None, ALU.mult)
                if c == 0:
                    ins = nc.gpsimd.tensor_scalar(dkd[:, h, :], k_, gt[:, 5, 0, h:h + 1], None, ALU.mult)
                else:
                    nc.gpsimd.tensor_scalar(dX[:, h, :], k_, gt[:, 0, 1, h:h + 1], -1.0, ALU.mult, ALU.mult).then_inc(d_vb, 1)
                    pool.wait_ge(d_vb, h + 1)
                    ins = nc.gpsimd.tensor_scalar(dX[:, h, :], dX[:, h, :], gt[:, 5, 1, h:h + 1], None, ALU.mult)
                if c == 1 and h == H - 1:
                    ins.then_inc(d_vb, 1)

            for i in range(4 * NL):
                lev, m = i // 4, i % 4
                pool.wait_ge(d_N, m + 1)
                if i >= 2:
                    pool.wait_ge(d_PP, i - 1)
                if 2 <= i < 6:
                    pool.wait_ge(d_TU, i - 1)
                nc.gpsimd.tensor_tensor(dB[i % 2][:, :, :], dN[:, 4 * m:4 * m + 4, :],
                                        cst[:, C_MASK + 1 + lev, :].unsqueeze(1).broadcast_to([P, 4, P]), ALU.mult).then_inc(d_B, 1)
                if 8 <= i < 8 + 2 * H:
                    scaled((i - 8) // H, (i - 8) % H)
            for h in range(H):
                q_ = proj2[:, 1, B_Q + h // 2 * P:B_Q + h // 2 * P + P]
                ins = nc.gpsimd.tensor_scalar(dqg[:, h, :], q_, gt[:, 5, 1, h:h + 1], None, ALU.mult)
            ins.then_inc(f_pool, 1)

        def delta_pe(pe):
            def operands(m):
                c, hf = m // 2, m % 2
                pe.wait_ge(d_pool, 4 * m + 4)
                if m >= 1:
                    pe.wait_ge(d_cp, m)
                    pe.wait_ge(d_E, m)
                for i, c0 in enumerate((B_K, B_K + P, B_Q, B_Q + P)):
                    c0 += 2 * hf * P
                    nc.tensor.transpose(pj[0][:, 0, i * P:(i + 1) * P], proj2[:, c, c0:c0 + P], ident)
                for i in range(4):
                    nc.tensor.transpose(pj[0][:, 1, i * P:(i + 1) * P], dkb[m % 2][:, i, :], ident)
                for i in range(4):
                    mm = nc.tensor.matmul(pj[1][:, 0, i * P:(i + 1) * P], dgS[m % 2][:, i, :], cst[:, C_LE, :], start=True, stop=True)
                mm.then_inc(d_T, 1)

            def scores(m):
                pe.wait_ge(d_cp, m + 1)
                if m >= 1:
                    pe.wait_ge(d_N, m)
                for i in range(4):
                    nc.tensor.matmul(pj[1][:, 1, i * P:(i + 1) * P], dkq[:, i // 2, :], dkbT[:, i, :], start=True, stop=True)
                for i in range(2):
                    mm = nc.tensor.matmul(pt[:, 0, i * P:(i + 1) * P], dkq[:, i, :], dkq[:, 2 + i, :], start=True, stop=True)
                mm.then_inc(d_S, 1)

            pe.wait_ge(l_step, 5)
            for i in range(5):
                if i < 4:
                    operands(i)
                if i >= 1:
                    scores(i - 1)

            def product(i):
                lev, m = i // 4, i % 4
                pe.wait_ge(d_B, i + 1)
                pe.wait_ge(d_cp, 4)
                if lev == 0:
                    if i >= 2:
                        pe.wait_ge(d_TU, i - 1)
                    for a in range(4):
                        mm = nc.tensor.transpose(pj[0][:, i % 2, a * P:(a + 1) * P], dB[i % 2][:, a, :], ident)
                else:
                    pe.wait_ge(d_TU, i - 3)
                    if i >= 6:
                        pe.wait_ge(d_Pc, i - 4 - 1)
                    for a in range(4):
                        mm = nc.tensor.matmul(pj[0][:, i % 2, a * P:(a + 1) * P], dB[i % 2][:, a, :], dT[:, 4 * m + a, :], start=True, stop=True)
                mm.then_inc(d_PP, 1)

            def deltas(i):
                lev, m = i // 4, i % 4
                if lev == 0:
                    return
                pe.wait_ge(d_Pc, i - 4 + 1)
                pe.wait_ge(d_N, 4)
                if i >= 6:
                    pe.wait_ge(d_TU, i - 1)
                p_ = dP[i % 2]
                if lev < NL - 1:
                    for a in range(4):
                        nc.tensor.matmul((pj[1], pt)[i % 2][:, 0, a * P:(a + 1) * P], dU[:, 4 * m + a, :], p_[:, a, :], start=True, stop=True)
                for a in range(4):
                    mm = nc.tensor.matmul((pj[1], pt)[i % 2][:, 1, a * P:(a + 1) * P], p_[:, a, :], dU[:, 4 * m + a, :], start=True, stop=True)
                mm.then_inc(d_dd, 1)

            for i in range(4 * NL + 1):
                if i < 4 * NL:
                    product(i)
                if i >= 1:
                    deltas(i - 1)

            def four(out, f):
                for a in range(4):
                    mm = f(out[:, a * P:(a + 1) * P], a)
                mm.then_inc(f_pe, 1)

            def mm1(o, l, r, start=True, stop=True):
                return nc.tensor.matmul(o, l, r, start=start, stop=stop, skip_group_check=True)

            V = lambda c, h: proj2[:, c, B_V + h * P:B_V + (h + 1) * P]
            pe.wait_ge(d_TU, 4 * NL)
            pe.wait_ge(d_vb, H + 1)
            for hf in range(2):
                four(pj[0][:, hf, :], lambda o, a: mm1(o, dU[:, 4 * hf + a, :], V(0, 4 * hf + a)))
            for hf in range(2):
                four(pj[1][:, hf, :], lambda o, a: mm1(o, dX[:, 4 * hf + a, :], dU[:, 8 + 4 * hf + a, :]))
            pe.wait_ge(f_pool, 1)
            for hf in range(2):
                four(pt[:, hf, :], lambda o, a: nc.tensor.transpose(o, dqg[:, 4 * hf + a, :], ident))
            for hf in range(2):
                pe.wait_ge(f_cp, hf + 1)
                four(pm[:, hf, :], lambda o, a: mm1(o, dkd[:, 4 * hf + a, :], dvn[hf][:, a, :]))
            for hf in range(2):
                four(pj[0][:, hf, :], lambda o, a: mm1(o, aqk(hf)[:, a * P:(a + 1) * P], dvn[hf][:, a, :]))
            pe.wait_ge(f_cp, 8)

            def v1(o, a):
                mm1(o, dU[:, 8 + 4 * hf + a, :], V(1, 4 * hf + a), stop=False)
                return mm1(o, dwT[:, 4 * hf + a, :], dS[:, 4 * hf + a, :], start=False)
            for hf in range(2):
                four(pj[1][:, hf, :], v1)

            def o1(o, a):
                mm1(o, dqgT[:, 4 * hf + a, :], dS[:, 4 * hf + a, :], stop=False)
                return mm1(o, aqk(2 + hf)[:, a * P:(a + 1) * P], dvn[2 + hf][:, a, :], start=False)
            for hf in range(2):
                pe.wait_ge(f_cp, 9 + hf)
                four(pt[:, hf, :], o1)

        def delta_act(act, n):
            for m in range(4):
                act.wait_ge(d_T, m + 1)
                if m >= 1:
                    act.wait_ge(d_S, m)
                if m >= 2:
                    act.wait_ge(d_Em, m - 1)
                nc.scalar.activation(dkq[:, :, :].rearrange("p a n -> p (a n)"), pj[0][:, 0, :], ACT.Copy)
                nc.scalar.activation(dkbT[:, :, :].rearrange("p a n -> p (a n)"), pj[0][:, 1, :], ACT.Copy).then_inc(d_cp, 1)
                nc.scalar.activation(dE[m % 2][:, :, :].rearrange("p a n -> p (a n)"), pj[1][:, 0, :], ACT.Exp).then_inc(d_E, 1)
            for i in range(4, 4 * NL):
                act.wait_ge(d_PP, i + 1)
                if i >= 6:
                    act.wait_ge(d_dd, i - 5)
                nc.scalar.activation(dP[i % 2][:, :, :].rearrange("p a n -> p (a n)"), pj[0][:, i % 2, :], ACT.Copy).then_inc(d_Pc, 1)
            outs = ([dvn[0], dvn[1], dwT[:, 0:4], dwT[:, 4:8], dqgT[:, 0:4], dqgT[:, 4:8], dS[:, 0:4], dS[:, 4:8]])
            banks = [b[:, i, :] for b in (pj[0], pj[1], pt, pm) for i in range(2)]
            for i, (o, b) in enumerate(zip(outs, banks)):
                act.wait_ge(f_pe, i + 1)
                nc.scalar.activation(o[:, :, :].rearrange("p a n -> p (a n)"), b, ACT.Copy).then_inc(f_cp, 1)
            for hf in range(2):
                act.wait_ge(f_pe, 11 + hf)
                nc.scalar.activation(dvn[2 + hf][:, :, :].rearrange("p a n -> p (a n)"), pj[1][:, hf, :], ACT.Copy).then_inc(f_cp, 1)

        def delta_dve(dve, n):
            for m in range(4):
                c = m // 2
                dve.wait_ge(d_E, m + 1)
                if m >= 1:
                    dve.wait_ge(d_N, m)
                nc.vector.tensor_tensor(dEm[:, :, :], dE[m % 2][:, :, :], cst[:, C_LE, :].unsqueeze(1).broadcast_to([P, 4, P]), ALU.mult).then_inc(d_Em, 1)
                dve.wait_ge(d_Em, m + 1)
                dve.wait_ge(d_S, m + 1)
                nc.vector.scalar_tensor_tensor(dN[:, 4 * m:4 * m + 4, :].rearrange("p a n -> p (a n)"), pj[1][:, 1, :], -1.0,
                                               dEm[:, :, :].rearrange("p a n -> p (a n)"), ALU.mult, ALU.mult)
                nc.vector.tensor_tensor(aqk(m).rearrange("p (a b n) -> p a b n", a=2, b=2),
                                        pt[:, 0, 0:256].rearrange("p (a n) -> p a n", a=2).unsqueeze(2).broadcast_to([P, 2, 2, P]),
                                        dEm[:, :, :].rearrange("p (a b) n -> p a b n", a=2), ALU.mult).then_inc(d_N, 1)
            eye = cst[:, C_ID, :].unsqueeze(1).broadcast_to([P, 4, P])
            for i in range(4 * NL):
                lev, m = i // 4, i % 4
                T_, U_ = dT[:, 4 * m:4 * m + 4, :], dU[:, 4 * m:4 * m + 4, :]
                if lev == 0:
                    dve.wait_ge(d_B, i + 1)
                    nc.vector.tensor_tensor(U_, dB[i % 2][:, :, :], eye, ALU.add)
                    dve.wait_ge(d_PP, i + 1)
                    nc.vector.tensor_tensor(T_, pj[0][:, i % 2, :].rearrange("p (a n) -> p a n", a=4), eye, ALU.add).then_inc(d_TU, 1)
                else:
                    dve.wait_ge(d_dd, i - 4 + 1)
                    bank = (pj[1], pt)[i % 2]
                    if lev < NL - 1:
                        nc.vector.tensor_tensor(T_, T_, bank[:, 0, :].rearrange("p (a n) -> p a n", a=4), ALU.add)
                    nc.vector.tensor_tensor(U_, U_, bank[:, 1, :].rearrange("p (a n) -> p a n", a=4), ALU.add).then_inc(d_TU, 1)
            for i in range(4):
                c, hf = i // 2, i % 2
                dve.wait_ge(f_pe, (9, 10, 13, 14)[i])
                o = proj2[:, c, A_F + hf * 512:A_F + hf * 512 + 512]
                nc.vector.tensor_copy(o, (pj[0], pt)[c][:, hf, :]).then_inc(f_dve, 1)


        def gate_silus(act):
            nc.scalar.activation(proj2[:, :, A_G:A_G + H * P], proj2[:, :, A_G:A_G + H * P], ACT.Silu)
            nc.scalar.activation(proj2[:, :, B_Z:B_Z + H * P], proj2[:, :, B_Z:B_Z + H * P], ACT.Silu).then_inc(m_step, 1)

        def mix_act(act, n):
            act.wait_ge(m_step, 3)
            nc.scalar.activation(mrs[:, :, :], mss[:, :, :], ACT.Sqrt).then_inc(m_step, 1)

        def mix_dve(dve, n):
            dve.wait_ge(f_dve, 4)
            o = proj2[:, :, A_F:A_F + H * P]
            link(dve, dve_link, n, nc.vector.tensor_tensor(dsq[:, :, :], o, o, ALU.mult))
            dve.wait_ge(m_step, 1)
            nc.vector.tensor_reduce(mss[:, :, H:2 * H], dsq[:, :, :].rearrange("p t (h n) -> p t h n", n=P), AX.X, ALU.add).then_inc(m_step, 1)
            dve.wait_ge(m_step, 2)
            nc.vector.tensor_scalar(mss[:, :, :], mss[:, :, :], 1.0 / HD, EPS, ALU.mult, ALU.add).then_inc(m_step, 1)
            dve.wait_ge(m_step, 4)
            link(dve, dve_link, n, nc.vector.reciprocal(mss[:, :, :], mrs[:, :, :]))
            for t in range(TT):
                o = proj2[:, t, 0:D].rearrange("p (h n) -> p h n", n=P)
                link(dve, dve_link, n, nc.vector.tensor_tensor(o, o, mss[:, t, :].unsqueeze(2).broadcast_to([P, 2 * H, P]), ALU.mult))
            for c0, g0 in ((0, A_G), (H * P, B_Z)):
                nc.vector.tensor_tensor(proj2[:, :, c0:c0 + H * P], proj2[:, :, c0:c0 + H * P], proj2[:, :, g0:g0 + H * P], ALU.mult).then_inc(m_step, 1)

        HS = 2 * H
        y = region(at_y + 4 * TT * NB)
        qn = y("qn", [P, TT, D])
        qT = y("qT", [P, HS, TT * P])
        sc = y("sc", [P, TT, HS, NK])
        keys = y("keys", [P, HS, NK])
        vals = y("vals", [P, TT, HS, TOPK])
        idx = y("idx", [P, TT, HS, TOPK], U32)
        y = region(at_tail)
        best = y("best", [P, TT, H, TOPK])
        pos = y("pos", [P, TT, H, TOPK], U32)
        at_q = at_y + 4 * TT * NB
        y = region(at_q)
        cand = y("cand", [P, TT, H, TOPK * TOPK])
        y = region(at_q)
        slotT = y("slotT", [P, 3, TT * P])
        hotA = [y(f"hotA{i}", [P, 4, NK]) for i in range(2)]
        hotB = [y(f"hotB{i}", [P, 4, NK]) for i in range(2)]
        slot_c = y("slot_c", [P, 64])
        y = region(at_q + 4 * TT * D)
        idxf = y("idxf", [P, TT, HS, TOPK])
        pq = y("pq", [P, 2, TT * H * TOPK], U32)
        pqf = y("pqf", [P, 2, TT, H * TOPK])
        res = y("res", [P, 3, TT, H * TOPK])
        gsum = y("gsum", [P, 2, TT * H])
        stage = [region(at_q + 4 * TT * D * (1 + i))(f"stage{i}", [P, NK, 32]) for i in range(2)]
        oh = region(at_q + 3 * 4 * TT * D)("oh", [P, H * TOPK, TOPK])
        r_keys, r_T, r_c, r_S, r_sc = sem("keys_loaded"), sem("query_transposed"), sem("query_copied"), sem("key_scores"), sem("key_scores_copied")
        tk, r_exp, r_sel, r_slotT, r_slot = sem("top_steps"), sem("gate_exp"), sem("select_steps"), sem("slots_transposed"), sem("slots_copied")
        r_A, r_B, r_G, r_gc = sem("first_onehots"), sem("second_onehots"), sem("gate_products"), sem("gates_copied")
        r_c64 = sem("slots_fixed")
        pool_step = sem("pool_passed_a_wait")
        g_wr = [sem("gates_written0"), sem("gates_written1")]
        GROUPS = TT * P // 4


        ON_DVE = 2

        def router_pe(pe, b, j):
            if b < 0:
                return
            if j == 0:
                pe.wait_ge(wq_evac, b + 1)
                if b:
                    pe.wait_ge(r_c, b)
                for i in range(4):
                    for t in range(TT):
                        at = (i % 2) * 256 + t * P
                        tr = nc.tensor.transpose(pt[:, i // 2, at:at + P], qn[:, t, (4 * b + i) * P:(4 * b + i + 1) * P], ident)
                tr.then_inc(r_T, 1)
            if j == 1:
                if b == 0:
                    pe.wait_ge(r_keys, 16)
                else:
                    pe.wait_ge(r_sc, b)
                pe.wait_ge(r_c, b + 1)
                for t in range(TT):
                    for i in range(4):
                        mm = nc.tensor.matmul(pm[:, t, i * P:(i + 1) * P], qT[:, 4 * b + i, t * P:(t + 1) * P],
                                              keys[:, 4 * b + i, :], start=True, stop=True)
                mm.then_inc(r_S, 1)

        def query_pe(pe, n):
            for g in range(4):
                if g >= 2:
                    pe.wait_ge(wq_evac, g - 1)
                for j in range(SLOTS):
                    if g == 0:
                        pe.wait_ge(tp_l, 4 * n + j + 1)
                    multiply(pe, Q_WQ + g, j, pj[g % 2], xh, xl, 4 * j, j == 0, j == SLOTS - 1)
                    router_pe(pe, g - 1, j)

        def router_act(act, b, j):
            if b < 0:
                return
            if j == 1:
                act.wait_ge(r_T, b + 1)
                nc.scalar.activation(qT[:, 4 * b:4 * b + 4, :].rearrange("p a n -> p (a n)"), pt[:, :, :].rearrange("p a n -> p (a n)"), ACT.Copy).then_inc(r_c, 1)
            if j == 2:
                act.wait_ge(r_S, b + 1)
                nc.scalar.activation(sc[:, :, 4 * b:4 * b + 4, :], pm[:, :, :].rearrange("p t (a n) -> p t a n", n=NK), ACT.Copy).then_inc(r_sc, 1)

        def query_act(act):
            for g in range(4):
                for j in range(SLOTS):
                    make_hi(act, *next_ones(Q_WQ + g, j))
                    router_act(act, g - 1, j)
                act.wait_ge(pe_used, (Q_WQ + g) * SLOTS + SLOTS)
                nc.scalar.activation(qn[:, :, g * NB:(g + 1) * NB], pj[g % 2][:, :, :], ACT.Copy).then_inc(wq_evac, 1)

        def sweeps(dve, base, n, ks, src, val, ind):
            for k in ks:
                for i in range(n):
                    if k:
                        dve.wait_ge(tk, base + (k - 1) * n + i + 1)
                    v, x_ = val(i), ind(i)
                    half = slice(0, 8) if k < 3 else slice(8, 16)
                    if k in (0, 3):
                        ins = nc.vector.max(v[:, half], src(i))
                    elif k in (1, 4):
                        ins = nc.vector.max_index(x_[:, half], v[:, half], src(i))
                    else:
                        ins = nc.vector.match_replace(src(i), v[:, 0:8], src(i), -3.0e38)
                    ins.then_inc(tk, 1)

        N_SUB, N_PAIR = TT * 4, TT * 2
        TK_GROUP = 5 * N_SUB + TT + 5 * N_PAIR

        def best_of_group(dve, b, part):
            base = b * TK_GROUP
            hs = lambda i: (slice(None), i // 4, 4 * b + i % 4, slice(None))
            hd = lambda i: (slice(None), i // 2, 2 * b + i % 2, slice(None))
            if part == 0:
                dve.wait_ge(r_sc, b + 1)
            if part < 2:
                sweeps(dve, base, N_SUB, (range(3), range(3, 5))[part], lambda i: sc[hs(i)], lambda i: vals[hs(i)], lambda i: idx[hs(i)])
            else:
                dve.wait_ge(tk, base + 5 * N_SUB + TT)
                sweeps(dve, base + 5 * N_SUB + TT, N_PAIR, (range(3), range(3, 5))[part - 2], lambda i: cand[hd(i)],
                       lambda i: best[hd(i)], lambda i: pos[hd(i)])
            if part == 1:
                dve.wait_ge(tk, base + 5 * N_SUB)
                v4 = vals[:, :, 4 * b:4 * b + 4, :].rearrange("p t (h s) k -> p t h s k", s=2)
                for t in range(TT):
                    nc.vector.tensor_tensor(cand[:, t, 2 * b:2 * b + 2, :].rearrange("p h (a b) -> p h a b", a=TOPK),
                                            v4[:, t, :, 0, :].unsqueeze(3).broadcast_to([P, 2, TOPK, TOPK]),
                                            v4[:, t, :, 1, :].unsqueeze(2).broadcast_to([P, 2, TOPK, TOPK]), ALU.add).then_inc(tk, 1)

        def router_dve(dve, b, j):
            if j >= 2 and b >= 0:
                best_of_group(dve, b, j - 2)
            if j < 2 and b >= 1:
                best_of_group(dve, b - 1, 2 + j)

        def query_dve(dve):
            for g in range(4):
                for j in range(SLOTS):
                    make_lo(dve, *next_ones(Q_WQ + g, j))
                    router_dve(dve, g - 1, j)

        def gates_build_dve(dve, n):
            best_of_group(dve, 3, 2)
            best_of_group(dve, 3, 3)
            dve.wait_ge(tk, 4 * TK_GROUP)
            gate_ = res[:, 0, :, :].rearrange("p t (h j) -> p (t h) j", j=TOPK)
            b_ = best[:, :, :, :].rearrange("p t h j -> p (t h) j")
            nc.vector.tensor_tensor(gate_, b_, b_[:, :, 0:1].broadcast_to([P, TT * H, TOPK]), ALU.subtract).then_inc(r_exp, 1)
            pos_ = pos[:, :, :, :].rearrange("p t h j -> p (t h j)")
            nc.vector.tensor_scalar(pq[:, 0, :], pos_, 4, None, ALU.logical_shift_right)
            nc.vector.tensor_copy(idxf[:, :, :, :], idx[:, :, :, :])
            link(dve, dve_link, n, nc.vector.tensor_scalar(pq[:, 1, :], pos_, 15, None, ALU.bitwise_and))
            link(dve, dve_link, n, nc.vector.tensor_copy(pqf[:, :, :, :].rearrange("p s t j -> p (s t j)"), pq[:, :, :].rearrange("p s j -> p (s j)")))
            dve.wait_ge(r_exp, 2)
            link(dve, dve_link, n, nc.vector.tensor_reduce(gsum[:, 0, :], gate_, AX.X, ALU.add))
            link(dve, dve_link, n, nc.vector.reciprocal(gsum[:, 1, :], gsum[:, 0, :]))
            nc.vector.tensor_tensor(gate_, gate_, gsum[:, 1, :].unsqueeze(2).broadcast_to([P, TT * H, TOPK]), ALU.mult)
            for s_ in range(2):
                for t in range(TT):
                    link(dve, dve_link, n, nc.vector.tensor_tensor(
                        oh[:, :, :], pqf[:, s_, t, :].unsqueeze(2).broadcast_to([P, H * TOPK, TOPK]),
                        cst[:, C_IOTA, 0:TOPK].unsqueeze(1).broadcast_to([P, H * TOPK, TOPK]), ALU.is_equal))
                    o4 = oh[:, :, :].rearrange("p (h j) a -> p h j a", h=H)
                    i4 = idxf[:, t, :, :].rearrange("p (h s) k -> p h s k", s=2)[:, :, s_, :]
                    link(dve, dve_link, n, nc.vector.tensor_tensor(o4, o4, i4.unsqueeze(2).broadcast_to([P, H, TOPK, TOPK]), ALU.mult))
                    link(dve, dve_link, n, nc.vector.tensor_reduce(res[:, 1 + s_, t, :], oh[:, :, :], AX.X, ALU.add))
            ins = nc.vector.tensor_copy(gsum[:, 0, 0:1], gsum[:, 1, 0:1])
            ins.then_inc(r_sel, 1)
            dve.wait_ge(r_slot, 2)

            def body(i):
                for g in range(16):
                    if not (isinstance(i, int) and i == 0 and g < 2):
                        dve.wait_ge(r_G, i * 16 + g - 1)
                    for a in range(4):
                        tok = i * 64 + (4 * g + a)
                        ins = nc.vector.tensor_scalar(hotA[g % 2][:, a, :], cst[:, C_IOTA, :], slotT[:, 1, bass.ds(tok, 1)],
                                                      slotT[:, 0, bass.ds(tok, 1)], ALU.is_equal, ALU.mult)
                    for a in range(ON_DVE):
                        tok = i * 64 + (4 * g + a)
                        ins = nc.vector.tensor_scalar(hotB[g % 2][:, a, :], cst[:, C_IOTA, :], slotT[:, 2, bass.ds(tok, 1)], None, ALU.is_equal)
                    ins.then_inc(r_A, 1)
            turns(dve, GROUPS // 16, body)

        def gates_build_pool(pool):
            pool.wait_ge(r_slot, 2)

            def body(i):
                if not (isinstance(i, int) and i == 0):
                    pool.wait_ge(r_B, i * 16)
                nc.gpsimd.tensor_copy(slot_c[:, :], slotT[:, 2, bass.ds(i * 64, 64)]).then_inc(r_c64, 1)
                pool.wait_ge(r_c64, i + 1)
                pool.sem_inc(pool_step, 1)
                for g in range(16):
                    if not (isinstance(i, int) and i == 0 and g < 2):
                        pool.wait_ge(r_G, i * 16 + g - 1)
                        pool.sem_inc(pool_step, 1)
                    for a in range(ON_DVE, 4):
                        ins = nc.gpsimd.tensor_scalar(hotB[g % 2][:, a, :], cst[:, C_IOTA, :], slot_c[:, 4 * g + a:4 * g + a + 1], None, ALU.is_equal)
                    ins.then_inc(r_B, 1)
            turns(pool, GROUPS // 16, body)

        def gates_build_pe(pe):
            pe.wait_ge(r_sel, 1)
            pe.wait_ge(r_sc, 4)
            for q_ in range(3):
                for t in range(TT):
                    tr = nc.tensor.transpose(pm[:, q_ // 2, (q_ % 2) * 256 + t * P:(q_ % 2) * 256 + t * P + P], res[:, q_, t, :], ident)
            tr.then_inc(r_slotT, 1)

            def body(i):
                for g in range(16):
                    first = isinstance(i, int) and i == 0
                    if first and g < 2:
                        pe.wait_ge(r_slot, 2)
                    else:
                        pe.wait_ge(r_gc, i * 16 + g - 1)
                    pe.wait_ge(r_A, i * 16 + g + 1)
                    pe.wait_ge(r_B, i * 16 + g + 1)
                    for a in range(4):
                        mm = nc.tensor.matmul(pm[:, g % 2, a * P:(a + 1) * P], hotA[g % 2][:, a, :], hotB[g % 2][:, a, :], start=True, stop=True)
                    mm.then_inc(r_G, 1)
            turns(pe, GROUPS // 16, body)

        def load_gates(act, s, par):
            act.dma_start(gate_e[par][:, :, :, :], gates_d[:, bass.ds(s, 1), :, :, :].rearrange("p a o b t -> p (a o) b t")).then_inc(gates_loaded[par], 16)

        def gates_build_act(act):
            act.wait_ge(r_exp, 1)
            nc.scalar.activation(res[:, 0, :, :], res[:, 0, :, :], ACT.Exp).then_inc(r_exp, 1)
            act.wait_ge(r_slotT, 1)
            nc.scalar.activation(slotT[:, 0:2, :].rearrange("p a n -> p (a n)"), pm[:, 0, :], ACT.Copy).then_inc(r_slot, 1)
            nc.scalar.activation(slotT[:, 2, :], pm[:, 1, 0:256], ACT.Copy).then_inc(r_slot, 1)

            def body(i):
                for g in range(16):
                    half, k = g // 8, g % 8
                    if k == 0 and not (isinstance(i, int) and i == 0):
                        act.wait_ge(g_wr[half], i * 16)
                    act.wait_ge(r_G, i * 16 + g + 1)
                    nc.scalar.activation(stage[half][:, :, 4 * k:4 * k + 4].rearrange("p b t -> p t b"),
                                         pm[:, g % 2, :].rearrange("p (t b) -> p t b", t=4), ACT.Copy).then_inc(r_gc, 1)
                    if k == 7:
                        act.wait_ge(r_gc, i * 16 + g + 1)
                        act.dma_start(gates_d[:, :, bass.ds(i * 2 + half, 1), :, :].rearrange("p s o b t -> p s (o b t)"),
                                      stage[half][:, :, :].rearrange("p (s b) t -> p s (b t)", b=4)).then_inc(g_wr[half], 16)
            turns(act, GROUPS // 16, body)
            for half in range(2):
                act.wait_ge(g_wr[half], 16 * (GROUPS // 16))
            load_gates(act, 0, 0)

        s_out = sem("out_written")
        gfin_in = sem("gfin_loaded")
        gates_loaded = [sem("gates_loaded0"), sem("gates_loaded1")]
        block = ctx.enter_context(nc.Block())

        @block.sync
        def _(sp):
            def stream(w, q0, quads, start=0):
                def body(i):
                    for j in range(SLOTS):
                        src = w[bass.ds(i * SLOTS + j, 1), :, :].rearrange("a p n -> p (a n)")
                        if not (isinstance(i, int) and q0 + i == 0):
                            sp.wait_ge(lo_ready, (i + q0) * SLOTS + j - 3)
                        sp.dma_start(raw[:, j, :], src).then_inc(raw_ready[j], 16)
                turns(sp, quads, body, start)

            for t in range(TT):
                sp.dma_start(resid[:, t, :], x_d[t * P:(t + 1) * P, :]).then_inc(s_x[t], 16)
            sp.dma_start(cst[:, :, :], cst_d).then_inc(s_const, 16)
            sp.dma_start(small[:, :], small_d).then_inc(s_const, 16)
            sp.dma_start(wtail[:, :, 0:8], wf_d).then_inc(wt_loaded, 16)
            sp.dma_start(att[:, :, :], att_d).then_inc(s_att, 16)
            sp.dma_start(gfin[:, :], gfin1_d.broadcast_to([P, D])).then_inc(gfin_in, 16)
            stream(w_in_d, Q_IN1, G1)
            stream(w_out_d, Q_OUT1, 4)
            sp.wait_ge(wt_l, 1)
            sp.dma_start(wtail[:, :, :], wba_d).then_inc(wt_loaded, 16)
            stream(w_mlp_d, Q_MLP, 2 * MLP_SB)
            stream(w_in2_d, Q_IN2, G2)
            stream(w_out2_d, Q_OUT2, 4)
            sp.wait_ge(tp_l, 20)
            sp.dma_start(keys[:, :, :], keys_d).then_inc(r_keys, 16)
            stream(wq_d, Q_WQ, 4)
            stream(w_peer_d, Q_PEER, 2 * PEER_SB)
            sp.wait_ge(ffn_sems["peer"]["coef"], 1)
            sp.dma_start(gfin[:, :], gfin2_d.broadcast_to([P, D])).then_inc(gfin_in, 16)
            for b in range(4):
                sp.wait_ge(nm_out, 20 + b + 1)
                cols = slice(b * NB, (b + 1) * NB)
                sp.dma_start(out_d[:, cols].rearrange("(t p) n -> p t n", p=P), nat[:, :, cols]).then_inc(s_out, 16)
            sp.wait_ge(s_out, 64)

        @block.scalar
        def _(act):
            n = [0]
            norm_act(act, 0, s_x)
            act.wait_ge(s_const, 32)
            make_hi(act, 0, 0, first=True)
            station_act(act, 0, lambda k: S_GATTN + k)
            for j in range(1, AHEAD):
                make_hi(act, 0, j, first=True)
            tail_act(act, 0, 8)
            wide_act(act, Q_IN1, G1, in1_evac, proj1)
            att1_act(act, n)
            station_act(act, 1, lambda k: S_GOUT1 + k)
            wide_act(act, Q_OUT1, 4, None, None)
            act.wait_ge(out1_evac, 4)
            norm_act(act, 1)
            station_act(act, 2, lambda k: S_GMLP + k)
            ffn_act(act, Q_MLP, MLP_SB, ffn_sems["mlp"], ACT.Relu, True, Q_END)
            act.wait_ge(ffn_sems["mlp"]["dn_evac"], 4 * MLP_SB)
            norm_act(act, 2)
            act.wait_ge(nm_out, 12)
            act.dma_start(lb[:, :, :], lbl_d.broadcast_to([P, 2, H * P])).then_inc(lbl_in, 16)
            norm_act(act, 3)
            tail_act(act, 1, 16)
            station_act(act, 3, lambda k: S_GATTN2 + k)
            wide_act(act, Q_IN2, G2, in2_evac, proj2, lambda: bound_act(act))
            hgrn_act(act, n)
            gates_act(act, n)
            conv_act(act, n)
            l2_act(act, n)
            gate_silus(act)
            delta_act(act, n)
            mix_act(act, n)
            station_act(act, 4, lambda k: S_GHGRN if k < H else S_GGDN)
            wide_act(act, Q_OUT2, 4, None, None)
            act.wait_ge(out2_evac, 4)
            norm_act(act, 4)
            station_act(act, 5, lambda k: S_GFFN + k)
            query_act(act)
            ffn_act(act, Q_PEER, PEER_SB, ffn_sems["peer"], ACT.Gelu, False, Q_END,
                    lambda j: router_act(act, 3, j), lambda: gates_build_act(act))
            act.wait_ge(ffn_sems["peer"]["dn_evac"], 4 * PEER_SB)
            norm_act(act, 5)

        @block.vector
        def _(dve):
            n = [0]
            norm_dve(dve, 0, nat)
            dve.wait_ge(s_const, 32)
            make_lo(dve, 0, 0)
            station_dve(dve, 0, lambda k: S_GATTN + k)
            for j in range(1, AHEAD):
                make_lo(dve, 0, j)
            tail_dve(dve, 0, 8)
            wide_dve(dve, Q_IN1, G1, None, False)
            att1_dve(dve, n)
            station_dve(dve, 1, lambda k: S_GOUT1 + k)
            wide_dve(dve, Q_OUT1, 4, out1_evac, True)
            norm_dve(dve, 1, nat)
            station_dve(dve, 2, lambda k: S_GMLP + k)
            ffn_dve(dve, Q_MLP, MLP_SB, ffn_sems["mlp"], None, Q_END)
            dve.wait_ge(gfin_in, 16)
            norm_dve(dve, 2, resid, gfin[:, :])
            norm_dve(dve, 3, nat)
            tail_dve(dve, 1, 16)
            station_dve(dve, 3, lambda k: S_GATTN2 + k)
            wide_dve(dve, Q_IN2, G2, None, False, lambda: bound_dve(dve, n))
            dve.wait_ge(wt_pe, 2)
            nc.vector.tensor_copy(tail[:, :, :], pm[:, :, 0:16]).then_inc(wt_out, 1)
            hgrn_dve(dve, n)
            gates_dve(dve, n)
            conv_dve(dve, n)
            l2_dve(dve, n)
            delta_dve(dve, n)
            mix_dve(dve, n)
            station_dve(dve, 4, lambda k: S_GHGRN if k < H else S_GGDN)
            wide_dve(dve, Q_OUT2, 4, out2_evac, True)
            norm_dve(dve, 4, nat)
            station_dve(dve, 5, lambda k: S_GFFN + k)
            query_dve(dve)
            ffn_dve(dve, Q_PEER, PEER_SB, ffn_sems["peer"], gates_loaded, Q_END,
                    lambda j: router_dve(dve, 3, j), lambda: gates_build_dve(dve, n))
            dve.wait_ge(gfin_in, 32)
            norm_dve(dve, 5, nat, gfin[:, :])

        @block.gpsimd
        def _(pool):
            att1_pool(pool)
            hgrn_pool(pool)
            delta_pool(pool)
            gates_build_pool(pool)

        @block.tensor
        def _(pe):
            pe.wait_ge(s_const, 32)
            station_pe(pe, 0, nat, 0)
            wide_pe(pe, Q_IN1, G1, in1_evac, 0)
            tail_pe(pe, 0, 8)
            att1_pe(pe)
            pe.wait_ge(hn_out, 2)
            station_pe(pe, 1, proj1)
            wide_pe(pe, Q_OUT1, 4, out1_evac, 1)
            station_pe(pe, 2, nat, 1)
            ffn_pe(pe, Q_MLP, MLP_SB, ffn_sems["mlp"], 2)
            station_pe(pe, 3, nat, 3)
            wide_pe(pe, Q_IN2, G2, in2_evac, 3)
            tail_pe(pe, 1, 16)
            pe.wait_ge(in2_evac, G2)
            pe.wait_ge(wt_out, 2)
            hgrn_pe(pe)
            gates_pe(pe)
            conv_pe(pe)
            delta_pe(pe)
            pe.wait_ge(m_step, 6)
            station_pe(pe, 4, proj2)
            wide_pe(pe, Q_OUT2, 4, out2_evac, 4)
            station_pe(pe, 5, nat, 4)
            query_pe(pe, 5)
            pe.wait_ge(wq_evac, 3)
            ffn_pe(pe, Q_PEER, PEER_SB, ffn_sems["peer"], 5,
                   lambda j: router_pe(pe, 3, j), lambda: gates_build_pe(pe))


def up_chunks(w):
    g = w.shape[1] // NB
    return np.ascontiguousarray(w.reshape(4, 4, P, g, NB).transpose(3, 0, 2, 1, 4)).reshape(4 * g, P, CH)


def down_chunks(w):
    s = w.shape[0] // NB
    return np.ascontiguousarray(w.reshape(s, 4, P, 4, NB).transpose(0, 3, 2, 1, 4)).reshape(4 * s, P, CH)


def ffn_chunks(up, down):
    n = up.shape[0] // 4
    up, down = up.reshape(n, 4, P, CH), down.reshape(n, 4, P, CH)
    out = np.empty((2 * n, 4, P, CH), np.float32)
    out[0], out[-1] = up[0], down[-1]
    out[1:-1:2], out[2:-1:2] = up[1:], down[:-1]
    return out.reshape(8 * n, P, CH)


def lay_out(x, g_attn, w_in, b_f, g_out_sb, g_out_fox, w_out, g_mlp, w_up, w_down, g_final,
            attn_norm_g_2, w_in_2, hgrn_lb_logits_2, hgrn_norm_g_2, gdn_conv_w_2, gdn_A_log_2,
            gdn_dt_bias_2, gdn_norm_g_2, w_out_2, ffn_norm_g_2, peer_w_query_2, peer_sub_keys_2,
            peer_u_2, peer_v_2, final_norm_g_2):
    f = lambda a: np.asarray(a, np.float32)
    cst, att = constants()
    col = lambda g: f(g).reshape(-1, P).T
    row = lambda g: np.broadcast_to(f(g).reshape(1, -1), (P, f(g).size))
    conv = f(gdn_conv_w_2)[0].reshape(4, 16, P).transpose(2, 1, 0).reshape(P, 64)
    small = np.concatenate([
        col(g_attn), col(g_out_sb), col(g_out_fox), col(g_mlp), col(attn_norm_g_2), col(hgrn_norm_g_2),
        col(gdn_norm_g_2), col(ffn_norm_g_2), row(b_f), row(gdn_A_log_2), row(gdn_dt_bias_2), conv], axis=1)
    w_in, w_in_2 = f(w_in)[0], f(w_in_2)[0]
    narrow = lambda w: np.ascontiguousarray(w.reshape(KT, P, -1).transpose(1, 0, 2))
    u = f(peer_u_2)[0].reshape(NK, PEER_SB, 4, 4, 4, P).transpose(1, 3, 5, 4, 2, 0)
    v = f(peer_v_2)[0].reshape(NK, PEER_SB, 4, 4, NB).transpose(1, 3, 0, 2, 4)
    keys = f(peer_sub_keys_2)[0].transpose(3, 1, 0, 2)
    return {
        "x": f(x)[0], "cst": cst, "att": att, "small": np.ascontiguousarray(small),
        "gfin1": f(g_final).reshape(1, D), "gfin2": f(final_norm_g_2).reshape(1, D),
        "lbl": f(hgrn_lb_logits_2).reshape(1, 2, H * P),
        "wf": narrow(w_in[:, W1:]), "wba": narrow(w_in_2[:, W2:]),
        "keys": np.ascontiguousarray(keys).reshape(P, 16, P),
        "w_in": up_chunks(w_in[:, :W1]), "w_out": up_chunks(f(w_out)[0]),
        "w_mlp": ffn_chunks(up_chunks(f(w_up)[0]), down_chunks(f(w_down)[0])),
        "w_in2": up_chunks(w_in_2[:, :W2]), "w_out2": up_chunks(f(w_out_2)[0]),
        "w_q": up_chunks(f(peer_w_query_2)[0].reshape(D, D)),
        "w_peer": ffn_chunks(np.ascontiguousarray(u).reshape(4 * PEER_SB, P, CH),
                             np.ascontiguousarray(v).reshape(4 * PEER_SB, P, CH)),
    }


def kernel(**inputs):
    import concourse.bacc as bacc
    from concourse.bass_utils import run_bass_kernel_spmd

    nc = bacc.Bacc("TRN2", target_bir_lowering=False, num_devices=1, dynamic_dma_scratch_size=1024)
    arrays = lay_out(**inputs)
    args = [nc.dram_tensor(name, a.shape, F32, kind="ExternalInput").ap() for name, a in arrays.items()]
    out = nc.dram_tensor("out", (TT * P, D), F32, kind="ExternalOutput").ap()
    two_blocks(nc, *args, out)
    r = run_bass_kernel_spmd(nc, [arrays], core_ids=[0])
    return r.results[0]["out"].reshape(1, TT * P, D)
```
